# Optimizing a Trainium2 kernel written in Bass

```python
import jax, jax.numpy as jnp
from jax import lax
import numpy as np

D_MODEL = 1024
BATCH = 1
SEQ = 256
DEPTH = 2
DEC_BATCH = 8
DEC_SEQ = 1
PAST_LEN = 2048
PAGE_SIZE = 128

N_MIXERS = 2
N_A_LAYERS = (DEPTH + 1) // 2
N_B_LAYERS = DEPTH // 2
CHUNK = 128
GMLP_WIDTH = D_MODEL
GMLP_GROUPS = 8
GMLP_GROUP_DIM = GMLP_WIDTH // GMLP_GROUPS
CONV_WIDTH = 31
CONV_STATE = CONV_WIDTH - 1
N_MEM = 256
XATTN_HEADS = 4
XATTN_HEAD_DIM = D_MODEL // XATTN_HEADS
FFN_DIM = 2816
N_EXPERTS = 8
TOP_K = 2
EXPERT_DIM = 3584
RMS_EPS = 1e-6
LN_EPS = 1e-5

kernel_name = "hybrid_gmlp_conformer_xattn_moe_step"

def rmsnorm(x, g):
    xf = x.astype(jnp.float32)
    y = xf * lax.rsqrt(jnp.mean(xf * xf, axis=-1, keepdims=True) + RMS_EPS)
    return (y * g.astype(jnp.float32)).astype(x.dtype)

def layernorm(x, g, b):
    xf = x.astype(jnp.float32)
    xc = xf - jnp.mean(xf, axis=-1, keepdims=True)
    var = jnp.mean(xc * xc, axis=-1, keepdims=True)
    y = xc * lax.rsqrt(var + LN_EPS) * g.astype(jnp.float32) + b.astype(jnp.float32)
    return y.astype(x.dtype)

def gmlp_mixer(h, w_in, ln_g, ln_b, w_s, b_s, w_out):
    bsz, s, _ = h.shape
    z = jax.nn.gelu(h @ w_in)
    u, v = jnp.split(z, 2, axis=-1)
    v = layernorm(v, ln_g, ln_b)
    lc = min(s, CHUNK)
    pad = (-s) % lc
    vp = jnp.pad(v, ((0, 0), (0, pad), (0, 0)))
    nc = (s + pad) // lc
    vr = vp.reshape(bsz, nc, lc, GMLP_GROUPS, GMLP_GROUP_DIM)
    causal = jnp.tril(jnp.ones((lc, lc), dtype=bool))
    w = jnp.where(causal[None], w_s[:, :lc, :lc], jnp.zeros((), w_s.dtype))
    bias = jnp.transpose(b_s[:, :lc])[None, None, :, :, None]
    mixed = jnp.einsum('gts,bcsgd->bctgd', w, vr) + bias
    mixed = mixed.reshape(bsz, nc * lc, GMLP_WIDTH)[:, :s]
    return (u * mixed) @ w_out, v

def causal_depthwise(ext, w_dw):
    return lax.conv_general_dilated(ext, w_dw[:, None, :], window_strides=(1,), padding='VALID',
                                    dimension_numbers=('NWC', 'WIO', 'NWC'),
                                    feature_group_count=ext.shape[-1])

def conformer_conv(h, buf, w_pw1, w_dw, b_dw, ln_g, ln_b, w_pw2):
    a, gate = jnp.split(h @ w_pw1, 2, axis=-1)
    c = a * jax.nn.sigmoid(gate)
    ext = jnp.concatenate([buf.astype(c.dtype), c], axis=1)
    y = causal_depthwise(ext, w_dw) + b_dw
    y = jax.nn.silu(layernorm(y, ln_g, ln_b))
    return y @ w_pw2, ext[:, -CONV_STATE:]

def memory_kv(mem, g, w_k, w_v):
    b, m, _ = mem.shape
    mn = rmsnorm(mem, g)
    k = (mn @ w_k).reshape(b, m, XATTN_HEADS, XATTN_HEAD_DIM)
    v = (mn @ w_v).reshape(b, m, XATTN_HEADS, XATTN_HEAD_DIM)
    return k, v

def cross_attention(h, k, v, w_q, w_o):
    b, s, _ = h.shape
    q = (h @ w_q).reshape(b, s, XATTN_HEADS, XATTN_HEAD_DIM)
    scores = jnp.einsum('bshd,bmhd->bhsm', q, k, preferred_element_type=jnp.float32) * (XATTN_HEAD_DIM ** -0.5)
    p = jax.nn.softmax(scores, axis=-1).astype(v.dtype)
    o = jnp.einsum('bhsm,bmhd->bshd', p, v).reshape(b, s, D_MODEL)
    return o @ w_o

def swiglu(h, w_gate, w_up, w_down):
    return (jax.nn.silu(h @ w_gate) * (h @ w_up)) @ w_down

def moe_swiglu(h, w_router, w_gate, w_up, w_down):
    logits = (h @ w_router).astype(jnp.float32)
    top_v, top_i = lax.top_k(logits, TOP_K)
    top_w = jax.nn.softmax(top_v, axis=-1)
    gates = jnp.sum(jax.nn.one_hot(top_i, N_EXPERTS, dtype=jnp.float32) * top_w[..., None], axis=-2)
    gates = gates.astype(h.dtype)
    out = jnp.zeros_like(h)
    for e in range(N_EXPERTS):
        out = out + gates[..., e:e + 1] * swiglu(h, w_gate[e], w_up[e], w_down[e])
    return out

def trunk(x, mem_k, mem_v, conv_buf, norm_mix, norm_xattn, norm_ffn, norm_final, w_xq, w_xo,
          a_w_in, a_ln_g, a_ln_b, a_w_s, a_b_s, a_w_out,
          b_w_pw1, b_w_dw, b_b_dw, b_ln_g, b_ln_b, b_w_pw2,
          ffn_w_gate, ffn_w_up, ffn_w_down, moe_w_router, moe_w_gate, moe_w_up, moe_w_down):
    h = x
    conv_new, v_rows = [], []
    for i in range(DEPTH):
        j = i // N_MIXERS
        hn = rmsnorm(h, norm_mix[i])
        if i % N_MIXERS == 0:
            mix, vr = gmlp_mixer(hn, a_w_in[j], a_ln_g[j], a_ln_b[j], a_w_s[j], a_b_s[j], a_w_out[j])
            v_rows.append(vr)
        else:
            mix, nb = conformer_conv(hn, conv_buf[j], b_w_pw1[j], b_w_dw[j], b_b_dw[j],
                                     b_ln_g[j], b_ln_b[j], b_w_pw2[j])
            conv_new.append(nb)
        h = h + mix
        h = h + cross_attention(rmsnorm(h, norm_xattn[i]), mem_k[i], mem_v[i], w_xq[i], w_xo[i])
        hn = rmsnorm(h, norm_ffn[i])
        if i % N_MIXERS == 0:
            h = h + swiglu(hn, ffn_w_gate[j], ffn_w_up[j], ffn_w_down[j])
        else:
            h = h + moe_swiglu(hn, moe_w_router[j], moe_w_gate[j], moe_w_up[j], moe_w_down[j])
    return rmsnorm(h, norm_final), conv_new, v_rows

def setup_inputs(seed: int = 0) -> dict:
    key = jax.random.key(seed)
    ks = iter(jax.random.split(key, 40))

    def nrm(shape, scale):
        return jax.random.normal(next(ks), shape, jnp.float32) * scale

    def gain(shape):
        return 1.0 + nrm(shape, 0.05)

    d = D_MODEL
    return {
        "x_prompt": nrm((BATCH, SEQ, d), 1.0),
        "x_sample": nrm((DEC_BATCH, DEC_SEQ, d), 1.0),
        "mem_prompt": nrm((BATCH, N_MEM, d), 1.0),
        "cache_mem_k": nrm((DEPTH, DEC_BATCH, N_MEM, XATTN_HEADS, XATTN_HEAD_DIM), 1.0),
        "cache_mem_v": nrm((DEPTH, DEC_BATCH, N_MEM, XATTN_HEADS, XATTN_HEAD_DIM), 1.0),
        "state_conv": nrm((N_B_LAYERS, DEC_BATCH, CONV_STATE, d), 0.5),
        "norm_mix": gain((DEPTH, d)),
        "norm_xattn": gain((DEPTH, d)),
        "norm_ffn": gain((DEPTH, d)),
        "norm_mem": gain((DEPTH, d)),
        "norm_final": gain((d,)),
        "w_xq": nrm((DEPTH, d, d), d ** -0.5),
        "w_xk": nrm((DEPTH, d, d), d ** -0.5),
        "w_xv": nrm((DEPTH, d, d), d ** -0.5),
        "w_xo": nrm((DEPTH, d, d), d ** -0.5),
        "a_w_in": nrm((N_A_LAYERS, d, 2 * GMLP_WIDTH), d ** -0.5),
        "a_ln_g": gain((N_A_LAYERS, GMLP_WIDTH)),
        "a_ln_b": nrm((N_A_LAYERS, GMLP_WIDTH), 0.02),
        "a_w_s": nrm((N_A_LAYERS, GMLP_GROUPS, CHUNK, CHUNK), CHUNK ** -0.5),
        "a_b_s": 1.0 + nrm((N_A_LAYERS, GMLP_GROUPS, CHUNK), 0.1),
        "a_w_out": nrm((N_A_LAYERS, GMLP_WIDTH, d), GMLP_WIDTH ** -0.5),
        "b_w_pw1": nrm((N_B_LAYERS, d, 2 * d), d ** -0.5),
        "b_w_dw": nrm((N_B_LAYERS, CONV_WIDTH, d), CONV_WIDTH ** -0.5),
        "b_b_dw": nrm((N_B_LAYERS, d), 0.02),
        "b_ln_g": gain((N_B_LAYERS, d)),
        "b_ln_b": nrm((N_B_LAYERS, d), 0.02),
        "b_w_pw2": nrm((N_B_LAYERS, d, d), d ** -0.5),
        "ffn_w_gate": nrm((N_A_LAYERS, d, FFN_DIM), d ** -0.5),
        "ffn_w_up": nrm((N_A_LAYERS, d, FFN_DIM), d ** -0.5),
        "ffn_w_down": nrm((N_A_LAYERS, FFN_DIM, d), FFN_DIM ** -0.5),
        "moe_w_router": nrm((N_B_LAYERS, d, N_EXPERTS), d ** -0.5),
        "moe_w_gate": nrm((N_B_LAYERS, N_EXPERTS, d, EXPERT_DIM), d ** -0.5),
        "moe_w_up": nrm((N_B_LAYERS, N_EXPERTS, d, EXPERT_DIM), d ** -0.5),
        "moe_w_down": nrm((N_B_LAYERS, N_EXPERTS, EXPERT_DIM, d), EXPERT_DIM ** -0.5),
    }

def reference(x_prompt, x_sample, mem_prompt, cache_mem_k, cache_mem_v, state_conv,
              norm_mix, norm_xattn, norm_ffn, norm_mem, norm_final, w_xq, w_xk, w_xv, w_xo,
              a_w_in, a_ln_g, a_ln_b, a_w_s, a_b_s, a_w_out,
              b_w_pw1, b_w_dw, b_b_dw, b_ln_g, b_ln_b, b_w_pw2,
              ffn_w_gate, ffn_w_up, ffn_w_down, moe_w_router, moe_w_gate, moe_w_up, moe_w_down):
    weights = (norm_mix, norm_xattn, norm_ffn, norm_final, w_xq, w_xo,
               a_w_in, a_ln_g, a_ln_b, a_w_s, a_b_s, a_w_out,
               b_w_pw1, b_w_dw, b_b_dw, b_ln_g, b_ln_b, b_w_pw2,
               ffn_w_gate, ffn_w_up, ffn_w_down, moe_w_router, moe_w_gate, moe_w_up, moe_w_down)

    mk, mv = [], []
    for i in range(DEPTH):
        k, v = memory_kv(mem_prompt, norm_mem[i], w_xk[i], w_xv[i])
        mk.append(k)
        mv.append(v)
    mem_k_prompt = jnp.stack(mk)
    mem_v_prompt = jnp.stack(mv)
    zero_buf = jnp.zeros((N_B_LAYERS, x_prompt.shape[0], CONV_STATE, D_MODEL), x_prompt.dtype)
    y_prompt, conv_p, _ = trunk(x_prompt, mem_k_prompt, mem_v_prompt, zero_buf, *weights)
    conv_state_prompt = jnp.stack(conv_p)

    y_sample, conv_s, v_s = trunk(x_sample, cache_mem_k, cache_mem_v, state_conv, *weights)
    conv_state_sample = jnp.stack(conv_s)
    chunk_v_sample = jnp.stack(v_s)

    return (y_prompt, y_sample, mem_k_prompt, mem_v_prompt, conv_state_prompt, conv_state_sample, chunk_v_sample)


_drawn_inputs = setup_inputs


def setup_inputs(seed=0):
    import zlib

    import numpy as np

    out = dict(_drawn_inputs(seed))
    spreads = {}
    factors = {'norm_xattn': 2.901, 'a_ln_b': 2.883}
    for name, (base, spread) in spreads.items():
        noise = np.random.default_rng([zlib.crc32(name.encode()), seed]).standard_normal(out[name].shape)
        drawn = base * np.exp(spread * noise) if base else spread * noise
        out[name] = __import__('jax').numpy.asarray(drawn.astype(out[name].dtype))
    for name, factor in factors.items():
        out[name] = (out[name] * factor).astype(out[name].dtype)
    return out
```

```python
from contextlib import ExitStack

import concourse.bass as bass
from concourse import mybir

F32 = mybir.dt.float32
F32R = mybir.dt.float32r
I32 = mybir.dt.int32
ALU = mybir.AluOpType
ACT = mybir.ActivationFunctionType
AX = mybir.AxisListType

P = 128
D = 1024
KT = D // P
TP = 256
TS = 8
T = TP + TS
MEM = 256
HEADS = 4
HD = D // HEADS
CHUNK = 128
TAPS = 31
STATE = TAPS - 1
FFN = 2816
FT = FFN // P
EXPERTS = 8
EDIM = 3584
RMS_EPS = 1e-6
LN_EPS = 1e-5
SCALE = float(HD) ** -0.5

RAW = 6
SPLIT = 3
PIECE = 2048
PC = 256

(V_MIX, V_XATT, V_FFN, V_MEM, V_ALNG, V_ALNB, V_BDW, V_BLNG, V_BLNB, V_DW) = (0, 2, 4, 6, 8, 9, 10, 11, 12, 13)
NV = V_DW + TAPS

EC = 512
CH = EDIM // EC
CAP = 128


def dense_pieces():
    out, first = [], {}

    def add(stage, weight, col, k0=0, nk=KT, opens=True, closes=True):
        first.setdefault(stage, len(out))
        out.append((weight, k0, nk, col, opens, closes))

    def whole(stage, weight, cols, base=0):
        for c in range(cols // PC):
            add(stage, weight, base + c * PC)

    whole("k0", "xk0", D)
    whole("v0", "xv0", D)
    whole("in_v", "a_in", D, D)
    whole("in_u", "a_in", D)
    whole("a_out", "a_out", D)
    whole("q0", "xq0", D)
    whole("o0", "xo0", D)
    for c in range(FFN // PC):
        add("gate_up", "gate", c * PC)
        add("gate_up", "up", c * PC)
    for c in range(D // PC):
        for k0 in range(0, FT, KT):
            add("down", "down", c * PC, k0, min(KT, FT - k0), k0 == 0, k0 + KT >= FT)
    for c in range(D // PC):
        add("pw1", "pw1", D + c * PC)
        add("pw1", "pw1", c * PC)
    whole("k1", "xk1", D)
    whole("v1", "xv1", D)
    whole("pw2", "pw2", D)
    whole("q1", "xq1", D)
    whole("o1", "xo1", D)
    groups, g = [], -1
    for p in out:
        g += p[4]
        groups.append(g)
    return out, groups, first


PIECES, GROUP, FIRST = dense_pieces()
ND = len(PIECES)
assert ND % RAW == 0 and ND % SPLIT == 0

EP = []
for _c in range(CH):
    EP += [("g", _c, 0), ("g", _c, 1), ("u", _c, 0), ("u", _c, 1)]
    if _c:
        EP += [("d", _c - 1, 0), ("d", _c - 1, 1)]
EP += [("d", CH - 1, 0), ("d", CH - 1, 1)]
NE = len(EP)
assert NE % RAW == 0 and NE % SPLIT == 0
SCATTER = ((0, 0), (0, 1), (1, 0), (1, 1), (2, 0), (2, 1))

AUX, _n = {}, 0
_ATT = [("rms_xatt", 1), ("q_tok", 2), ("scores", 4), ("q_bc", 16), ("s_t", 1), ("p_t", 4), ("ps_t", 1), ("o_t", 4),
        ("s_o", 2), ("os_t", 1)]
for _name, _count in (
    [("vec", 1), ("mem_t", 4), ("x_t", 8), ("ws_t", 2), ("ws_0", 1), ("rms_mix0", 1), ("k_tok0", 4), ("ln_a0", 1), ("ln_b0", 1),
     ("v_smp", 2), ("v_tok", 4), ("mixed", 4)] + [(n + "0", c) for n, c in _ATT]
    + [("rms_ffn0", 1), ("rms_mix1", 1), ("state_t", 4), ("k_tok1", 4), ("c_tok", 4), ("ln_a1", 1), ("ln_b1", 1)]
    + [(n + "1", c) for n, c in _ATT] + [("rms_ffn1", 1), ("route", 1), ("pos", 2), ("hn_tok", 6), ("y_tok", 6)]
):
    AUX[_name] = _n
    _n += _count

XW = {n: 8 * i for i, n in enumerate(["mix0", "mixed", "xatt0", "att0", "ffn0", "mix1", "mem1", "conv", "xatt1", "att1"])}
FEED = {n: 8 * i for i, n in enumerate(["mix0", "mixed", "xatt0", "ffn0", "mix1", "conv", "xatt1"])}
SQ = {n: i + 1 for i, n in enumerate(["mix0", "xatt0", "ffn0", "mix1", "xatt1", "ffn1"])}


def same(x, y):
    return x is y


class Own:

    def __init__(self, eng, chain):
        self.eng, self.chain, self.count, self.waited = eng, chain, 0, 0

    def __call__(self, ins):
        self.count += 1
        return ins.then_inc(self.chain, 1)

    def settle(self, lag=0):
        if self.count - lag > self.waited:
            self.waited = self.count - lag
            self.eng.wait_ge(self.chain, self.waited)


def build_step(nc, ctx, a, out):
    place = [-(-nc.sbuf_base // 32) * 32]

    def at(name, shape, dt, off=None):
        size = 4
        for n in shape[1:]:
            size *= n
        if off is None:
            off = place[0]
            place[0] += -(-size // 32) * 32
        assert off % 32 == 0 and off + size <= nc.sbuf_usable_end, (name, off + size, nc.sbuf_usable_end)
        return nc.alloc_sbuf_tensor_at(name, shape, dt, offset=off)

    def sem(name):
        return ctx.enter_context(nc.semaphore(name))

    raw = at("raw", [P, RAW, PIECE], F32)
    whi = at("whi", [P, SPLIT, PIECE], F32R)
    wlo = at("wlo", [P, SPLIT, PIECE], F32R)
    vecs = at("vecs", [P, KT, NV], F32)
    ident = at("ident", [P, P], F32)
    ones = at("ones", [P, P], F32)
    stat = at("stat", [P, 3, T], F32)
    pz = at("pz", [P, 2, HEADS, TS, TS], F32)
    wr = at("wr", [P, KT, EXPERTS], F32)
    small = at("small", [P, 48], F32)
    os8 = at("os8", [P, KT, TS], F32)
    flag = at("flag", [P, 8], I32)
    b_off = place[0]
    hT = at("hT", [P, KT, T], F32)
    xh = at("xh", [P, KT, T], F32R)
    xl = at("xl", [P, KT, T], F32R)
    sq_off = place[0]
    sq = at("sq", [P, KT, T], F32)
    c_off = place[0]
    memT = at("memT", [P, KT, MEM], F32)
    kT = at("kT", [P, KT, MEM], F32)
    vm = at("vm", [P, 2, D], F32)
    e_off = place[0]
    mh = at("mh", [P, KT, MEM], F32R, e_off)
    ml = at("ml", [P, KT, MEM], F32R, e_off + 8192)
    mem_in = at("mem_in", [P, 2, D], F32, e_off + 16384)
    x_in = at("x_in", [P, 3, D], F32, e_off + 24576)
    rows = at("rows", [NV, D], F32, e_off + 37376)
    ws_in = at("ws_in", [P, KT, P], F32, e_off + 41472)
    uT = at("uT", [P, KT, T], F32, e_off)
    vT = at("vT", [P, KT, T], F32, e_off + 8448)
    vtok = at("vtok", [P, 2, D], F32, e_off + 16896)
    kst = at("kst", [P, 2, D], F32, e_off + 25088)
    wsT = at("wsT", [P, KT, P], F32, e_off + 33280)
    bsb = at("bsb", [P, KT, P], F32, e_off + 37376)
    vs_out = at("vs_out", [TS, D], F32, e_off + 41472)
    qT = at("qT", [P, KT, T], F32, e_off)
    pT = at("pT", [P, 2, HEADS, TP], F32, e_off + 8448)
    qs = at("qs", [TS, D], F32, e_off + 16640)
    kv = at("kv", [P, 3, 2, D], F32, e_off + 20736)
    sc = at("sc", [P, 2, TS * HEADS], F32, e_off + 45312)
    att = at("att", [P, 64], F32, e_off + 45568)
    psm = at("psm", [TS * HEADS, MEM], F32, e_off + 45824)
    pr = at("pr", [P, 2, HEADS, MEM], F32, sq_off)
    ah = at("ah", [P, FT, T], F32R, e_off)
    al = at("al", [P, FT, T], F32R, e_off + 23232)
    sg = at("sg", [P, 4, T], F32, sq_off)
    af = at("af", [P, 4, T], F32, sq_off + 4224)
    ce = at("ce", [P, KT, STATE + TP], F32, e_off)
    se = at("se", [P, KT, TS, TAPS], F32, e_off + 9152)
    cv = at("cv", [P, KT, T], F32, e_off + 17088)
    st_in = at("st_in", [4 * STATE, 2, D], F32, e_off + 25536)
    kst1 = at("kst1", [P, 2, D], F32, e_off + 33728)
    c_out = at("c_out", [STATE, D], F32, e_off + 41920)
    cs_out = at("cs_out", [TS, D], F32, e_off + 29632)
    hth = at("hth", [P, 3, D], F32R, e_off)
    htl = at("htl", [P, 3, D], F32R, e_off + 12288)
    ytok = at("ytok", [P, 3, D], F32, e_off + 24576)
    hb = at("hb", [P, 2, EC], F32, e_off + 36864)
    sf = at("sf", [P, 3, CAP], F32, e_off + 40960)
    sr = at("sr", [P, 3, CAP], F32R, e_off + 42496)
    st = at("st", [CAP, T], F32R, e_off + 44032)
    gr = at("gr", [CAP, 8], F32, e_off + 45088)
    iota = at("iota", [P, CAP], F32, e_off + 45120)
    tri = at("tri", [P, P], F32, e_off + 45632)
    xeh = at("xeh", [P, KT, CAP], F32R, c_off)
    xel = at("xel", [P, KT, CAP], F32R, c_off + 4096)
    hTh = at("hTh", [P, EC], F32R, c_off + 8192)
    hTl = at("hTl", [P, EC], F32R, c_off + 10240)
    oeh = at("oeh", [CAP, D], F32R, c_off + 12288)
    oel = at("oel", [CAP, D], F32R, c_off + 16384)
    grow = at("grow", [P, D], F32, c_off + 20480)
    rt = at("rt", [P, 16, 3, EXPERTS + 1], F32, b_off + 8448)
    yo = at("yo", [P, 3, D], F32, b_off)

    bank = [nc.alloc_psum_tensor(f"bank{i}", [P, 512], F32) for i in range(8)]
    eps_r, eps_l = small[:, 0:1], small[:, 1:2]
    ws0, bs0 = small[:, 8:16], bsb[:, :, 0]
    order8 = small[:, 24:32]

    landed = [sem(f"raw{i}_landed") for i in range(RAW)]
    hi_done, lo_done, piece_done, tile0_done = sem("hi_done"), sem("lo_done"), sem("piece_done"), sem("tile0_done")
    evac = [sem(f"bank{i}_evac") for i in range(4)]
    aux_ready = sem("aux_ready")
    aux_free = [sem(f"aux{i}_free") for i in range(4)]
    act_own, dve_own, pool_own = sem("act_own"), sem("dve_own"), sem("pool_own")
    x_done, xn_done, xh_done, xoh_done, osh_done, mh_done, m_done, sq_done = (
        sem(n) for n in ("x_done", "xn_done", "xh_done", "xoh_done", "osh_done", "mh_done", "m_done", "sq_done"))
    consts, ld_mem, ld_x, ld_rows, ld_ws, ld_misc, ld_state, ld_wr, ld_grow = (
        sem(n) for n in ("consts", "ld_mem", "ld_x", "ld_rows", "ld_ws", "ld_misc", "ld_state", "ld_wr", "ld_grow"))
    kv_in = [sem(f"kv{i}_in") for i in range(3)]
    mem_sum, mem_root, mem_n, ws_masked, kst_out, vm_out, stored, eps_set = (
        sem(n) for n in ("mem_sum", "mem_root", "mem_n", "ws_masked", "kst_out", "vm_out", "stored", "eps_set"))
    ah_done, a_done, lnsq_done, lnv_done, conv_done, nmax_done, p_done, snmax_done, sp_done, vused, pad_done = (
        sem(n) for n in ("ah_done", "a_done", "lnsq_done", "lnv_done", "conv_done", "nmax_done", "p_done", "snmax_done",
                         "sp_done", "vused", "pad_done"))
    hn_ready, gate_gap, gate_exp, mask_done, hth_done, flag_ready, moe_const = (
        sem(n) for n in ("hn_ready", "gate_gap", "gate_exp", "mask_done", "hth_done", "flag_ready", "moe_const"))
    t_ready, gat_ready, sca_ready, prep_ready = (sem(n) for n in ("t_ready", "gat_ready", "sca_ready", "prep_ready"))
    silu_done, hTh_done, xeh_done, oeh_done = (sem(n) for n in ("silu_done", "hTh_done", "xeh_done", "oeh_done"))
    h_done, hTl_done, xel_done, oel_done, y_added, s_built, prep_done, pos_moved = (
        sem(n) for n in ("h_done", "hTl_done", "xel_done", "oel_done", "y_added", "s_built", "prep_done", "pos_moved"))
    fin_sum, fin_root, fin_done = sem("fin_sum"), sem("fin_root"), sem("fin_done")

    def by_row_tiles(w):
        return w.rearrange("(t p) n -> p t n", p=P)

    W = {"a_in": by_row_tiles(a["a_w_in"][0]), "a_out": by_row_tiles(a["a_w_out"][0]),
         "gate": by_row_tiles(a["ffn_w_gate"][0]), "up": by_row_tiles(a["ffn_w_up"][0]),
         "down": by_row_tiles(a["ffn_w_down"][0]), "pw1": by_row_tiles(a["b_w_pw1"][0]),
         "pw2": by_row_tiles(a["b_w_pw2"][0])}
    for i in range(2):
        for n in "qkvo":
            W[f"x{n}{i}"] = by_row_tiles(a[f"w_x{n}"][i])
    moe = {"g": a["moe_w_gate"].rearrange("o e (t p) n -> p (o e t) n", p=P),
           "u": a["moe_w_up"].rearrange("o e (t p) n -> p (o e t) n", p=P),
           "d": a["moe_w_down"].rearrange("o e (t p) n -> p (o e t) n", p=P)}

    def moe_source(e, p):
        kind, c, half = EP[p]
        if kind == "d":
            return moe["d"][:, bass.ds(e * (EDIM // P) + 4 * c, 4), half * EC:(half + 1) * EC]
        return moe[kind][:, bass.ds(e * KT + 4 * half, 4), c * EC:(c + 1) * EC]

    def piece_no(ps, e, p):
        return ND + ps * (EXPERTS * NE) + e * NE + p

    def tile_ready(n, o):
        return (tile0_done, GROUP[n] + 1) if o == 0 else (piece_done, n + 1)

    def tile_out(n, o):
        return evac[2 * (GROUP[n] % 2) + o], GROUP[n] // 2 + 1

    def stage_out(stage, count):
        return tile_out(FIRST[stage] + count - 1, 1)

    def job_out(name, j=0):
        n = AUX[name] + j
        return aux_free[n % 4], n // 4 + 1

    def job_bank(name, j=0):
        return bank[4 + (AUX[name] + j) % 4]

    def piece_bank(n, o):
        return bank[2 * (GROUP[n] % 2) + o]

    block = ctx.enter_context(nc.Block())

    @block.sync
    def _(sp):
        sp.dma_start(mem_in[:, :, :], a["mem_prompt"][0].rearrange("(m p) d -> p m d", p=P)).then_inc(ld_mem, 16)
        for v0, n, name in ((V_MIX, 2, "norm_mix"), (V_XATT, 2, "norm_xattn"), (V_FFN, 2, "norm_ffn"), (V_MEM, 2, "norm_mem"),
                            (V_ALNG, 1, "a_ln_g"), (V_ALNB, 1, "a_ln_b"), (V_BDW, 1, "b_b_dw"), (V_BLNG, 1, "b_ln_g"),
                            (V_BLNB, 1, "b_ln_b")):
            sp.dma_start(rows[v0:v0 + n, :], a[name]).then_inc(ld_rows, 16)
        sp.dma_start(rows[V_DW:NV, :], a["b_w_dw"][0]).then_inc(ld_rows, 16)
        sp.dma_start(x_in[:, 0:2, :], a["x_prompt"][0].rearrange("(m p) d -> p m d", p=P)).then_inc(ld_x, 16)
        sp.dma_start(x_in[0:TS, 2, :], a["x_sample"].rearrange("b s d -> (b s) d")).then_inc(ld_x, 16)
        sp.dma_start(ws_in[:, :, :], a["a_w_s"][0].rearrange("g t s -> t g s")).then_inc(ld_ws, 16)
        for n, (w, k0, nk, c0, _, _) in enumerate(PIECES):
            if n >= RAW:
                sp.wait_ge(lo_done, n - RAW + 1)
            dst = raw[:, n % RAW, 0:nk * PC].rearrange("p (t n) -> p t n", n=PC)
            sp.dma_start(dst, W[w][:, k0:k0 + nk, c0:c0 + PC]).then_inc(landed[n % RAW], 16)

        def load(ps, e, p, source_expert):
            sp.wait_ge(lo_done, piece_no(ps, e, p) - RAW + 1)
            dst = raw[:, p % RAW, :].rearrange("p (t n) -> p t n", n=EC)
            sp.dma_start(dst, moe_source(source_expert, p)).then_inc(landed[p % RAW], 16)

        def run_pass(ps):
            with sp.Fori(0, EXPERTS) as e:
                for p in range(SPLIT, NE):
                    load(ps, e, p, e)
                for p in range(SPLIT):
                    load(ps, e + 1, p, (e + 1) % EXPERTS)

        for p in range(SPLIT):
            load(0, 0, p, 0)
        run_pass(0)
        sp.wait_ge(flag_ready, 1)
        most = sp.value_load(flag[0:1, 0:1])
        with sp.If(most > CAP):
            with sp.Fori(1, 3) as ps:
                run_pass(ps)
        sp.wait_ge(stored, 16 * 6)

    @block.gpsimd
    def _(pool):
        own = Own(pool, pool_own)
        own(pool.memset(ident[:, :], 0.0))
        pool.memset(ones[:, :], 1.0).then_inc(consts, 1)
        own.settle()
        pool.affine_select(out=ident[:, :], in_=ident[:, :], compare_op=ALU.not_equal, fill=1.0, base=0,
                           pattern=[[-1, P]], channel_multiplier=1).then_inc(consts, 1)
        pool.dma_start(wr[:, :, :], a["moe_w_router"][0].rearrange("(t p) n -> p t n", p=P)).then_inc(ld_wr, 16)
        pool.wait_ge(*job_out("vec"))
        pool.dma_start(bsb[:, :, :], a["a_b_s"].to_broadcast([P, KT, P])).then_inc(ld_misc, 16)
        pool.wait_ge(*job_out("ws_t", 0))
        pool.wait_ge(*job_out("ws_t", 1))
        pool.affine_select(out=wsT[:, :, :], in_=wsT[:, :, :], compare_op=ALU.is_ge, fill=0.0, base=0,
                           pattern=[[0, KT], [1, P]], channel_multiplier=-1).then_inc(ws_masked, 1)

        def store_memory(i, stage):
            pool.wait_ge(*stage_out(f"v{i}", 4))
            pool.dma_start(out["v"][i, 0].rearrange("(m p) h d -> p m (h d)", p=P), vm[:, :, :]).then_inc(vm_out, 16)
            pool.wait_ge(*job_out(f"k_tok{i}", 3))
            pool.dma_start(out["k"][i, 0].rearrange("(m p) h d -> p m (h d)", p=P), stage[:, :, :]).then_inc(kst_out, 16)

        def load_caches(i):
            for j in range(2 * TS):
                n = i * 2 * TS + j
                if n >= 3:
                    li, lj = (n - 3) // (2 * TS), (n - 3) % (2 * TS)
                    if lj < TS:
                        pool.wait_ge(*job_out(f"q_bc{li}", 2 * lj + 1))
                    elif lj < 2 * TS - 1:
                        pool.wait_ge(vused, (TS - 1) * li + lj - TS + 1)
                    else:
                        pool.wait_ge(aux_ready, AUX[f"s_o{li}"] + 2)
                src = a["cache_mem_v" if j >= TS else "cache_mem_k"][i, j % TS].rearrange("(m p) h d -> p m (h d)", p=P)
                pool.dma_start(kv[:, n % 3, :, :], src).then_inc(kv_in[n % 3], 16)

        store_memory(0, kst)
        pool.wait_ge(*job_out("v_smp", 1))
        pool.dma_start(out["chunk"].rearrange("l b s d -> (l b s) d"), vs_out[:, :]).then_inc(stored, 16)
        pool.wait_ge(kst_out, 16)
        pool.wait_ge(stored, 16)
        pool.wait_ge(x_done, XW["mixed"] + 8)
        load_caches(0)
        pool.wait_ge(piece_done, FIRST["pw1"])
        pool.memset(ce[:, :, 0:STATE], 0.0).then_inc(pad_done, 1)
        for half in range(2):
            src = a["state_conv"][0, 4 * half:4 * half + 4].rearrange("s j d -> (s j) d")
            pool.dma_start(st_in[:, half, :], src).then_inc(ld_state, 16)
        pool.dma_start(out["conv_s"][0, :, 0:STATE - 1, :], a["state_conv"][0, :, 1:STATE, :]).then_inc(stored, 16)
        store_memory(1, kst1)
        pool.wait_ge(*job_out("c_tok", 3))
        pool.wait_ge(*job_out("c_tok", 1))
        pool.dma_start(out["conv_p"][0, 0], c_out[:, :]).then_inc(stored, 16)
        pool.dma_start(out["conv_s"][0, :, STATE - 1, :], cs_out[:, :]).then_inc(stored, 16)
        pool.wait_ge(kst_out, 32)
        pool.wait_ge(vm_out, 32)
        pool.wait_ge(stored, 16 * 4)
        pool.wait_ge(x_done, XW["conv"] + 8)
        load_caches(1)
        pool.wait_ge(piece_done, ND)
        pool.dma_start(grow[:, :], a["norm_final"].rearrange("(o d) -> o d", o=1).to_broadcast([P, D])).then_inc(ld_grow, 16)
        pool.iota(iota[:, :], pattern=[[1, CAP]], base=0, channel_multiplier=0,
                  allow_small_or_imprecise_dtypes=True).then_inc(moe_const, 1)
        own(pool.memset(tri[:, :], 1.0))
        own.settle()
        pool.affine_select(out=tri[:, :], in_=tri[:, :], compare_op=ALU.is_gt, fill=0.0, base=0,
                           pattern=[[1, P]], channel_multiplier=-1).then_inc(moe_const, 1)
        pool.wait_ge(fin_done, 3)
        pool.dma_start(out["y"][0].rearrange("(m p) d -> p m d", p=P), yo[:, 0:2, :]).then_inc(stored, 16)
        pool.dma_start(out["ys"].rearrange("b s d -> (b s) d"), yo[0:TS, 2, :]).then_inc(stored, 16)
        pool.wait_ge(stored, 16 * 6)

    @block.tensor
    def _(pe):
        def aux(name, j=0):
            n = AUX[name] + j
            if n >= 4:
                pe.wait_ge(aux_free[n % 4], n // 4)
            return bank[4 + n % 4]

        def product(stage, count, hi, lo, ready=None, tokens_stationary=False, start=0):
            for n in range(FIRST[stage] + start, FIRST[stage] + start + count):
                _, k0, nk, _, opens, closes = PIECES[n]
                g = GROUP[n]
                pe.wait_ge(lo_done, n + 1)
                for o in range(2):
                    b = 2 * (g % 2) + o
                    if opens and g >= 2:
                        pe.wait_ge(evac[b], g // 2)
                    for k in range(nk):
                        if ready is not None and n == FIRST[stage] and o == 0:
                            pe.wait_ge(ready[0], ready[1] + k + 1)
                        w_hi = whi[:, n % SPLIT, k * PC:(k + 1) * PC]
                        w_lo = wlo[:, n % SPLIT, k * PC:(k + 1) * PC]
                        first, last = opens and k == 0, closes and k == nk - 1
                        if tokens_stationary:
                            x_hi, x_lo = hi[:, k0 + k, o * P:(o + 1) * P], lo[:, k0 + k, o * P:(o + 1) * P]
                            y = bank[b][:, 0:PC]
                            pe.matmul(y, x_hi, w_hi, start=first, stop=False)
                            pe.matmul(y, x_hi, w_lo, start=False, stop=False)
                            mm = pe.matmul(y, x_lo, w_hi, start=False, stop=last)
                        else:
                            x_hi, x_lo = hi[:, k0 + k, :], lo[:, k0 + k, :]
                            y = bank[b][:, 0:hi.shape[2]]
                            cols = slice(o * P, (o + 1) * P)
                            pe.matmul(y, w_hi[:, cols], x_hi, start=first, stop=False)
                            pe.matmul(y, w_hi[:, cols], x_lo, start=False, stop=False)
                            mm = pe.matmul(y, w_lo[:, cols], x_hi, start=False, stop=last)
                    if o == 0 and closes:
                        mm.then_inc(tile0_done, 1)
                mm.then_inc(piece_done, 1)

        def channel_sum(job, src, ready):
            y = aux(job)
            pe.wait_ge(*ready)
            for k in range(KT):
                mm = pe.matmul(y[:, 0:T], ones[:, :], src[:, k, :], start=(k == 0), stop=(k == KT - 1))
            mm.then_inc(aux_ready, 1)

        def turn(dst, src, rows_):
            return pe.transpose(dst, src, ident[0:rows_, 0:rows_])

        pe.wait_ge(consts, 2)
        pe.wait_ge(ld_rows, 160)
        y = aux("vec")
        for k in range(KT):
            mm = turn(y[:, k * NV:(k + 1) * NV], rows[:, k * P:(k + 1) * P], NV)
        mm.then_inc(aux_ready, 1)
        pe.wait_ge(mem_n, 2)
        for j in range(4):
            y = aux("mem_t", j)
            for kk in range(2):
                for m in range(2):
                    k = 2 * j + kk
                    mm = turn(y[:, kk * MEM + m * P:kk * MEM + (m + 1) * P], mem_in[:, m, k * P:(k + 1) * P], P)
            mm.then_inc(aux_ready, 1)
        pe.wait_ge(ld_x, 32)
        for k in range(KT):
            y = aux("x_t", k)
            for m in range(2):
                turn(y[:, m * P:(m + 1) * P], x_in[:, m, k * P:(k + 1) * P], P)
            turn(y[:, TP:T], x_in[0:TS, 2, k * P:(k + 1) * P], TS).then_inc(aux_ready, 1)
        pe.wait_ge(ld_ws, 16)
        for j in range(2):
            y = aux("ws_t", j)
            for gg in range(4):
                mm = turn(y[:, gg * P:(gg + 1) * P], ws_in[:, 4 * j + gg, :], P)
            mm.then_inc(aux_ready, 1)
        pe.matmul(aux("ws_0")[:, 0:KT], ones[0:1, :], ws_in[0:1, :, 0], start=True, stop=True).then_inc(aux_ready, 1)

        def memory(i, hi, lo, ready):
            product(f"k{i}", 4, hi, lo, ready)
            if i == 0:
                channel_sum("rms_mix0", sq, (sq_done, SQ["mix0"]))
            product(f"v{i}", 4, hi, lo, None, True)
            pe.wait_ge(*stage_out(f"k{i}", 4))
            for j in range(4):
                y = aux(f"k_tok{i}", j)
                m, half = j // 2, j % 2
                for kk in range(4):
                    mm = turn(y[:, kk * P:(kk + 1) * P], kT[:, 4 * half + kk, m * P:(m + 1) * P], P)
                mm.then_inc(aux_ready, 1)

        memory(0, mh[:, :, :], ml[:, :, :], (m_done, 0))
        x_hi, x_lo = xh[:, :, :], xl[:, :, :]
        product("in_v", 4, x_hi, x_lo, (x_done, XW["mix0"]))
        product("in_u", 1, x_hi, x_lo)
        channel_sum("ln_a0", vT, stage_out("in_v", 4))
        product("in_u", 2, x_hi, x_lo, start=1)
        channel_sum("ln_b0", sq, (lnsq_done, 1))
        product("in_u", 1, x_hi, x_lo, start=3)
        pe.wait_ge(lnv_done, 1)
        for j in range(2):
            y = aux("v_smp", j)
            for kk in range(4):
                mm = turn(y[0:TS, kk * P:(kk + 1) * P], vT[:, 4 * j + kk, TP:T], P)
            mm.then_inc(aux_ready, 1)
        for j in range(4):
            y = aux("v_tok", j)
            c, half = j // 2, j % 2
            for kk in range(4):
                mm = turn(y[:, kk * P:(kk + 1) * P], vT[:, 4 * half + kk, c * CHUNK:(c + 1) * CHUNK], P)
            mm.then_inc(aux_ready, 1)
        pe.wait_ge(ws_masked, 1)
        pe.wait_ge(*job_out("v_tok", 3))
        for j in range(4):
            y = aux("mixed", j)
            for gg in range(2):
                g = 2 * j + gg
                for c in range(2):
                    mm = pe.matmul(y[:, (2 * gg + c) * P:(2 * gg + c + 1) * P], vtok[:, c, g * P:(g + 1) * P], wsT[:, g, :],
                                   start=(gg == 0 and c == 0), stop=True, skip_group_check=True)
            mm.then_inc(aux_ready, 1)
        product("a_out", 4, x_hi, x_lo, (x_done, XW["mixed"]))

        def attention(i):
            channel_sum(f"rms_xatt{i}", sq, (sq_done, SQ[f"xatt{i}"]))
            product(f"q{i}", 4, x_hi, x_lo, (x_done, XW[f"xatt{i}"]))
            pe.wait_ge(*stage_out(f"q{i}", 4))
            for j in range(2):
                y = aux(f"q_tok{i}", j)
                for kk in range(4):
                    mm = turn(y[0:TS, kk * P:(kk + 1) * P], qT[:, 4 * j + kk, TP:T], P)
                mm.then_inc(aux_ready, 1)
            for j in range(4):
                y = aux(f"scores{i}", j)
                tt, hh = j // 2, j % 2
                for h2 in range(2):
                    for dh in range(2):
                        f = 2 * (2 * hh + h2) + dh
                        mm = pe.matmul(y[:, h2 * MEM:(h2 + 1) * MEM], qT[:, f, tt * P:(tt + 1) * P], kT[:, f, :],
                                       start=(h2 == 0 and dh == 0), stop=(dh == 1), skip_group_check=True)
                mm.then_inc(aux_ready, 1)
            pe.wait_ge(*job_out(f"q_tok{i}", 1))
            for s in range(TS):
                for c in range(2):
                    y = aux(f"q_bc{i}", 2 * s + c)
                    pe.matmul(y[:, :], ident[0:TS, s:s + 1].to_broadcast([TS, P]), qs[:, c * 512:(c + 1) * 512],
                              start=True, stop=True).then_inc(aux_ready, 1)
            pe.wait_ge(*job_out(f"q_bc{i}", 15))
            y = aux(f"s_t{i}")
            for mt in range(2):
                mm = turn(y[0:TS * HEADS, mt * P:(mt + 1) * P], sc[:, mt, :], P)
            mm.then_inc(aux_ready, 1)
            for j in range(4):
                tt, mt = j // 2, j % 2
                y = aux(f"p_t{i}", j)
                pe.wait_ge(p_done, 4 * i + 2 * tt + 2)
                for h in range(HEADS):
                    mm = turn(y[:, h * P:(h + 1) * P], pr[:, tt, h, mt * P:(mt + 1) * P], P)
                mm.then_inc(aux_ready, 1)
            y = aux(f"ps_t{i}")
            pe.wait_ge(sp_done, i + 1)
            for mt in range(2):
                mm = turn(y[:, mt * 32:(mt + 1) * 32], psm[:, mt * P:(mt + 1) * P], TS * HEADS)
            mm.then_inc(aux_ready, 1)
            pe.wait_ge(*job_out(f"p_t{i}", 3))
            for j in range(4):
                y = aux(f"o_t{i}", j)
                for ff in range(2):
                    f = 2 * j + ff
                    for mt in range(2):
                        mm = pe.matmul(y[:, ff * TP:(ff + 1) * TP], vm[:, mt, f * P:(f + 1) * P], pT[:, mt, f // 2, :],
                                       start=(ff == 0 and mt == 0), stop=(mt == 1), skip_group_check=True)
                mm.then_inc(aux_ready, 1)
            y = [aux(f"s_o{i}", 0), aux(f"s_o{i}", 1)]
            pe.wait_ge(*job_out(f"ps_t{i}"))
            for s in range(TS):
                n = i * 2 * TS + TS + s
                pe.wait_ge(kv_in[n % 3], 16 * (n // 3 + 1))
                for h in range(HEADS):
                    for mt in range(2):
                        mm = pe.matmul(y[h // 2][0:TS, (h % 2) * HD:(h % 2 + 1) * HD], pz[:, mt, h, s, :],
                                       kv[:, n % 3, mt, h * HD:(h + 1) * HD],
                                       start=(s == 0 and h % 2 == 0 and mt == 0), stop=(s == TS - 1 and mt == 1),
                                       skip_group_check=True)
                    if s == TS - 1 and h % 2 == 1:
                        mm.then_inc(aux_ready, 1)
                if s < TS - 1:
                    mm.then_inc(vused, 1)
            y = aux(f"os_t{i}")
            pe.wait_ge(*job_out(f"s_o{i}", 1))
            for k in range(KT):
                mm = turn(y[:, k * TS:(k + 1) * TS], qs[:, k * P:(k + 1) * P], TS)
            mm.then_inc(aux_ready, 1)
            product(f"o{i}", 4, x_hi, x_lo, (x_done, XW[f"att{i}"]))

        attention(0)
        channel_sum("rms_ffn0", sq, (sq_done, SQ["ffn0"]))
        product("gate_up", 22, x_hi, x_lo, (x_done, XW["ffn0"]))
        pe.wait_ge(a_done, FT)
        product("down", 12, ah[:, :, :], al[:, :, :])
        channel_sum("rms_mix1", sq, (sq_done, SQ["mix1"]))
        product("pw1", 8, x_hi, x_lo, (x_done, XW["mix1"]))
        pe.wait_ge(ld_state, 32)
        for j in range(4):
            y = aux("state_t", j)
            half, kq = j // 2, j % 2
            for kk in range(4):
                mm = turn(y[:, kk * 120:(kk + 1) * 120], st_in[:, half, (4 * kq + kk) * P:(4 * kq + kk + 1) * P], 4 * STATE)
            mm.then_inc(aux_ready, 1)
        memory(1, xh[:, :, 0:MEM], xl[:, :, 0:MEM], (x_done, XW["mem1"]))
        for j in range(4):
            y = aux("c_tok", j)
            for kk in range(4):
                k = 4 * (j % 2) + kk
                if j < 2:
                    mm = turn(y[0:STATE, kk * P:(kk + 1) * P], ce[:, k, TP:TP + STATE], P)
                else:
                    mm = turn(y[0:TS, kk * P:(kk + 1) * P], se[:, k, :, STATE], P)
            mm.then_inc(aux_ready, 1)
        channel_sum("ln_a1", cv, (conv_done, 1))
        channel_sum("ln_b1", sq, (lnsq_done, 2))
        product("pw2", 4, x_hi, x_lo, (x_done, XW["conv"]))
        attention(1)
        channel_sum("rms_ffn1", sq, (sq_done, SQ["ffn1"]))

        TT = ((0, P), (1, P), (2, TS))
        E1 = EXPERTS + 1
        y = aux("route")
        pe.wait_ge(hn_ready, 8)
        pe.wait_ge(ld_wr, 16)
        for tt, n_rows in TT:
            for k in range(KT):
                mm = pe.matmul(y[0:n_rows, tt * 16:tt * 16 + EXPERTS], sq[:, k, tt * P:tt * P + n_rows], wr[:, k, :],
                               start=(tt == 0 and k == 0), stop=(k == KT - 1), skip_group_check=True)
        mm.then_inc(aux_ready, 1)
        pe.wait_ge(mask_done, 1)
        pe.wait_ge(moe_const, 2)
        chosen = rt[:, 0, :, :]
        y = aux("pos", 0)
        for tt, n_rows in TT:
            for t2 in range(tt):
                pe.matmul(y[0:n_rows, tt * 16:tt * 16 + E1], ones[:, 0:n_rows], chosen[:, t2, :],
                          start=(tt == 0), stop=False, skip_group_check=True)
            mm = pe.matmul(y[0:n_rows, tt * 16:tt * 16 + E1], tri[0:n_rows, 0:n_rows], chosen[0:n_rows, tt, :],
                           start=(tt == 0), stop=True, skip_group_check=True)
        mm.then_inc(aux_ready, 1)
        y = aux("pos", 1)
        for tt, n_rows in TT:
            mm = pe.matmul(y[:, 0:E1], ones[0:n_rows, :], chosen[0:n_rows, tt, :], start=(tt == 0), stop=(tt == 2))
        mm.then_inc(aux_ready, 1)
        for name, src in (("hn_tok", sq), ("y_tok", hT)):
            for j in range(6):
                y = aux(name, j)
                tt, half = j // 2, j % 2
                n_rows = TT[tt][1]
                for kk in range(4):
                    mm = turn(y[0:n_rows, kk * P:(kk + 1) * P], src[:, 4 * half + kk, tt * P:tt * P + n_rows], P)
                mm.then_inc(aux_ready, 1)

        G, U, ACC, TB, XB = (bank[0], bank[2]), (bank[1], bank[3]), (bank[4], bank[5]), bank[6], bank[7]

        def gather(ready):
            pe.wait_ge(s_built, ready)
            for dst, k0 in ((XB, 0), (G[1], 4)):
                for kk in range(4):
                    for tt, n_rows in TT:
                        for part in (hth, htl):
                            mm = pe.matmul(dst[:, kk * CAP:(kk + 1) * CAP], part[0:n_rows, tt, (k0 + kk) * P:(k0 + kk + 1) * P],
                                           sr[0:n_rows, tt, :], start=(tt == 0 and kk == 0 and same(part, hth)),
                                           stop=(tt == 2 and same(part, htl)), skip_group_check=True)
                mm.then_inc(gat_ready, 1)

        def prepare(column):
            for tt, n_rows in TT:
                pe.matmul(XB[:, tt * P:tt * P + n_rows], sf[0:n_rows, tt, :], ident[0:n_rows, 0:n_rows], is_transpose=True,
                          start=(tt == 0), stop=True, skip_group_check=True)
            for tt, n_rows in TT:
                mm = pe.matmul(XB[:, 272:273], sf[0:n_rows, tt, :], rt[0:n_rows, 1, tt, bass.ds(column, 1)],
                               start=False, stop=(tt == 2), skip_group_check=True)
            mm.then_inc(prep_ready, 1)

        def transposes(ps, e, c):
            pe.wait_ge(h_done, 56 * ps + 7 * e + c + 1)
            if c == 0:
                pe.wait_ge(y_added, 48 * ps + 6 * e + 2)
            else:
                pe.wait_ge(hTl_done, 56 * ps + 7 * e + c)
            for k in range(4):
                mm = turn(TB[:, k * P:(k + 1) * P], hb[:, c % 2, k * P:(k + 1) * P], P)
            mm.then_inc(t_ready, 1)

        def expert(ps, e):
            for p, (kind, c, half) in enumerate(EP):
                if kind == "u" and half == 0 and c >= 1:
                    transposes(ps, e, c - 1)
                if p == NE - 2:
                    transposes(ps, e, CH - 1)
                    pe.wait_ge(prep_done, 9 * ps + e + 1)
                    gather(9 * ps + e + 2)
                pe.wait_ge(lo_done, piece_no(ps, e, p) + 1)
                if half == 0:
                    if kind == "g" and c == 0:
                        pe.wait_ge(xel_done, 18 * ps + 2 * e + 2)
                    if kind == "g" and c < 2:
                        pe.wait_ge(y_added, 48 * ps + 6 * e + 4 + 2 * c)
                    elif kind == "g":
                        pe.wait_ge(silu_done, 56 * ps + 7 * e + c - 1)
                    elif kind == "u" and c >= 2:
                        pe.wait_ge(h_done, 56 * ps + 7 * e + c - 1)
                    elif kind == "d":
                        pe.wait_ge(hTl_done, 56 * ps + 7 * e + c + 1)
                y = {"g": G[c % 2], "u": U[c % 2], "d": ACC[half]}[kind]
                for k in range(4):
                    w_hi, w_lo = whi[:, p % SPLIT, k * EC:(k + 1) * EC], wlo[:, p % SPLIT, k * EC:(k + 1) * EC]
                    if kind == "d":
                        x_hi, x_lo = hTh[:, k * P:(k + 1) * P], hTl[:, k * P:(k + 1) * P]
                        first, last = c == 0 and k == 0, c == CH - 1 and k == 3
                    else:
                        x_hi, x_lo = xeh[:, 4 * half + k, :], xel[:, 4 * half + k, :]
                        first, last = half == 0 and k == 0, half == 1 and k == 3
                    pe.matmul(y[:, :], x_hi, w_hi, start=first, stop=False)
                    pe.matmul(y[:, :], x_hi, w_lo, start=False, stop=False)
                    mm = pe.matmul(y[:, :], x_lo, w_hi, start=False, stop=last)
                mm.then_inc(piece_done, 1)
            pe.wait_ge(oel_done, 16 * ps + 2 * e + 2)
            pe.wait_ge(xel_done, 18 * ps + 2 * e + 4)
            for j, dst in enumerate((XB, TB, G[0], U[0], G[1], U[1])):
                tt, half = SCATTER[j]
                n_rows = TT[tt][1]
                cols = slice(half * 512, (half + 1) * 512)
                pe.matmul(dst[0:n_rows, :], st[:, tt * P:tt * P + n_rows], oeh[:, cols], start=True, stop=False)
                pe.matmul(dst[0:n_rows, :], st[:, tt * P:tt * P + n_rows], oel[:, cols], start=False,
                          stop=True).then_inc(sca_ready, 1)
            pe.wait_ge(y_added, 48 * ps + 6 * e + 7)
            prepare(e + 1)

        def run_pass(ps):
            if not (isinstance(ps, int) and ps == 0):
                pe.wait_ge(y_added, 48 * ps + 6)
                pe.wait_ge(prep_done, 9 * ps)
            gather(9 * ps + 1)
            pe.wait_ge(xel_done, 18 * ps + 2)
            prepare(0)
            with pe.Fori(0, EXPERTS) as e:
                expert(ps, e)

        pe.wait_ge(*job_out("y_tok", 5))
        run_pass(0)
        pe.wait_ge(flag_ready, 1)
        most = pe.value_load(flag[0:1, 0:1])
        with pe.If(most > CAP):
            with pe.Fori(1, 3) as ps:
                run_pass(ps)

    @block.scalar
    def _(act):
        own = Own(act, act_own)

        def width(n):
            return PIECES[n][2] * PC if n < ND else PIECE

        def split(n):
            act.wait_ge(landed[n % RAW], 16 * (n // RAW + 1))
            if n >= SPLIT:
                act.wait_ge(piece_done, n - SPLIT + 1)
            w = width(n)
            act.activation(whi[:, n % SPLIT, 0:w], raw[:, n % RAW, 0:w], ACT.Copy).then_inc(hi_done, 1)

        def pieces(stage, count, post=None, start=0):
            for n in range(FIRST[stage] + start, FIRST[stage] + start + count):
                if post is not None:
                    post(n)
                split(n + SPLIT)

        def job_copy(name, j, dst, rows_=P, cols=512):
            act.wait_ge(aux_ready, AUX[name] + j + 1)
            act.activation(dst, job_bank(name, j)[0:rows_, 0:cols], ACT.Copy).then_inc(job_out(name, j)[0], 1)

        def root(job, slot, eps):
            act.wait_ge(aux_ready, AUX[job] + 1)
            act.activation(stat[:, slot, :], job_bank(job)[:, 0:T], ACT.Sqrt, bias=eps, scale=1.0 / D).then_inc(job_out(job)[0], 1)

        def feed(tag, row=None):
            for k in range(KT):
                act.wait_ge(xn_done, FEED[tag] + k + 1)
                scale = 1.0 if row is None else vecs[:, k, row:row + 1]
                act.activation(xh[:, k, :], sq[:, k, :], ACT.Copy, scale=scale).then_inc(xh_done, 1)

        def memory_hi(i, dst):
            act.wait_ge(*job_out("vec"))
            act.wait_ge(*job_out("mem_t", 3))
            for k in range(KT):
                act.activation(dst[:, k, 0:MEM], memT[:, k, :], ACT.Copy, scale=vecs[:, k, V_MEM + i:V_MEM + i + 1])\
                    .then_inc(mh_done, 1)

        act.wait_ge(mem_sum, 2)
        act.wait_ge(eps_set, 1)
        act.activation(small[:, 4:6], small[:, 2:4], ACT.Sqrt, bias=eps_r, scale=1.0 / D).then_inc(mem_root, 1)
        memory_hi(0, mh)
        for n in range(SPLIT):
            split(n)
        for j in range(2):
            job_copy("ws_t", j, wsT[:, 4 * j:4 * j + 4, :].rearrange("p g s -> p (g s)"))
        pieces("k0", 4)
        root("rms_mix0", 0, eps_r)
        feed("mix0", V_MIX)

        def values(i):
            def post(n):
                for o in range(2):
                    act.wait_ge(*tile_ready(n, o))
                    c = PIECES[n][3]
                    act.activation(vm[:, o, c:c + PC], piece_bank(n, o)[:, 0:PC], ACT.Copy).then_inc(tile_out(n, o)[0], 1)
            return post

        def keys_out(i, dst):
            for j in range(4):
                m, half = j // 2, j % 2
                job_copy(f"k_tok{i}", j, dst[:, m, half * 512:(half + 1) * 512])

        pieces("v0", 4, values(0))
        act.wait_ge(piece_done, FIRST["in_v"])
        keys_out(0, kst)

        def gelu(dst, base):
            def post(n):
                for o in range(2):
                    act.wait_ge(*tile_ready(n, o))
                    f = (PIECES[n][3] - base) // P + o
                    act.activation(dst[:, f, :], piece_bank(n, o)[:, 0:T], ACT.Gelu_apprx_tanh).then_inc(tile_out(n, o)[0], 1)
            return post

        pieces("in_v", 4, gelu(vT, D))
        pieces("in_u", 3, gelu(uT, 0))
        root("ln_b0", 1, eps_l)
        pieces("in_u", 1, gelu(uT, 0), start=3)
        for j in range(2):
            job_copy("v_smp", j, vs_out[:, j * 512:(j + 1) * 512], TS)
        for j in range(4):
            c, half = j // 2, j % 2
            job_copy("v_tok", j, vtok[:, c, half * 512:(half + 1) * 512])
        feed("mixed")
        pieces("a_out", 4)

        def attention(i):
            root(f"rms_xatt{i}", 0, eps_r)
            feed(f"xatt{i}", V_XATT + i)
            pieces(f"q{i}", 4)
            for j in range(4):
                tt, hh = j // 2, j % 2
                act.wait_ge(nmax_done, 4 * i + j + 1)
                for h2 in range(2):
                    h = 2 * hh + h2
                    ins = act.activation(pr[:, tt, h, :], job_bank(f"scores{i}", j)[:, h2 * MEM:(h2 + 1) * MEM], ACT.Exp,
                                         bias=att[:, 8 + 4 * tt + h:9 + 4 * tt + h], scale=SCALE,
                                         accum_out=att[:, 16 + 4 * tt + h:17 + 4 * tt + h])
                ins.then_inc(job_out(f"scores{i}", j)[0], 1)
            act.wait_ge(snmax_done, i + 1)
            n32 = TS * HEADS
            act.activation(psm[:, :], job_bank(f"s_t{i}")[0:n32, 0:MEM], ACT.Exp, bias=att[0:n32, 33:34], scale=SCALE,
                           accum_out=att[0:n32, 34:35]).then_inc(job_out(f"s_t{i}")[0], 1)
            for j in range(4):
                act.wait_ge(aux_ready, AUX[f"o_t{i}"] + j + 1)
                act.activation(xh[:, 2 * j:2 * j + 2, 0:TP],
                               job_bank(f"o_t{i}", j)[:, :].rearrange("p (f t) -> p f t", f=2), ACT.Copy).then_inc(xoh_done, 1)
            act.wait_ge(*job_out(f"os_t{i}"))
            act.activation(xh[:, :, TP:T], os8[:, :, :], ACT.Copy).then_inc(osh_done, 1)
            pieces(f"o{i}", 4)

        attention(0)
        root("rms_ffn0", 0, eps_r)
        feed("ffn0", V_FFN)

        def gated(func, split_h):
            def post(n):
                c = (n - FIRST["gate_up" if split_h else "pw1"]) // 2
                gate = (n - FIRST["gate_up"]) % 2 == 0
                for o in range(2):
                    slot = 2 * (c % 2) + o
                    if gate:
                        act.wait_ge(*tile_ready(n, o))
                        if c >= 2:
                            act.wait_ge(*tile_out(n - 3, o))
                        act.activation(sg[:, slot, :], piece_bank(n, o)[:, 0:T], func).then_inc(tile_out(n, o)[0], 1)
                    elif split_h:
                        act.wait_ge(*tile_out(n, o))
                        act.activation(ah[:, 2 * c + o, :], af[:, slot, :], ACT.Copy).then_inc(ah_done, 1)
            return post

        pieces("gate_up", 22, gated(ACT.Silu, True))
        pieces("down", 12)
        root("rms_mix1", 0, eps_r)
        feed("mix1", V_MIX + 1)
        act.wait_ge(x_done, XW["mix1"] + 8)
        pieces("pw1", 8, gated(ACT.Sigmoid, False))
        act.wait_ge(piece_done, FIRST["k1"])
        memory_hi(1, xh)
        for j in range(4):
            half, kq = j // 2, j % 2
            act.wait_ge(aux_ready, AUX["state_t"] + j + 1)
            act.activation(se[:, 4 * kq:4 * kq + 4, 4 * half:4 * half + 4, 0:STATE],
                           job_bank("state_t", j)[:, 0:480].rearrange("p (k s j) -> p k s j", k=4, s=4),
                           ACT.Copy).then_inc(job_out("state_t", j)[0], 1)
        pieces("k1", 4)
        act.wait_ge(vm_out, 16)
        pieces("v1", 4, values(1))
        keys_out(1, kst1)
        for j in range(4):
            if j < 2:
                job_copy("c_tok", j, c_out[:, j * 512:(j + 1) * 512], STATE)
            else:
                job_copy("c_tok", j, cs_out[:, (j - 2) * 512:(j - 1) * 512], TS)
        root("ln_b1", 1, eps_l)
        act.wait_ge(lnv_done, 2)
        for k in range(KT):
            act.activation(sq[:, k, :], cv[:, k, :], ACT.Silu).then_inc(xn_done, 1)
        feed("conv")
        pieces("pw2", 4)
        attention(1)
        root("rms_ffn1", 0, eps_r)
        act.wait_ge(gate_gap, 1)
        act.activation(rt[:, 13, :, 0:1], rt[:, 12, :, 0:1], ACT.Exp).then_inc(gate_exp, 1)
        for j in range(6):
            tt, half = j // 2, j % 2
            n_rows = P if tt < 2 else TS
            act.wait_ge(aux_ready, AUX["hn_tok"] + j + 1)
            act.activation(hth[0:n_rows, tt, half * 512:(half + 1) * 512], job_bank("hn_tok", j)[0:n_rows, :],
                           ACT.Copy).then_inc(hth_done, 1)

        G, XB, TB, ACC = (bank[0], bank[2]), bank[7], bank[6], (bank[4], bank[5])

        def split_moe(ps, e, p):
            act.wait_ge(landed[p % RAW], 16 * (ND // RAW + ps * (EXPERTS * NE // RAW) + e * (NE // RAW) + p // RAW + 1))
            act.wait_ge(piece_done, piece_no(ps, e, p) - SPLIT + 1)
            act.activation(whi[:, p % SPLIT, :], raw[:, p % RAW, :], ACT.Copy).then_inc(hi_done, 1)

        def tokens_hi(first):
            for j, src in enumerate((XB, G[1])):
                act.wait_ge(gat_ready, first + j)
                act.activation(xeh[:, 4 * j:4 * j + 4, :], src[:, :].rearrange("p (k r) -> p k r", k=4), ACT.Copy)\
                    .then_inc(xeh_done, 1)

        def h_hi(value):
            act.wait_ge(t_ready, value)
            act.activation(hTh[:, :], TB[:, :], ACT.Copy).then_inc(hTh_done, 1)

        def run_pass(ps):
            tokens_hi(18 * ps + 1)
            with act.Fori(0, EXPERTS) as e:
                for p, (kind, c, half) in enumerate(EP):
                    if kind == "g" and half == 1:
                        act.wait_ge(piece_done, piece_no(ps, e, p) + 1)
                        act.activation(hb[:, c % 2, :], G[c % 2][:, :], ACT.Silu).then_inc(silu_done, 1)
                    if kind == "u" and half == 0 and c >= 1:
                        h_hi(56 * ps + 7 * e + c)
                    if p == NE - 2:
                        h_hi(56 * ps + 7 * e + CH)
                        tokens_hi(18 * ps + 2 * e + 3)
                    split_moe(ps, e, p + SPLIT)
                act.wait_ge(prep_done, 9 * ps + e + 1)
                act.wait_ge(piece_done, piece_no(ps, e, NE))
                for half in range(2):
                    act.activation(oeh[:, half * 512:(half + 1) * 512], ACC[half][:, :], ACT.Copy, scale=gr[:, 0:1])\
                        .then_inc(oeh_done, 1)

        run_pass(0)
        act.wait_ge(flag_ready, 1)
        most = act.value_load(flag[0:1, 0:1])
        with act.If(most > CAP):
            with act.Fori(1, 3) as ps:
                run_pass(ps)
        act.wait_ge(fin_sum, 1)
        act.activation(small[:, 36:39], small[:, 32:35], ACT.Sqrt, bias=eps_r, scale=1.0 / D).then_inc(fin_root, 1)

    @block.vector
    def _(dve):
        own = Own(dve, dve_own)

        def width(n):
            return PIECES[n][2] * PC if n < ND else PIECE

        def split(n):
            dve.wait_ge(hi_done, n + 1)
            w = width(n)
            dve.tensor_tensor(wlo[:, n % SPLIT, 0:w], raw[:, n % RAW, 0:w], whi[:, n % SPLIT, 0:w].bitcast(F32),
                              ALU.subtract).then_inc(lo_done, 1)

        def pieces(stage, count, post=None, start=0):
            for n in range(FIRST[stage] + start, FIRST[stage] + start + count):
                if post is not None:
                    post(n)
                split(n + SPLIT)

        def job_copy(name, j, dst, rows_=P, cols=512):
            dve.wait_ge(aux_ready, AUX[name] + j + 1)
            dve.tensor_copy(dst, job_bank(name, j)[0:rows_, 0:cols]).then_inc(job_out(name, j)[0], 1)

        def to_sbuf(dst, base):
            def post(n):
                for o in range(2):
                    dve.wait_ge(*tile_ready(n, o))
                    f = (PIECES[n][3] - base) // P + o
                    dve.tensor_copy(dst[:, f, :], piece_bank(n, o)[:, 0:dst.shape[2]]).then_inc(tile_out(n, o)[0], 1)
            return post

        def add_residual(n):
            if not PIECES[n][5]:
                return
            for o in range(2):
                dve.wait_ge(*tile_ready(n, o))
                f = PIECES[n][3] // P + o
                dve.tensor_tensor(hT[:, f, :], hT[:, f, :], piece_bank(n, o)[:, 0:T], ALU.add).then_inc(tile_out(n, o)[0], 1)

        def square(before):
            dve.wait_ge(*before)
            dve.tensor_tensor(sq[:, :, :], hT[:, :, :], hT[:, :, :], ALU.mult).then_inc(sq_done, 1)

        def inverse_root(job):
            dve.wait_ge(*job_out(job))
            own(dve.reciprocal(stat[:, 1, :], stat[:, 0, :]))
            own.settle()

        def feed_lo(tag, row=None):
            for k in range(KT):
                dve.wait_ge(xh_done, FEED[tag] + k + 1)
                hi = xh[:, k, :].bitcast(F32)
                if row is None:
                    ins = dve.tensor_tensor(xl[:, k, :], sq[:, k, :], hi, ALU.subtract)
                else:
                    ins = dve.scalar_tensor_tensor(out=xl[:, k, :], in0=sq[:, k, :], scalar=vecs[:, k, row:row + 1], in1=hi,
                                                   op0=ALU.mult, op1=ALU.subtract)
                ins.then_inc(x_done, 1)

        def rms_feed(tag, job, row):
            inverse_root(job)
            for k in range(KT):
                dve.tensor_tensor(sq[:, k, :], hT[:, k, :], stat[:, 1, :], ALU.mult).then_inc(xn_done, 1)
            feed_lo(tag, row)

        def memory_lo(i, hi, lo, done):
            for k in range(KT):
                dve.wait_ge(mh_done, 8 * i + k + 1)
                dve.scalar_tensor_tensor(out=lo[:, k, 0:MEM], in0=memT[:, k, :], scalar=vecs[:, k, V_MEM + i:V_MEM + i + 1],
                                         in1=hi[:, k, 0:MEM].bitcast(F32), op0=ALU.mult, op1=ALU.subtract).then_inc(done, 1)

        def layer_norm_a(job, x):
            dve.wait_ge(aux_ready, AUX[job] + 1)
            dve.tensor_scalar(stat[:, 0, :], job_bank(job)[:, 0:T], 1.0 / D, None, ALU.mult).then_inc(job_out(job)[0], 1)
            dve.wait_ge(*job_out(job))
            for k in range(KT):
                own(dve.tensor_tensor(x[:, k, :], x[:, k, :], stat[:, 0, :], ALU.subtract))
            own.settle()
            dve.tensor_tensor(sq[:, :, :], x[:, :, :], x[:, :, :], ALU.mult).then_inc(lnsq_done, 1)

        def layer_norm_b(job, x, row_g, row_b):
            dve.wait_ge(*job_out(job))
            own(dve.reciprocal(stat[:, 2, :], stat[:, 1, :]))
            own.settle()
            for k in range(KT):
                own(dve.tensor_tensor(x[:, k, :], x[:, k, :], stat[:, 2, :], ALU.mult))
            for k in range(KT):
                own.settle(KT - 1)
                ins = own(dve.tensor_scalar(x[:, k, :], x[:, k, :], vecs[:, k, row_g:row_g + 1], vecs[:, k, row_b:row_b + 1],
                                            ALU.mult, ALU.add))
            own.settle()
            own_signal(lnv_done)

        def own_signal(s):
            dve.sem_inc(s, 1)

        own(dve.memset(small[:, 0:1], RMS_EPS))
        own(dve.memset(small[:, 1:2], LN_EPS))
        for e in range(EXPERTS):
            own(dve.memset(small[:, 24 + e:25 + e], float(EXPERTS - e)))
        own(dve.memset(pz[:, :, :, :, :], 0.0))
        dve.memset(small[:, 32:35], 1.0).then_inc(eps_set, 1)
        dve.wait_ge(ld_mem, 16)
        for m in range(2):
            dve.tensor_tensor_reduce(sq[:, :, :].rearrange("p k t -> p (k t)")[:, m * D:(m + 1) * D], mem_in[:, m, :],
                                     mem_in[:, m, :], 1.0, 0.0, ALU.mult, ALU.add, small[:, 2 + m:3 + m]).then_inc(mem_sum, 1)
        dve.wait_ge(mem_root, 1)
        own(dve.reciprocal(small[:, 6:8], small[:, 4:6]))
        own.settle()
        for m in range(2):
            dve.tensor_scalar(mem_in[:, m, :], mem_in[:, m, :], small[:, 6 + m:7 + m], None, ALU.mult).then_inc(mem_n, 1)
        job_copy("vec", 0, vecs[:, :, :].rearrange("p k v -> p (k v)"), P, KT * NV)
        for j in range(4):
            job_copy("mem_t", j, memT[:, 2 * j:2 * j + 2, :].rearrange("p k m -> p (k m)"))
        memory_lo(0, mh, ml, m_done)
        for k in range(KT):
            job_copy("x_t", k, hT[:, k, :], P, T)
        dve.wait_ge(mem_sum, 2)
        square(job_out("x_t", KT - 1))
        job_copy("ws_0", 0, ws0, P, KT)
        for n in range(SPLIT):
            split(n)
        pieces("k0", 4, to_sbuf(kT, 0))
        rms_feed("mix0", "rms_mix0", V_MIX)
        pieces("v0", 4)
        pieces("in_v", 4)
        pieces("in_u", 1)
        layer_norm_a("ln_a0", vT)
        pieces("in_u", 2, start=1)
        layer_norm_b("ln_b0", vT, V_ALNG, V_ALNB)
        pieces("in_u", 1, start=3)
        dve.wait_ge(ld_misc, 16)
        dve.wait_ge(*job_out("ws_0"))
        own(dve.tensor_tensor(sq[:, :, TP:T], vT[:, :, TP:T], ws0.unsqueeze(2).to_broadcast([P, KT, TS]), ALU.mult))
        own.settle()
        own(dve.tensor_tensor(sq[:, :, TP:T], sq[:, :, TP:T], bs0.unsqueeze(2).to_broadcast([P, KT, TS]), ALU.add))
        for j in range(4):
            dve.wait_ge(aux_ready, AUX["mixed"] + j + 1)
            for gg in range(2):
                g = 2 * j + gg
                ins = dve.tensor_tensor(sq[:, g, 0:TP].rearrange("p (c t) -> p c t", c=2),
                                        job_bank("mixed", j)[:, gg * TP:(gg + 1) * TP].rearrange("p (c t) -> p c t", c=2),
                                        bsb[:, g:g + 1, :].to_broadcast([P, 2, P]), ALU.add)
            ins.then_inc(job_out("mixed", j)[0], 1)
        dve.wait_ge(*stage_out("in_u", 4))
        own.settle()
        for k in range(KT):
            if k % 2 == 0:
                dve.wait_ge(*job_out("mixed", k // 2))
            dve.tensor_tensor(sq[:, k, :], sq[:, k, :], uT[:, k, :], ALU.mult).then_inc(xn_done, 1)
        feed_lo("mixed")
        pieces("a_out", 4, add_residual)
        square(stage_out("a_out", 4))

        def attention(i):
            rms_feed(f"xatt{i}", f"rms_xatt{i}", V_XATT + i)
            pieces(f"q{i}", 4, to_sbuf(qT, 0))
            if i == 1:
                dve.wait_ge(stored, 16 * 4)
            for j in range(2):
                job_copy(f"q_tok{i}", j, qs[:, j * 512:(j + 1) * 512], TS)
            for j in range(4):
                tt, hh = j // 2, j % 2
                c = 4 * tt + 2 * hh
                dve.wait_ge(aux_ready, AUX[f"scores{i}"] + j + 1)
                own(dve.tensor_reduce(att[:, c:c + 2], job_bank(f"scores{i}", j)[:, :].rearrange("p (h m) -> p h m", h=2),
                                      AX.X, ALU.max))
                own.settle()
                dve.tensor_scalar(att[:, 8 + c:10 + c], att[:, c:c + 2], -SCALE, None, ALU.mult).then_inc(nmax_done, 1)
            for j in range(4):
                tt, hh = j // 2, j % 2
                c = 4 * tt + 2 * hh
                dve.wait_ge(*job_out(f"scores{i}", j))
                own(dve.reciprocal(att[:, 24 + c:26 + c], att[:, 16 + c:18 + c]))
                own.settle()
                for h2 in range(2):
                    h = 2 * hh + h2
                    ins = dve.tensor_scalar(pr[:, tt, h, :], pr[:, tt, h, :], att[:, 24 + c + h2:25 + c + h2], None, ALU.mult)
                ins.then_inc(p_done, 1)
            for s in range(TS):
                n = i * 2 * TS + s
                dve.wait_ge(kv_in[n % 3], 16 * (n // 3 + 1))
                for c in range(2):
                    j = 2 * s + c
                    dve.wait_ge(aux_ready, AUX[f"q_bc{i}"] + j + 1)
                    for h in (2 * c, 2 * c + 1):
                        for mt in range(2):
                            k = kv[:, n % 3, mt, h * HD:(h + 1) * HD]
                            ins = dve.tensor_tensor_reduce(k, k, job_bank(f"q_bc{i}", j)[:, (h % 2) * HD:(h % 2 + 1) * HD],
                                                           1.0, 0.0, ALU.mult, ALU.add,
                                                           sc[:, mt, s * HEADS + h:s * HEADS + h + 1])
                    ins.then_inc(job_out(f"q_bc{i}", j)[0], 1)
            n32 = TS * HEADS
            dve.wait_ge(aux_ready, AUX[f"s_t{i}"] + 1)
            own(dve.tensor_reduce(att[0:n32, 32:33], job_bank(f"s_t{i}")[0:n32, 0:MEM], AX.X, ALU.max))
            own.settle()
            dve.tensor_scalar(att[0:n32, 33:34], att[0:n32, 32:33], -SCALE, None, ALU.mult).then_inc(snmax_done, 1)
            for j in range(2):
                job_copy(f"p_t{i}", j, pT[:, j, :, 0:P])
            dve.wait_ge(*job_out(f"s_t{i}"))
            own(dve.reciprocal(att[0:n32, 35:36], att[0:n32, 34:35]))
            own.settle()
            dve.tensor_scalar(psm[:, :], psm[:, :], att[0:n32, 35:36], None, ALU.mult).then_inc(sp_done, 1)
            for j in range(2, 4):
                job_copy(f"p_t{i}", j, pT[:, j - 2, :, P:TP])
            dve.wait_ge(aux_ready, AUX[f"ps_t{i}"] + 1)
            for mt in range(2):
                src = job_bank(f"ps_t{i}")[:, mt * n32:(mt + 1) * n32].rearrange("p (s h) -> p h s", h=HEADS)
                ins = dve.tensor_copy(pz[:, mt, :, :, :].rearrange("p h s t -> p h (s t)")[:, :, 0:64:9], src)
            ins.then_inc(job_out(f"ps_t{i}")[0], 1)
            for j in range(4):
                dve.wait_ge(xoh_done, 4 * i + j + 1)
                dve.tensor_tensor(xl[:, 2 * j:2 * j + 2, 0:TP], job_bank(f"o_t{i}", j)[:, :].rearrange("p (f t) -> p f t", f=2),
                                  xh[:, 2 * j:2 * j + 2, 0:TP].bitcast(F32), ALU.subtract).then_inc(job_out(f"o_t{i}", j)[0], 1)
            for j in range(2):
                job_copy(f"s_o{i}", j, qs[:, j * 512:(j + 1) * 512], TS)
            job_copy(f"os_t{i}", 0, os8[:, :, :].rearrange("p k s -> p (k s)"), P, KT * TS)
            dve.wait_ge(osh_done, i + 1)
            dve.wait_ge(*job_out(f"o_t{i}", 3))
            for k in range(KT):
                dve.tensor_tensor(xl[:, k, TP:T], os8[:, k, :], xh[:, k, TP:T].bitcast(F32), ALU.subtract).then_inc(x_done, 1)
            pieces(f"o{i}", 4, add_residual)
            square(stage_out(f"o{i}", 4))

        attention(0)
        rms_feed("ffn0", "rms_ffn0", V_FFN)

        def gated(n):
            c = (n - FIRST["gate_up"]) // 2
            if (n - FIRST["gate_up"]) % 2 == 0:
                return
            for o in range(2):
                slot = 2 * (c % 2) + o
                dve.wait_ge(*tile_out(n - 1, o))
                dve.wait_ge(*tile_ready(n, o))
                if c >= 2:
                    dve.wait_ge(a_done, 2 * (c - 2) + o + 1)
                dve.tensor_tensor(af[:, slot, :], sg[:, slot, :], piece_bank(n, o)[:, 0:T], ALU.mult)\
                    .then_inc(tile_out(n, o)[0], 1)
            for o in range(2):
                dve.wait_ge(ah_done, 2 * c + o + 1)
                dve.tensor_tensor(al[:, 2 * c + o, :], af[:, 2 * (c % 2) + o, :], ah[:, 2 * c + o, :].bitcast(F32),
                                  ALU.subtract).then_inc(a_done, 1)

        pieces("gate_up", 22, gated)
        pieces("down", 12, add_residual)
        dve.wait_ge(a_done, FT)
        square(stage_out("down", 12))
        rms_feed("mix1", "rms_mix1", V_MIX + 1)

        def glu(n):
            if (n - FIRST["pw1"]) % 2 == 0:
                return
            c = (n - FIRST["pw1"]) // 2
            for o in range(2):
                f, gate = 2 * c + o, sg[:, 2 * (c % 2) + o, :]
                dve.wait_ge(*tile_out(n - 1, o))
                dve.wait_ge(*tile_ready(n, o))
                y = piece_bank(n, o)
                dve.tensor_tensor(ce[:, f, STATE:STATE + TP], y[:, 0:TP], gate[:, 0:TP], ALU.mult)
                dve.tensor_tensor(se[:, f, :, STATE], y[:, TP:T], gate[:, TP:T], ALU.mult).then_inc(tile_out(n, o)[0], 1)

        pieces("pw1", 8, glu)
        memory_lo(1, xh, xl, x_done)

        def conv_part(quarter):
            k0, q = 4 * (quarter // 4), quarter % 4
            if quarter == 0:
                dve.wait_ge(pad_done, 1)
                dve.wait_ge(*stage_out("pw1", 8))
            for j in range(8 * q, min(8 * q + 8, TAPS)):
                for k in range(k0, k0 + 4):
                    w = vecs[:, k, V_DW + j:V_DW + j + 1]
                    if j == 0:
                        own(dve.tensor_scalar(cv[:, k, 0:TP], ce[:, k, 0:TP], w, vecs[:, k, V_BDW:V_BDW + 1], ALU.mult, ALU.add))
                    else:
                        own.settle(3)
                        own(dve.scalar_tensor_tensor(out=cv[:, k, 0:TP], in0=ce[:, k, j:j + TP], scalar=w, in1=cv[:, k, 0:TP],
                                                     op0=ALU.mult, op1=ALU.add))

        def with_conv(post, first):
            def both(n):
                if post is not None:
                    post(n)
                conv_part(n - FIRST["k1"])
            return both

        pieces("k1", 4, with_conv(to_sbuf(kT, 0), 0))
        pieces("v1", 4, with_conv(None, 4))
        dve.wait_ge(*job_out("state_t", 3))
        for k in range(KT):
            own(dve.tensor_tensor(sq[:, k, 0:TS * TAPS].rearrange("p (s j) -> p s j", s=TS), se[:, k, :, :],
                                  vecs[:, k:k + 1, V_DW:NV].to_broadcast([P, TS, TAPS]), ALU.mult))
        for k in range(KT):
            own.settle(KT - 1)
            own(dve.tensor_reduce(cv[:, k, TP:T], sq[:, k, 0:TS * TAPS].rearrange("p (s j) -> p s j", s=TS), AX.X, ALU.add))
        for k in range(KT):
            own.settle(KT - 1)
            own(dve.tensor_scalar(cv[:, k, TP:T], cv[:, k, TP:T], vecs[:, k, V_BDW:V_BDW + 1], None, ALU.add))
        own.settle()
        own_signal(conv_done)
        layer_norm_a("ln_a1", cv)
        layer_norm_b("ln_b1", cv, V_BLNG, V_BLNB)
        feed_lo("conv")
        pieces("pw2", 4, add_residual)
        square(stage_out("pw2", 4))
        attention(1)

        inverse_root("rms_ffn1")
        for k in range(KT):
            dve.scalar_tensor_tensor(out=sq[:, k, :], in0=hT[:, k, :], scalar=vecs[:, k, V_FFN + 1:V_FFN + 2],
                                     in1=stat[:, 1, :], op0=ALU.mult, op1=ALU.mult).then_inc(hn_ready, 1)
        E = EXPERTS
        own(dve.memset(rt[:, :, :, :], 0.0))
        own.settle()
        dve.wait_ge(aux_ready, AUX["route"] + 1)
        y = job_bank("route")
        own(dve.tensor_copy(rt[:, 3, 0:2, 0:E], y[:, 0:32].rearrange("p (t e) -> p t e", e=16)[:, :, 0:E]))
        dve.tensor_copy(rt[0:TS, 3, 2, 0:E], y[0:TS, 32:32 + E]).then_inc(job_out("route")[0], 1)
        dve.wait_ge(*job_out("route"))
        own.settle()
        L = rt[:, 3, :, 0:E]
        order = order8.unsqueeze(1).to_broadcast([P, 3, E])

        def wide(x):
            return x.to_broadcast([P, 3, E])

        def first_of_largest(x, top, tmp, best, sel):
            own(dve.tensor_reduce(top, x, AX.X, ALU.max))
            own.settle()
            own(dve.tensor_tensor(tmp, x, wide(top), ALU.is_equal))
            own.settle()
            own(dve.tensor_tensor(tmp, tmp, order, ALU.mult))
            own.settle()
            own(dve.tensor_reduce(best, tmp, AX.X, ALU.max))
            own.settle()
            own(dve.tensor_tensor(sel, tmp, wide(best), ALU.is_equal))
            own.settle()

        top1, top2, best = rt[:, 10, :, 0:1], rt[:, 11, :, 0:1], rt[:, 9, :, 0:1]
        sel1, sel2, L2 = rt[:, 5, :, 0:E], rt[:, 8, :, 0:E], rt[:, 6, :, 0:E]
        first_of_largest(L, top1, rt[:, 4, :, 0:E], best, sel1)
        own(dve.scalar_tensor_tensor(out=L2, in0=sel1, scalar=-3.0e38, in1=L, op0=ALU.mult, op1=ALU.add))
        own.settle()
        first_of_largest(L2, top2, rt[:, 4, :, 0:E], best, sel2)
        dve.tensor_tensor(rt[:, 12, :, 0:1], top2, top1, ALU.subtract).then_inc(gate_gap, 1)
        own(dve.tensor_tensor(rt[:, 0, :, 0:E], sel1, sel2, ALU.add))
        own.settle()
        own_signal(mask_done)
        dve.wait_ge(gate_exp, 1)
        gexp, den, w1, w2 = rt[:, 13, :, 0:1], rt[:, 14, :, 0:1], rt[:, 15, :, 0:1], rt[:, 15, :, 1:2]
        own(dve.tensor_scalar(den, gexp, 1.0, None, ALU.add))
        own.settle()
        own(dve.reciprocal(w1, den))
        own.settle()
        own(dve.tensor_tensor(w2, gexp, w1, ALU.mult))
        own(dve.tensor_tensor(sel1, sel1, wide(w1), ALU.mult))
        own.settle()
        own(dve.tensor_tensor(sel2, sel2, wide(w2), ALU.mult))
        own.settle()
        own(dve.tensor_tensor(rt[:, 1, :, 0:E], sel1, sel2, ALU.add))
        dve.wait_ge(aux_ready, AUX["pos"] + 1)
        y = job_bank("pos", 0)
        own(dve.tensor_copy(rt[:, 2, 0:2, :], y[:, 0:32].rearrange("p (t e) -> p t e", e=16)[:, :, 0:E + 1]))
        dve.tensor_copy(rt[0:TS, 2, 2, :], y[0:TS, 32:33 + E]).then_inc(job_out("pos", 0)[0], 1)
        dve.wait_ge(*job_out("pos", 0))
        dve.wait_ge(aux_ready, AUX["pos"] + 2)
        dve.tensor_reduce(small[:, 40:41], job_bank("pos", 1)[:, 0:E], AX.X, ALU.max).then_inc(job_out("pos", 1)[0], 1)
        dve.wait_ge(*job_out("pos", 1))
        dve.tensor_copy(flag[:, 0:1], small[:, 40:41]).then_inc(flag_ready, 1)
        for j in range(6):
            tt, half = j // 2, j % 2
            n_rows = P if tt < 2 else TS
            cols = slice(half * 512, (half + 1) * 512)
            dve.wait_ge(hth_done, j + 1)
            dve.tensor_tensor(htl[0:n_rows, tt, cols], job_bank("hn_tok", j)[0:n_rows, :], hth[0:n_rows, tt, cols].bitcast(F32),
                              ALU.subtract).then_inc(job_out("hn_tok", j)[0], 1)
        for j in range(6):
            tt, half = j // 2, j % 2
            n_rows = P if tt < 2 else TS
            job_copy("y_tok", j, ytok[0:n_rows, tt, half * 512:(half + 1) * 512], n_rows)
        dve.wait_ge(*job_out("y_tok", 5))
        own.settle()
        dve.wait_ge(flag_ready, 1)

        G, U, ACC, TB, XB = (bank[0], bank[2]), (bank[1], bank[3]), (bank[4], bank[5]), bank[6], bank[7]
        ROWS = (P, P, TS)

        def split_moe(ps, e, p):
            dve.wait_ge(hi_done, piece_no(ps, e, p) + 1)
            dve.tensor_tensor(wlo[:, p % SPLIT, :], raw[:, p % RAW, :], whi[:, p % SPLIT, :].bitcast(F32),
                              ALU.subtract).then_inc(lo_done, 1)

        def build_s(column):
            for tt, n_rows in enumerate(ROWS):
                for dst in (sf, sr):
                    ins = dve.tensor_scalar(dst[0:n_rows, tt, :], iota[0:n_rows, :], rt[0:n_rows, 2, tt, bass.ds(column, 1)],
                                            rt[0:n_rows, 0, tt, bass.ds(column, 1)], ALU.is_equal, ALU.mult)
            ins.then_inc(s_built, 1)

        def tokens_lo(first):
            for j, src in enumerate((XB, G[1])):
                dve.wait_ge(xeh_done, first + j)
                dve.tensor_tensor(xel[:, 4 * j:4 * j + 4, :], src[:, :].rearrange("p (k r) -> p k r", k=4),
                                  xeh[:, 4 * j:4 * j + 4, :].bitcast(F32), ALU.subtract).then_inc(xel_done, 1)

        def take_prepared(value):
            dve.wait_ge(prep_ready, value)
            dve.tensor_copy(st[:, :], XB[:, 0:T])
            dve.tensor_copy(gr[:, 0:1], XB[:, 272:273]).then_inc(prep_done, 1)

        def h_lo(value):
            dve.wait_ge(hTh_done, value)
            dve.tensor_tensor(hTl[:, :], TB[:, :], hTh[:, :].bitcast(F32), ALU.subtract).then_inc(hTl_done, 1)

        def run_pass(ps):
            if not (isinstance(ps, int) and ps == 0):
                dve.wait_ge(prep_ready, 9 * ps)
                dve.wait_ge(prep_done, 9 * ps)
                dve.tensor_scalar(rt[:, 2, :, :], rt[:, 2, :, :], float(-CAP), None, ALU.add).then_inc(pos_moved, 1)
                dve.wait_ge(pos_moved, ps)
            build_s(0)
            tokens_lo(18 * ps + 1)
            take_prepared(9 * ps + 1)
            with dve.Fori(0, EXPERTS) as e:
                for p, (kind, c, half) in enumerate(EP):
                    if kind == "u" and half == 0 and c >= 1:
                        h_lo(56 * ps + 7 * e + c)
                    if kind == "u" and half == 1:
                        dve.wait_ge(silu_done, 56 * ps + 7 * e + c + 1)
                        dve.wait_ge(piece_done, piece_no(ps, e, p) + 1)
                        dve.tensor_tensor(hb[:, c % 2, :], hb[:, c % 2, :], U[c % 2][:, :], ALU.mult).then_inc(h_done, 1)
                    if kind == "g" and half == 0 and c == 3:
                        dve.wait_ge(prep_ready, 9 * ps + e + 1)
                        build_s(e + 1)
                    if p == NE - 2:
                        h_lo(56 * ps + 7 * e + CH)
                        tokens_lo(18 * ps + 2 * e + 3)
                    split_moe(ps, e, p + SPLIT)
                for half in range(2):
                    dve.wait_ge(oeh_done, 16 * ps + 2 * e + half + 1)
                    dve.scalar_tensor_tensor(out=oel[:, half * 512:(half + 1) * 512], in0=ACC[half][:, :], scalar=gr[:, 0:1],
                                             in1=oeh[:, half * 512:(half + 1) * 512].bitcast(F32), op0=ALU.mult,
                                             op1=ALU.subtract).then_inc(oel_done, 1)
                dve.wait_ge(y_added, 48 * ps + 6 * e + 6)
                for j, src in enumerate((XB, TB, G[0], U[0], G[1], U[1])):
                    tt, half = SCATTER[j]
                    y = ytok[0:ROWS[tt], tt, half * 512:(half + 1) * 512]
                    dve.wait_ge(sca_ready, 48 * ps + 6 * e + j + 1)
                    dve.tensor_tensor(y, y, src[0:ROWS[tt], :], ALU.add).then_inc(y_added, 1)
                take_prepared(9 * ps + e + 2)
            dve.wait_ge(y_added, 48 * ps + 54)

        dve.sem_inc(y_added, 6)
        dve.wait_ge(moe_const, 2)
        run_pass(0)
        most = dve.value_load(flag[0:1, 0:1])
        with dve.If(most > CAP):
            with dve.Fori(1, 3) as ps:
                run_pass(ps)

        dve.wait_ge(prep_done, 9)
        for tt, n_rows in enumerate(ROWS):
            ins = dve.tensor_tensor_reduce(yo[0:n_rows, tt, :], ytok[0:n_rows, tt, :], ytok[0:n_rows, tt, :], 1.0, 0.0, ALU.mult,
                                           ALU.add, small[0:n_rows, 32 + tt:33 + tt])
        ins.then_inc(fin_sum, 1)
        dve.wait_ge(fin_root, 1)
        own(dve.reciprocal(small[:, 42:45], small[:, 36:39]))
        own.settle()
        dve.wait_ge(ld_grow, 16)
        for tt, n_rows in enumerate(ROWS):
            dve.scalar_tensor_tensor(out=yo[0:n_rows, tt, :], in0=ytok[0:n_rows, tt, :], scalar=small[0:n_rows, 42 + tt:43 + tt],
                                     in1=grow[0:n_rows, :], op0=ALU.mult, op1=ALU.mult).then_inc(fin_done, 1)


_IN = ['x_prompt', 'x_sample', 'mem_prompt', 'cache_mem_k', 'cache_mem_v', 'state_conv', 'norm_mix', 'norm_xattn', 'norm_ffn',
       'norm_mem', 'norm_final', 'w_xq', 'w_xk', 'w_xv', 'w_xo', 'a_w_in', 'a_ln_g', 'a_ln_b', 'a_w_s', 'a_b_s', 'a_w_out',
       'b_w_pw1', 'b_w_dw', 'b_b_dw', 'b_ln_g', 'b_ln_b', 'b_w_pw2', 'ffn_w_gate', 'ffn_w_up', 'ffn_w_down', 'moe_w_router',
       'moe_w_gate', 'moe_w_up', 'moe_w_down']
_OUT = [("y", (1, TP, D)), ("ys", (TS, 1, D)), ("k", (2, 1, MEM, HEADS, HD)), ("v", (2, 1, MEM, HEADS, HD)),
        ("conv_p", (1, 1, STATE, D)), ("conv_s", (1, TS, STATE, D)), ("chunk", (1, TS, 1, D))]


def kernel(**inputs):
    import numpy as np
    import concourse.bacc as bacc
    from concourse.bass_utils import run_bass_kernel_spmd

    nc = bacc.Bacc("TRN2", target_bir_lowering=False, num_devices=1)
    arrays, a, out = {}, {}, {}
    for name in _IN:
        arrays["in_" + name] = np.ascontiguousarray(inputs[name])
        a[name] = nc.dram_tensor("in_" + name, arrays["in_" + name].shape, F32, kind="ExternalInput").ap()
    for name, shape in _OUT:
        out[name] = nc.dram_tensor("out_" + name, shape, F32, kind="ExternalOutput").ap()
    with ExitStack() as ctx:
        build_step(nc, ctx, a, out)
    r = run_bass_kernel_spmd(nc, [arrays], core_ids=[0])
    return tuple(r.results[0]["out_" + name] for name, _ in _OUT)
```

```python
from contextlib import ExitStack

import concourse.bass as bass
from concourse import mybir

F32 = mybir.dt.float32
F32R = mybir.dt.float32r
I32 = mybir.dt.int32
ALU = mybir.AluOpType
ACT = mybir.ActivationFunctionType
AX = mybir.AxisListType

P = 128
D = 1024
KT = D // P
TP = 256
TS = 8
T = TP + TS
MEM = 256
HEADS = 4
HD = D // HEADS
CHUNK = 128
TAPS = 31
STATE = TAPS - 1
FFN = 2816
FT = FFN // P
EXPERTS = 8
EDIM = 3584
RMS_EPS = 1e-6
LN_EPS = 1e-5
SCALE = float(HD) ** -0.5

RAW = 6
SPLIT = 3
PIECE = 2048
PC = 256

(V_MIX, V_XATT, V_FFN, V_MEM, V_ALNG, V_ALNB, V_BDW, V_BLNG, V_BLNB, V_DW) = (0, 2, 4, 6, 8, 9, 10, 11, 12, 13)
NV = V_DW + TAPS

CONV_POOL = 4

EC = 512
CH = EDIM // EC
CAP = 128


def dense_pieces():
    out, first = [], {}

    def add(stage, weight, col, k0=0, nk=KT, opens=True, closes=True):
        first.setdefault(stage, len(out))
        out.append((weight, k0, nk, col, opens, closes))

    def whole(stage, weight, cols, base=0):
        for c in range(cols // PC):
            add(stage, weight, base + c * PC)

    whole("k0", "xk0", D)
    whole("v0", "xv0", D)
    whole("in_v", "a_in", D, D)
    whole("in_u", "a_in", D)
    whole("a_out", "a_out", D)
    whole("q0", "xq0", D)
    whole("o0", "xo0", D)
    for c in range(FFN // PC):
        add("gate_up", "gate", c * PC)
        add("gate_up", "up", c * PC)
    for c in range(D // PC):
        for k0 in range(0, FT, KT):
            add("down", "down", c * PC, k0, min(KT, FT - k0), k0 == 0, k0 + KT >= FT)
    for c in range(D // PC):
        add("pw1", "pw1", D + c * PC)
        add("pw1", "pw1", c * PC)
    whole("k1", "xk1", D)
    whole("v1", "xv1", D)
    whole("pw2", "pw2", D)
    whole("q1", "xq1", D)
    whole("o1", "xo1", D)
    groups, g = [], -1
    for p in out:
        g += p[4]
        groups.append(g)
    return out, groups, first


PIECES, GROUP, FIRST = dense_pieces()
ND = len(PIECES)
assert ND % RAW == 0 and ND % SPLIT == 0

EP = []
for _c in range(CH):
    EP += [("g", _c, 0), ("g", _c, 1), ("u", _c, 0), ("u", _c, 1)]
    if _c:
        EP += [("d", _c - 1, 0), ("d", _c - 1, 1)]
EP += [("d", CH - 1, 0), ("d", CH - 1, 1)]
NE = len(EP)
assert NE % RAW == 0 and NE % SPLIT == 0
SCATTER = ((0, 0), (0, 1), (1, 0), (1, 1), (2, 0), (2, 1))

AUX, _n = {}, 0
_ATT = [("rms_xatt", 1), ("q_tok", 2), ("scores", 4), ("q_bc", 16), ("s_t", 1), ("p_t", 4), ("ps_t", 1), ("o_t", 4),
        ("s_o", 2), ("os_t", 1)]
for _name, _count in (
    [("vec", 1), ("mem_t", 4), ("x_t", 8), ("ws_t", 2), ("ws_0", 1), ("rms_mix0", 1), ("k_tok0", 4), ("ln_a0", 1), ("ln_b0", 1),
     ("v_smp", 2), ("v_tok", 4), ("mixed", 4)] + [(n + "0", c) for n, c in _ATT]
    + [("rms_ffn0", 1), ("rms_mix1", 1), ("state_t", 4), ("k_tok1", 4), ("c_tok", 4), ("ln_a1", 1), ("ln_b1", 1)]
    + [(n + "1", c) for n, c in _ATT] + [("rms_ffn1", 1), ("route", 1), ("pos", 2), ("hn_tok", 6), ("y_tok", 6)]
):
    AUX[_name] = _n
    _n += _count

XW = {n: 8 * i for i, n in enumerate(["mix0", "mixed", "xatt0", "att0", "ffn0", "mix1", "mem1", "conv", "xatt1", "att1"])}
FEED = {n: 8 * i for i, n in enumerate(["mix0", "mixed", "xatt0", "ffn0", "mix1", "conv", "xatt1"])}
XN = {n: 8 * i for i, n in enumerate(["mix0", "mixed", "conv"])}
SQ = {n: i + 1 for i, n in enumerate(["mix0", "xatt0", "ffn0", "mix1", "xatt1", "ffn1"])}


class Own:

    def __init__(self, eng, chain):
        self.eng, self.chain, self.count, self.waited = eng, chain, 0, 0

    def __call__(self, ins):
        self.count += 1
        return ins.then_inc(self.chain, 1)

    def settle(self, lag=0):
        if self.count - lag > self.waited:
            self.waited = self.count - lag
            self.eng.wait_ge(self.chain, self.waited)


def build_step(nc, ctx, a, out):
    place = [-(-nc.sbuf_base // 32) * 32]

    def at(name, shape, dt, off=None):
        size = 4
        for n in shape[1:]:
            size *= n
        if off is None:
            off = place[0]
            place[0] += -(-size // 32) * 32
        assert off % 32 == 0 and off + size <= nc.sbuf_usable_end, (name, off + size, nc.sbuf_usable_end)
        return nc.alloc_sbuf_tensor_at(name, shape, dt, offset=off)

    def sem(name):
        return ctx.enter_context(nc.semaphore(name))

    raw = at("raw", [P, RAW, PIECE], F32)
    whi = at("whi", [P, SPLIT, PIECE], F32R)
    wlo = at("wlo", [P, SPLIT, PIECE], F32R)
    vecs = at("vecs", [P, KT, NV], F32)
    ident = at("ident", [P, P], F32)
    ones = at("ones", [P, P], F32)
    stat = at("stat", [P, 3, T], F32)
    pz = at("pz", [P, 2, HEADS, TS, TS], F32)
    wr = at("wr", [P, KT, EXPERTS], F32)
    small = at("small", [P, 48], F32)
    os8 = at("os8", [P, KT, TS], F32)
    flag = at("flag", [P, 8], I32)
    b_off = place[0]
    hT = at("hT", [P, KT, T], F32)
    xh = at("xh", [P, KT, T], F32R)
    xl = at("xl", [P, KT, T], F32R)
    sq_off = place[0]
    sq = at("sq", [P, KT, T], F32)
    c_off = place[0]
    memT = at("memT", [P, KT, MEM], F32)
    kT = at("kT", [P, KT, MEM], F32)
    vm = at("vm", [P, 2, D], F32)
    e_off = place[0]
    mh = at("mh", [P, KT, MEM], F32R, e_off)
    ml = at("ml", [P, KT, MEM], F32R, e_off + 8192)
    mem_in = at("mem_in", [P, 2, D], F32, e_off + 16384)
    x_in = at("x_in", [P, 3, D], F32, e_off + 24576)
    rows = at("rows", [NV, D], F32, e_off + 37376)
    ws_in = at("ws_in", [P, KT, P], F32, e_off + 41472)
    uT = at("uT", [P, KT, T], F32, e_off)
    vT = at("vT", [P, KT, T], F32, e_off + 8448)
    vtok = at("vtok", [P, 2, D], F32, e_off + 16896)
    kst = at("kst", [P, 2, D], F32, e_off + 25088)
    wsT = at("wsT", [P, KT, P], F32, e_off + 33280)
    bsb = at("bsb", [P, KT, P], F32, e_off + 37376)
    vs_out = at("vs_out", [TS, D], F32, e_off + 41472)
    qT = at("qT", [P, KT, T], F32, e_off)
    pT = at("pT", [P, 2, HEADS, TP], F32, e_off + 8448)
    qs = at("qs", [TS, D], F32, e_off + 16640)
    kv = at("kv", [P, 3, 2, D], F32, e_off + 20736)
    sc = at("sc", [P, 2, TS * HEADS], F32, e_off + 45312)
    att = at("att", [P, 64], F32, e_off + 45568)
    psm = at("psm", [TS * HEADS, MEM], F32, e_off + 45824)
    pr = at("pr", [P, 2, HEADS, MEM], F32, sq_off)
    ah = at("ah", [P, FT, T], F32R, e_off)
    al = at("al", [P, FT, T], F32R, e_off + 23232)
    sg = at("sg", [P, 4, T], F32, sq_off)
    af = at("af", [P, 4, T], F32, sq_off + 4224)
    ce = at("ce", [P, KT, STATE + TP], F32, e_off)
    se = at("se", [P, KT, TS, TAPS], F32, e_off + 9152)
    cv = at("cv", [P, KT, T], F32, e_off + 17088)
    st_in = at("st_in", [4 * STATE, 2, D], F32, e_off + 25536)
    kst1 = at("kst1", [P, 2, D], F32, e_off + 33728)
    tap = at("tap", [P, 2, 2, TP], F32, e_off + 41920)
    c_out = at("c_out", [STATE, D], F32, e_off + 41920)
    cs_out = at("cs_out", [TS, D], F32, e_off + 29632)
    hth = at("hth", [P, 3, D], F32R, e_off)
    htl = at("htl", [P, 3, D], F32R, e_off + 12288)
    ytok = at("ytok", [P, 3, D], F32, e_off + 24576)
    hb = at("hb", [P, 2, EC], F32, e_off + 36864)
    sf = at("sf", [P, 3, CAP], F32, e_off + 40960)
    sr = at("sr", [P, 3, CAP], F32R, e_off + 42496)
    st = at("st", [CAP, T], F32R, e_off + 44032)
    gr = at("gr", [CAP, 8], F32, e_off + 45088)
    iota = at("iota", [P, CAP], F32, e_off + 45120)
    tri = at("tri", [P, P], F32, e_off + 45632)
    xeh = at("xeh", [P, KT, CAP], F32R, c_off)
    xel = at("xel", [P, KT, CAP], F32R, c_off + 4096)
    hTh = at("hTh", [P, EC], F32R, c_off + 8192)
    hTl = at("hTl", [P, EC], F32R, c_off + 10240)
    oeh = at("oeh", [CAP, D], F32R, c_off + 12288)
    oel = at("oel", [CAP, D], F32R, c_off + 16384)
    grow = at("grow", [P, D], F32, c_off + 20480)
    rt = at("rt", [P, 16, 3, EXPERTS + 1], F32, b_off + 8448)
    yo = at("yo", [P, 3, D], F32, b_off)

    bank = [nc.alloc_psum_tensor(f"bank{i}", [P, 512], F32) for i in range(8)]
    eps_r, eps_l = small[:, 0:1], small[:, 1:2]
    ws0, bs0 = small[:, 8:16], bsb[:, :, 0]
    order8 = small[:, 24:32]

    landed = [sem(f"raw{i}_landed") for i in range(RAW)]
    hi_done, lo_done, piece_done, tile0_done = sem("hi_done"), sem("lo_done"), sem("piece_done"), sem("tile0_done")
    evac = [sem(f"bank{i}_evac") for i in range(4)]
    aux_ready = sem("aux_ready")
    aux_free = [sem(f"aux{i}_free") for i in range(4)]
    act_own, dve_own, pool_own = sem("act_own"), sem("dve_own"), sem("pool_own")
    x_done, xn_done, xh_done, xoh_done, osh_done, mh_done, m_done, sq_done = (
        sem(n) for n in ("x_done", "xn_done", "xh_done", "xoh_done", "osh_done", "mh_done", "m_done", "sq_done"))
    consts, ld_mem, ld_x, ld_rows, ld_ws, ld_misc, ld_state, ld_wr, ld_grow = (
        sem(n) for n in ("consts", "ld_mem", "ld_x", "ld_rows", "ld_ws", "ld_misc", "ld_state", "ld_wr", "ld_grow"))
    kv_in = [sem(f"kv{i}_in") for i in range(3)]
    mem_sum, mem_root, mem_n, ws_masked, kst_out, vm_out, stored, eps_set = (
        sem(n) for n in ("mem_sum", "mem_root", "mem_n", "ws_masked", "kst_out", "vm_out", "stored", "eps_set"))
    ah_done, a_done, lnsq_done, lnv_done, conv_done, nmax_done, p_done, snmax_done, sp_done, vused, pad_done = (
        sem(n) for n in ("ah_done", "a_done", "lnsq_done", "lnv_done", "conv_done", "nmax_done", "p_done", "snmax_done",
                         "sp_done", "vused", "pad_done"))
    hn_ready, gate_gap, gate_exp, mask_done, hth_done, flag_ready, moe_const = (
        sem(n) for n in ("hn_ready", "gate_gap", "gate_exp", "mask_done", "hth_done", "flag_ready", "moe_const"))
    t_ready, gat_ready, sca_ready, prep_ready = (sem(n) for n in ("t_ready", "gat_ready", "sca_ready", "prep_ready"))
    silu_done, hTh_done, xeh_done, oeh_done = (sem(n) for n in ("silu_done", "hTh_done", "xeh_done", "oeh_done"))
    h_done, hTl_done, xel_done, oel_done, y_added, s_built, prep_done, pos_moved = (
        sem(n) for n in ("h_done", "hTl_done", "xel_done", "oel_done", "y_added", "s_built", "prep_done", "pos_moved"))
    gate_done, af_done, glu_done, tap_done, tap_added = (sem(n) for n in ("gate_done", "af_done", "glu_done", "tap_done", "tap_added"))
    fin_sum, fin_root, fin_done = sem("fin_sum"), sem("fin_root"), sem("fin_done")

    def by_row_tiles(w):
        return w.rearrange("(t p) n -> p t n", p=P)

    W = {"a_in": by_row_tiles(a["a_w_in"][0]), "a_out": by_row_tiles(a["a_w_out"][0]),
         "gate": by_row_tiles(a["ffn_w_gate"][0]), "up": by_row_tiles(a["ffn_w_up"][0]),
         "down": by_row_tiles(a["ffn_w_down"][0]), "pw1": by_row_tiles(a["b_w_pw1"][0]),
         "pw2": by_row_tiles(a["b_w_pw2"][0])}
    for i in range(2):
        for n in "qkvo":
            W[f"x{n}{i}"] = by_row_tiles(a[f"w_x{n}"][i])
    moe = {"g": a["moe_w_gate"].rearrange("o e (t p) n -> p (o e t) n", p=P),
           "u": a["moe_w_up"].rearrange("o e (t p) n -> p (o e t) n", p=P),
           "d": a["moe_w_down"].rearrange("o e (t p) n -> p (o e t) n", p=P)}

    def moe_source(e, p):
        kind, c, half = EP[p]
        if kind == "d":
            return moe["d"][:, bass.ds(e * (EDIM // P) + 4 * c, 4), half * EC:(half + 1) * EC]
        return moe[kind][:, bass.ds(e * KT + 4 * half, 4), c * EC:(c + 1) * EC]

    def piece_no(ps, e, p):
        return ND + ps * (EXPERTS * NE) + e * NE + p

    def sums(ps, e, j):
        return 48 * ps + 6 * e + j + 1

    def tile_ready(n, o):
        return (tile0_done, GROUP[n] + 1) if o == 0 else (piece_done, n + 1)

    def tile_out(n, o):
        return evac[2 * (GROUP[n] % 2) + o], GROUP[n] // 2 + 1

    def stage_out(stage, count):
        return tile_out(FIRST[stage] + count - 1, 1)

    def residual_out(stage, count, k):
        return tile_out(FIRST[stage] + (k // 2 + 1) * (count // 4) - 1, k % 2)

    def job_out(name, j=0):
        n = AUX[name] + j
        return aux_free[n % 4], n // 4 + 1

    def job_bank(name, j=0):
        return bank[4 + (AUX[name] + j) % 4]

    def piece_bank(n, o):
        return bank[2 * (GROUP[n] % 2) + o]

    block = ctx.enter_context(nc.Block())

    @block.sync
    def _(sp):
        sp.dma_start(mem_in[:, :, :], a["mem_prompt"][0].rearrange("(m p) d -> p m d", p=P)).then_inc(ld_mem, 16)
        for v0, n, name in ((V_MIX, 2, "norm_mix"), (V_XATT, 2, "norm_xattn"), (V_FFN, 2, "norm_ffn"), (V_MEM, 2, "norm_mem"),
                            (V_ALNG, 1, "a_ln_g"), (V_ALNB, 1, "a_ln_b"), (V_BDW, 1, "b_b_dw"), (V_BLNG, 1, "b_ln_g"),
                            (V_BLNB, 1, "b_ln_b")):
            sp.dma_start(rows[v0:v0 + n, :], a[name]).then_inc(ld_rows, 16)
        sp.dma_start(rows[V_DW:NV, :], a["b_w_dw"][0]).then_inc(ld_rows, 16)
        sp.dma_start(x_in[:, 0:2, :], a["x_prompt"][0].rearrange("(m p) d -> p m d", p=P)).then_inc(ld_x, 16)
        sp.dma_start(x_in[0:TS, 2, :], a["x_sample"].rearrange("b s d -> (b s) d")).then_inc(ld_x, 16)
        sp.dma_start(ws_in[:, :, :], a["a_w_s"][0].rearrange("g t s -> t g s")).then_inc(ld_ws, 16)
        for n, (w, k0, nk, c0, _, _) in enumerate(PIECES):
            if n >= RAW:
                sp.wait_ge(lo_done, n - RAW + 1)
            dst = raw[:, n % RAW, 0:nk * PC].rearrange("p (t n) -> p t n", n=PC)
            sp.dma_start(dst, W[w][:, k0:k0 + nk, c0:c0 + PC]).then_inc(landed[n % RAW], 16)

        def load(ps, e, p):
            sp.wait_ge(lo_done, piece_no(ps, e, p) - RAW + 1)
            dst = raw[:, p % RAW, :].rearrange("p (t n) -> p t n", n=EC)
            sp.dma_start(dst, moe_source(e, p)).then_inc(landed[p % RAW], 16)

        def run_pass(ps):
            with sp.Fori(0, EXPERTS) as e:
                for p in range(NE):
                    load(ps, e, p)

        run_pass(0)
        sp.wait_ge(flag_ready, 1)
        most = sp.value_load(flag[0:1, 0:1])
        with sp.If(most > CAP):
            with sp.Fori(1, 3) as ps:
                run_pass(ps)
        sp.wait_ge(stored, 16 * 6)

    @block.gpsimd
    def _(pool):
        own = Own(pool, pool_own)
        own(pool.memset(ident[:, :], 0.0))
        pool.memset(ones[:, :], 1.0).then_inc(consts, 1)
        own.settle()
        pool.affine_select(out=ident[:, :], in_=ident[:, :], compare_op=ALU.not_equal, fill=1.0, base=0,
                           pattern=[[-1, P]], channel_multiplier=1).then_inc(consts, 1)
        pool.dma_start(wr[:, :, :], a["moe_w_router"][0].rearrange("(t p) n -> p t n", p=P)).then_inc(ld_wr, 16)
        pool.wait_ge(*job_out("vec"))
        pool.dma_start(bsb[:, :, :], a["a_b_s"].to_broadcast([P, KT, P])).then_inc(ld_misc, 16)
        pool.wait_ge(*job_out("ws_t", 0))
        pool.wait_ge(*job_out("ws_t", 1))
        pool.affine_select(out=wsT[:, :, :], in_=wsT[:, :, :], compare_op=ALU.is_ge, fill=0.0, base=0,
                           pattern=[[0, KT], [1, P]], channel_multiplier=-1).then_inc(ws_masked, 1)

        def store_memory(i, stage):
            pool.wait_ge(*stage_out(f"v{i}", 4))
            pool.dma_start(out["v"][i, 0].rearrange("(m p) h d -> p m (h d)", p=P), vm[:, :, :]).then_inc(vm_out, 16)
            pool.wait_ge(*job_out(f"k_tok{i}", 3))
            pool.dma_start(out["k"][i, 0].rearrange("(m p) h d -> p m (h d)", p=P), stage[:, :, :]).then_inc(kst_out, 16)

        def load_caches(i):
            for j in range(2 * TS):
                n = i * 2 * TS + j
                if n >= 3:
                    li, lj = (n - 3) // (2 * TS), (n - 3) % (2 * TS)
                    if lj < TS:
                        pool.wait_ge(*job_out(f"q_bc{li}", 2 * lj + 1))
                    elif lj < 2 * TS - 1:
                        pool.wait_ge(vused, (TS - 1) * li + lj - TS + 1)
                    else:
                        pool.wait_ge(aux_ready, AUX[f"s_o{li}"] + 2)
                src = a["cache_mem_v" if j >= TS else "cache_mem_k"][i, j % TS].rearrange("(m p) h d -> p m (h d)", p=P)
                pool.dma_start(kv[:, n % 3, :, :], src).then_inc(kv_in[n % 3], 16)

        store_memory(0, kst)
        pool.wait_ge(*job_out("v_smp", 1))
        pool.dma_start(out["chunk"].rearrange("l b s d -> (l b s) d"), vs_out[:, :]).then_inc(stored, 16)
        pool.wait_ge(kst_out, 16)
        pool.wait_ge(stored, 16)
        pool.wait_ge(x_done, XW["mixed"] + 8)
        load_caches(0)
        pool.wait_ge(piece_done, FIRST["pw1"])
        pool.memset(ce[:, :, 0:STATE], 0.0).then_inc(pad_done, 1)
        for half in range(2):
            src = a["state_conv"][0, 4 * half:4 * half + 4].rearrange("s j d -> (s j) d")
            pool.dma_start(st_in[:, half, :], src).then_inc(ld_state, 16)
        pool.dma_start(out["conv_s"][0, :, 0:STATE - 1, :], a["state_conv"][0, :, 1:STATE, :]).then_inc(stored, 16)
        for u in range(CONV_POOL // 2 * TAPS):
            pair, j = u // TAPS, u % TAPS
            if j == 0:
                continue
            i = u - pair - 1
            pool.wait_ge(tap_done, u + 1)
            if i > 0:
                pool.wait_ge(tap_added, i)
            acc = cv[:, 2 * pair:2 * pair + 2, 0:TP]
            pool.tensor_tensor(acc, acc, tap[:, i % 2, :, :], ALU.add).then_inc(tap_added, 1)
        store_memory(1, kst1)
        pool.wait_ge(*job_out("c_tok", 3))
        pool.wait_ge(*job_out("c_tok", 1))
        pool.dma_start(out["conv_p"][0, 0], c_out[:, :]).then_inc(stored, 16)
        pool.dma_start(out["conv_s"][0, :, STATE - 1, :], cs_out[:, :]).then_inc(stored, 16)
        pool.wait_ge(kst_out, 32)
        pool.wait_ge(vm_out, 32)
        pool.wait_ge(stored, 16 * 4)
        pool.wait_ge(x_done, XW["conv"] + 8)
        load_caches(1)
        pool.wait_ge(piece_done, ND)
        pool.dma_start(grow[:, :], a["norm_final"].rearrange("(o d) -> o d", o=1).to_broadcast([P, D])).then_inc(ld_grow, 16)
        pool.iota(iota[:, :], pattern=[[1, CAP]], base=0, channel_multiplier=0,
                  allow_small_or_imprecise_dtypes=True).then_inc(moe_const, 1)
        own(pool.memset(tri[:, :], 1.0))
        own.settle()
        pool.affine_select(out=tri[:, :], in_=tri[:, :], compare_op=ALU.is_gt, fill=0.0, base=0,
                           pattern=[[1, P]], channel_multiplier=-1).then_inc(moe_const, 1)
        pool.wait_ge(fin_done, 3)
        pool.dma_start(out["y"][0].rearrange("(m p) d -> p m d", p=P), yo[:, 0:2, :]).then_inc(stored, 16)
        pool.dma_start(out["ys"].rearrange("b s d -> (b s) d"), yo[0:TS, 2, :]).then_inc(stored, 16)
        pool.wait_ge(stored, 16 * 6)

    @block.tensor
    def _(pe):
        def aux(name, j=0):
            n = AUX[name] + j
            if n >= 4:
                pe.wait_ge(aux_free[n % 4], n // 4)
            return bank[4 + n % 4]

        def product(stage, count, hi, lo, ready=None, tokens_stationary=False, start=0):
            for n in range(FIRST[stage] + start, FIRST[stage] + start + count):
                _, k0, nk, _, opens, closes = PIECES[n]
                g = GROUP[n]
                pe.wait_ge(lo_done, n + 1)
                for o in range(2):
                    b = 2 * (g % 2) + o
                    if opens and g >= 2:
                        pe.wait_ge(evac[b], g // 2)
                    for k in range(nk):
                        if ready is not None and n == FIRST[stage] and o == 0:
                            pe.wait_ge(ready[0], ready[1] + k + 1)
                        w_hi = whi[:, n % SPLIT, k * PC:(k + 1) * PC]
                        w_lo = wlo[:, n % SPLIT, k * PC:(k + 1) * PC]
                        first, last = opens and k == 0, closes and k == nk - 1
                        if tokens_stationary:
                            x_hi, x_lo = hi[:, k0 + k, o * P:(o + 1) * P], lo[:, k0 + k, o * P:(o + 1) * P]
                            y = bank[b][:, 0:PC]
                            pe.matmul(y, x_hi, w_hi, start=first, stop=False)
                            pe.matmul(y, x_hi, w_lo, start=False, stop=False)
                            mm = pe.matmul(y, x_lo, w_hi, start=False, stop=last)
                        else:
                            x_hi, x_lo = hi[:, k0 + k, :], lo[:, k0 + k, :]
                            y = bank[b][:, 0:hi.shape[2]]
                            cols = slice(o * P, (o + 1) * P)
                            pe.matmul(y, w_hi[:, cols], x_hi, start=first, stop=False)
                            pe.matmul(y, w_hi[:, cols], x_lo, start=False, stop=False)
                            mm = pe.matmul(y, w_lo[:, cols], x_hi, start=False, stop=last)
                    if o == 0 and closes:
                        mm.then_inc(tile0_done, 1)
                mm.then_inc(piece_done, 1)

        def channel_sum(job, src, ready):
            y = aux(job)
            pe.wait_ge(*ready)
            for k in range(KT):
                mm = pe.matmul(y[:, 0:T], ones[:, :], src[:, k, :], start=(k == 0), stop=(k == KT - 1))
            mm.then_inc(aux_ready, 1)

        def turn(dst, src, rows_):
            return pe.transpose(dst, src, ident[0:rows_, 0:rows_])

        pe.wait_ge(consts, 2)
        pe.wait_ge(ld_rows, 160)
        y = aux("vec")
        for k in range(KT):
            mm = turn(y[:, k * NV:(k + 1) * NV], rows[:, k * P:(k + 1) * P], NV)
        mm.then_inc(aux_ready, 1)
        pe.wait_ge(mem_n, 2)
        for j in range(4):
            y = aux("mem_t", j)
            for kk in range(2):
                for m in range(2):
                    k = 2 * j + kk
                    mm = turn(y[:, kk * MEM + m * P:kk * MEM + (m + 1) * P], mem_in[:, m, k * P:(k + 1) * P], P)
            mm.then_inc(aux_ready, 1)
        pe.wait_ge(ld_x, 32)
        for k in range(KT):
            y = aux("x_t", k)
            for m in range(2):
                turn(y[:, m * P:(m + 1) * P], x_in[:, m, k * P:(k + 1) * P], P)
            turn(y[:, TP:T], x_in[0:TS, 2, k * P:(k + 1) * P], TS).then_inc(aux_ready, 1)
        pe.wait_ge(ld_ws, 16)
        for j in range(2):
            y = aux("ws_t", j)
            for gg in range(4):
                mm = turn(y[:, gg * P:(gg + 1) * P], ws_in[:, 4 * j + gg, :], P)
            mm.then_inc(aux_ready, 1)
        pe.matmul(aux("ws_0")[:, 0:KT], ones[0:1, :], ws_in[0:1, :, 0], start=True, stop=True).then_inc(aux_ready, 1)

        def memory(i, hi, lo, ready):
            product(f"k{i}", 4, hi, lo, ready)
            if i == 0:
                channel_sum("rms_mix0", sq, (sq_done, SQ["mix0"]))
            product(f"v{i}", 4, hi, lo, None, True)
            pe.wait_ge(*stage_out(f"k{i}", 4))
            for j in range(4):
                y = aux(f"k_tok{i}", j)
                m, half = j // 2, j % 2
                for kk in range(4):
                    mm = turn(y[:, kk * P:(kk + 1) * P], kT[:, 4 * half + kk, m * P:(m + 1) * P], P)
                mm.then_inc(aux_ready, 1)

        memory(0, mh[:, :, :], ml[:, :, :], (m_done, 0))
        x_hi, x_lo = xh[:, :, :], xl[:, :, :]
        product("in_v", 4, x_hi, x_lo, (x_done, XW["mix0"]))
        product("in_u", 1, x_hi, x_lo)
        channel_sum("ln_a0", vT, stage_out("in_v", 4))
        product("in_u", 2, x_hi, x_lo, start=1)
        channel_sum("ln_b0", sq, (lnsq_done, 1))
        product("in_u", 1, x_hi, x_lo, start=3)
        pe.wait_ge(lnv_done, 1)
        for j in range(2):
            y = aux("v_smp", j)
            for kk in range(4):
                mm = turn(y[0:TS, kk * P:(kk + 1) * P], vT[:, 4 * j + kk, TP:T], P)
            mm.then_inc(aux_ready, 1)
        for j in range(4):
            y = aux("v_tok", j)
            c, half = j // 2, j % 2
            for kk in range(4):
                mm = turn(y[:, kk * P:(kk + 1) * P], vT[:, 4 * half + kk, c * CHUNK:(c + 1) * CHUNK], P)
            mm.then_inc(aux_ready, 1)
        pe.wait_ge(ws_masked, 1)
        pe.wait_ge(*job_out("v_tok", 3))
        for j in range(4):
            y = aux("mixed", j)
            for gg in range(2):
                g = 2 * j + gg
                for c in range(2):
                    mm = pe.matmul(y[:, (2 * gg + c) * P:(2 * gg + c + 1) * P], vtok[:, c, g * P:(g + 1) * P], wsT[:, g, :],
                                   start=(gg == 0 and c == 0), stop=True, skip_group_check=True)
            mm.then_inc(aux_ready, 1)
        product("a_out", 4, x_hi, x_lo, (x_done, XW["mixed"]))

        def normed_product(stage, count, tag):
            product(stage, 1, x_hi, x_lo, (x_done, XW[tag]))
            channel_sum("rms_" + tag, sq, (sq_done, SQ[tag]))
            product(stage, count - 1, x_hi, x_lo, start=1)

        def attention(i):
            normed_product(f"q{i}", 4, f"xatt{i}")
            pe.wait_ge(*stage_out(f"q{i}", 4))
            for j in range(2):
                y = aux(f"q_tok{i}", j)
                for kk in range(4):
                    mm = turn(y[0:TS, kk * P:(kk + 1) * P], qT[:, 4 * j + kk, TP:T], P)
                mm.then_inc(aux_ready, 1)
            for j in range(4):
                y = aux(f"scores{i}", j)
                tt, hh = j // 2, j % 2
                for h2 in range(2):
                    for dh in range(2):
                        f = 2 * (2 * hh + h2) + dh
                        mm = pe.matmul(y[:, h2 * MEM:(h2 + 1) * MEM], qT[:, f, tt * P:(tt + 1) * P], kT[:, f, :],
                                       start=(h2 == 0 and dh == 0), stop=(dh == 1), skip_group_check=True)
                mm.then_inc(aux_ready, 1)
            pe.wait_ge(*job_out(f"q_tok{i}", 1))
            for s in range(TS):
                for c in range(2):
                    y = aux(f"q_bc{i}", 2 * s + c)
                    pe.matmul(y[:, :], ident[0:TS, s:s + 1].to_broadcast([TS, P]), qs[:, c * 512:(c + 1) * 512],
                              start=True, stop=True).then_inc(aux_ready, 1)
            pe.wait_ge(*job_out(f"q_bc{i}", 15))
            y = aux(f"s_t{i}")
            for mt in range(2):
                mm = turn(y[0:TS * HEADS, mt * P:(mt + 1) * P], sc[:, mt, :], P)
            mm.then_inc(aux_ready, 1)
            for j in range(4):
                tt, mt = j // 2, j % 2
                y = aux(f"p_t{i}", j)
                pe.wait_ge(p_done, 4 * i + 2 * tt + 2)
                for h in range(HEADS):
                    mm = turn(y[:, h * P:(h + 1) * P], pr[:, tt, h, mt * P:(mt + 1) * P], P)
                mm.then_inc(aux_ready, 1)
            y = aux(f"ps_t{i}")
            pe.wait_ge(sp_done, i + 1)
            for mt in range(2):
                mm = turn(y[:, mt * 32:(mt + 1) * 32], psm[:, mt * P:(mt + 1) * P], TS * HEADS)
            mm.then_inc(aux_ready, 1)
            pe.wait_ge(*job_out(f"p_t{i}", 3))
            for j in range(4):
                y = aux(f"o_t{i}", j)
                for ff in range(2):
                    f = 2 * j + ff
                    for mt in range(2):
                        mm = pe.matmul(y[:, ff * TP:(ff + 1) * TP], vm[:, mt, f * P:(f + 1) * P], pT[:, mt, f // 2, :],
                                       start=(ff == 0 and mt == 0), stop=(mt == 1), skip_group_check=True)
                mm.then_inc(aux_ready, 1)
            y = [aux(f"s_o{i}", 0), aux(f"s_o{i}", 1)]
            pe.wait_ge(*job_out(f"ps_t{i}"))
            for s in range(TS):
                n = i * 2 * TS + TS + s
                pe.wait_ge(kv_in[n % 3], 16 * (n // 3 + 1))
                for h in range(HEADS):
                    for mt in range(2):
                        mm = pe.matmul(y[h // 2][0:TS, (h % 2) * HD:(h % 2 + 1) * HD], pz[:, mt, h, s, :],
                                       kv[:, n % 3, mt, h * HD:(h + 1) * HD],
                                       start=(s == 0 and h % 2 == 0 and mt == 0), stop=(s == TS - 1 and mt == 1),
                                       skip_group_check=True)
                    if s == TS - 1 and h % 2 == 1:
                        mm.then_inc(aux_ready, 1)
                if s < TS - 1:
                    mm.then_inc(vused, 1)
            y = aux(f"os_t{i}")
            pe.wait_ge(*job_out(f"s_o{i}", 1))
            for k in range(KT):
                mm = turn(y[:, k * TS:(k + 1) * TS], qs[:, k * P:(k + 1) * P], TS)
            mm.then_inc(aux_ready, 1)
            product(f"o{i}", 4, x_hi, x_lo, (x_done, XW[f"att{i}"]))

        attention(0)
        normed_product("gate_up", 22, "ffn0")
        pe.wait_ge(a_done, FT)
        product("down", 12, ah[:, :, :], al[:, :, :])
        normed_product("pw1", 8, "mix1")
        pe.wait_ge(ld_state, 32)
        for j in range(4):
            y = aux("state_t", j)
            half, kq = j // 2, j % 2
            for kk in range(4):
                mm = turn(y[:, kk * 120:(kk + 1) * 120], st_in[:, half, (4 * kq + kk) * P:(4 * kq + kk + 1) * P], 4 * STATE)
            mm.then_inc(aux_ready, 1)
        memory(1, xh[:, :, 0:MEM], xl[:, :, 0:MEM], (x_done, XW["mem1"]))
        pe.wait_ge(glu_done, KT)
        for j in range(4):
            y = aux("c_tok", j)
            for kk in range(4):
                k = 4 * (j % 2) + kk
                if j < 2:
                    mm = turn(y[0:STATE, kk * P:(kk + 1) * P], ce[:, k, TP:TP + STATE], P)
                else:
                    mm = turn(y[0:TS, kk * P:(kk + 1) * P], se[:, k, :, STATE], P)
            mm.then_inc(aux_ready, 1)
        channel_sum("ln_a1", cv, (conv_done, 1))
        channel_sum("ln_b1", sq, (lnsq_done, 2))
        product("pw2", 4, x_hi, x_lo, (x_done, XW["conv"]))
        attention(1)
        channel_sum("rms_ffn1", sq, (sq_done, SQ["ffn1"]))

        TT = ((0, P), (1, P), (2, TS))
        E1 = EXPERTS + 1
        y = aux("route")
        pe.wait_ge(hn_ready, 8)
        pe.wait_ge(ld_wr, 16)
        for tt, n_rows in TT:
            for k in range(KT):
                mm = pe.matmul(y[0:n_rows, tt * 16:tt * 16 + EXPERTS], sq[:, k, tt * P:tt * P + n_rows], wr[:, k, :],
                               start=(tt == 0 and k == 0), stop=(k == KT - 1), skip_group_check=True)
        mm.then_inc(aux_ready, 1)
        pe.wait_ge(mask_done, 1)
        pe.wait_ge(moe_const, 2)
        chosen = rt[:, 0, :, :]
        y = aux("pos", 0)
        for tt, n_rows in TT:
            for t2 in range(tt):
                pe.matmul(y[0:n_rows, tt * 16:tt * 16 + E1], ones[:, 0:n_rows], chosen[:, t2, :],
                          start=(tt == 0), stop=False, skip_group_check=True)
            mm = pe.matmul(y[0:n_rows, tt * 16:tt * 16 + E1], tri[0:n_rows, 0:n_rows], chosen[0:n_rows, tt, :],
                           start=(tt == 0), stop=True, skip_group_check=True)
        mm.then_inc(aux_ready, 1)
        y = aux("pos", 1)
        for tt, n_rows in TT:
            mm = pe.matmul(y[:, 0:E1], ones[0:n_rows, :], chosen[0:n_rows, tt, :], start=(tt == 0), stop=(tt == 2))
        mm.then_inc(aux_ready, 1)
        for name, src in (("hn_tok", sq), ("y_tok", hT)):
            for j in range(6):
                y = aux(name, j)
                tt, half = j // 2, j % 2
                n_rows = TT[tt][1]
                for kk in range(4):
                    mm = turn(y[0:n_rows, kk * P:(kk + 1) * P], src[:, 4 * half + kk, tt * P:tt * P + n_rows], P)
                mm.then_inc(aux_ready, 1)

        G, U, ACC, TB, XB = (bank[0], bank[2]), (bank[1], bank[3]), (bank[4], bank[5]), bank[6], bank[7]

        def gather(ready):
            pe.wait_ge(s_built, ready)
            for dst, k0 in ((XB, 0), (G[1], 4)):
                for kk in range(4):
                    for tt, n_rows in TT:
                        for part in (hth, htl):
                            mm = pe.matmul(dst[:, kk * CAP:(kk + 1) * CAP], part[0:n_rows, tt, (k0 + kk) * P:(k0 + kk + 1) * P],
                                           sr[0:n_rows, tt, :], start=(tt == 0 and kk == 0 and part is hth),
                                           stop=(tt == 2 and part is htl), skip_group_check=True)
                mm.then_inc(gat_ready, 1)

        def prepare(column):
            for tt, n_rows in TT:
                pe.matmul(XB[:, tt * P:tt * P + n_rows], sf[0:n_rows, tt, :], ident[0:n_rows, 0:n_rows], is_transpose=True,
                          start=(tt == 0), stop=True, skip_group_check=True)
            for tt, n_rows in TT:
                mm = pe.matmul(XB[:, 272:273], sf[0:n_rows, tt, :], rt[0:n_rows, 1, tt, bass.ds(column, 1)],
                               start=False, stop=(tt == 2), skip_group_check=True)
            mm.then_inc(prep_ready, 1)

        def transposes(ps, e, c):
            pe.wait_ge(h_done, 56 * ps + 7 * e + c + 1)
            if c == 0:
                pe.wait_ge(y_added, sums(ps, e, 1))
            else:
                pe.wait_ge(hTl_done, 56 * ps + 7 * e + c)
            for k in range(4):
                mm = turn(TB[:, k * P:(k + 1) * P], hb[:, c % 2, k * P:(k + 1) * P], P)
            mm.then_inc(t_ready, 1)

        def piece(ps, e, p, opens_pass=False, last=False):
            kind, c, half = EP[p]
            if kind == "u" and half == 0 and c >= 1:
                transposes(ps, e, c - 1)
            if kind == "u" and half == 1 and c == 0:
                pe.wait_ge(y_added, sums(ps, e, 0))
                prepare(e)
            if p == NE - 2:
                transposes(ps, e, CH - 1)
                if not last:
                    pe.wait_ge(prep_done, 8 * ps + e + 1)
                    gather(8 * ps + e + 2)
            pe.wait_ge(lo_done, piece_no(ps, e, p) + 1)
            if half == 0:
                if kind == "g" and c == 0:
                    pe.wait_ge(xel_done, 16 * ps + 2 * e + 2)
                    if not opens_pass:
                        pe.wait_ge(silu_done, 56 * ps + 7 * e)
                elif kind == "g" and c == 1:
                    pe.wait_ge(y_added, sums(ps, e, 4))
                elif kind == "g":
                    pe.wait_ge(silu_done, 56 * ps + 7 * e + c - 1)
                elif kind == "u" and c == 1:
                    pe.wait_ge(y_added, sums(ps, e, 5))
                elif kind == "u" and c >= 2:
                    pe.wait_ge(h_done, 56 * ps + 7 * e + c - 1)
                elif kind == "d":
                    pe.wait_ge(hTl_done, 56 * ps + 7 * e + c + 1)
                    if c == 0:
                        pe.wait_ge(y_added, sums(ps, e, 3))
            y = {"g": G[c % 2], "u": U[c % 2], "d": ACC[half]}[kind]
            for k in range(4):
                w_hi, w_lo = whi[:, p % SPLIT, k * EC:(k + 1) * EC], wlo[:, p % SPLIT, k * EC:(k + 1) * EC]
                if kind == "d":
                    x_hi, x_lo = hTh[:, k * P:(k + 1) * P], hTl[:, k * P:(k + 1) * P]
                    first, last = c == 0 and k == 0, c == CH - 1 and k == 3
                else:
                    x_hi, x_lo = xeh[:, 4 * half + k, :], xel[:, 4 * half + k, :]
                    first, last = half == 0 and k == 0, half == 1 and k == 3
                pe.matmul(y[:, :], x_hi, w_hi, start=first, stop=False)
                pe.matmul(y[:, :], x_hi, w_lo, start=False, stop=False)
                mm = pe.matmul(y[:, :], x_lo, w_hi, start=False, stop=last)
            mm.then_inc(piece_done, 1)

        def expert(ps, e, last=False):
            for p in range(2, NE):
                piece(ps, e, p, last=last)
            if not last:
                piece(ps, e + 1, 0)
                piece(ps, e + 1, 1)
            pe.wait_ge(oel_done, 16 * ps + 2 * e + 2)
            for j, dst in enumerate((XB, TB, ACC[0], ACC[1], G[1], U[1])):
                tt, half = SCATTER[j]
                n_rows = TT[tt][1]
                cols = slice(half * 512, (half + 1) * 512)
                pe.matmul(dst[0:n_rows, :], st[:, tt * P:tt * P + n_rows], oeh[:, cols], start=True, stop=False)
                pe.matmul(dst[0:n_rows, :], st[:, tt * P:tt * P + n_rows], oel[:, cols], start=False,
                          stop=True).then_inc(sca_ready, 1)

        def run_pass(ps):
            if not (isinstance(ps, int) and ps == 0):
                pe.wait_ge(y_added, sums(ps, 0, 5))
            gather(8 * ps + 1)
            piece(ps, 0, 0, opens_pass=True)
            piece(ps, 0, 1)
            with pe.Fori(0, EXPERTS - 1) as e:
                expert(ps, e)
            expert(ps, EXPERTS - 1, last=True)

        pe.wait_ge(*job_out("y_tok", 5))
        run_pass(0)
        pe.wait_ge(flag_ready, 1)
        most = pe.value_load(flag[0:1, 0:1])
        with pe.If(most > CAP):
            with pe.Fori(1, 3) as ps:
                run_pass(ps)

    @block.scalar
    def _(act):
        own = Own(act, act_own)

        def width(n):
            return PIECES[n][2] * PC if n < ND else PIECE

        def split(n):
            act.wait_ge(landed[n % RAW], 16 * (n // RAW + 1))
            if n >= SPLIT:
                act.wait_ge(piece_done, n - SPLIT + 1)
            w = width(n)
            act.activation(whi[:, n % SPLIT, 0:w], raw[:, n % RAW, 0:w], ACT.Copy).then_inc(hi_done, 1)

        def pieces(stage, count, post=None, start=0):
            for n in range(FIRST[stage] + start, FIRST[stage] + start + count):
                if post is not None:
                    post(n)
                split(n + SPLIT)

        def job_copy(name, j, dst, rows_=P, cols=512):
            act.wait_ge(aux_ready, AUX[name] + j + 1)
            act.activation(dst, job_bank(name, j)[0:rows_, 0:cols], ACT.Copy).then_inc(job_out(name, j)[0], 1)

        def root(job, slot, eps):
            act.wait_ge(aux_ready, AUX[job] + 1)
            act.activation(stat[:, slot, :], job_bank(job)[:, 0:T], ACT.Sqrt, bias=eps, scale=1.0 / D).then_inc(job_out(job)[0], 1)

        def feed(tag, row=None):
            for k in range(KT):
                act.wait_ge(xn_done, XN[tag] + k + 1)
                scale = 1.0 if row is None else vecs[:, k, row:row + 1]
                act.activation(xh[:, k, :], sq[:, k, :], ACT.Copy, scale=scale).then_inc(xh_done, 1)

        def residual_hi(row, before, count, after):
            act.wait_ge(piece_done, FIRST[after])
            for k in range(KT):
                act.wait_ge(*residual_out(before, count, k))
                act.activation(xh[:, k, :], hT[:, k, :], ACT.Copy, scale=vecs[:, k, row:row + 1]).then_inc(xh_done, 1)

        def normed_pieces(stage, count, tag, post=None):
            pieces(stage, 1)
            root("rms_" + tag, 0, eps_r)
            if post is not None:
                post(FIRST[stage])
            pieces(stage, count - 1, post, start=1)

        def memory_hi(i, dst):
            act.wait_ge(*job_out("vec"))
            act.wait_ge(*job_out("mem_t", 3))
            for k in range(KT):
                act.activation(dst[:, k, 0:MEM], memT[:, k, :], ACT.Copy, scale=vecs[:, k, V_MEM + i:V_MEM + i + 1])\
                    .then_inc(mh_done, 1)

        act.wait_ge(mem_sum, 2)
        act.wait_ge(eps_set, 1)
        act.activation(small[:, 4:6], small[:, 2:4], ACT.Sqrt, bias=eps_r, scale=1.0 / D).then_inc(mem_root, 1)
        memory_hi(0, mh)
        for n in range(SPLIT):
            split(n)
        for j in range(2):
            job_copy("ws_t", j, wsT[:, 4 * j:4 * j + 4, :].rearrange("p g s -> p (g s)"))
        pieces("k0", 4)
        root("rms_mix0", 0, eps_r)
        feed("mix0", V_MIX)

        def values(i):
            def post(n):
                for o in range(2):
                    act.wait_ge(*tile_ready(n, o))
                    c = PIECES[n][3]
                    act.activation(vm[:, o, c:c + PC], piece_bank(n, o)[:, 0:PC], ACT.Copy).then_inc(tile_out(n, o)[0], 1)
            return post

        def keys_out(i, dst):
            for j in range(4):
                m, half = j // 2, j % 2
                job_copy(f"k_tok{i}", j, dst[:, m, half * 512:(half + 1) * 512])

        pieces("v0", 4, values(0))
        act.wait_ge(piece_done, FIRST["in_v"])
        keys_out(0, kst)

        def gelu(dst, base):
            def post(n):
                for o in range(2):
                    act.wait_ge(*tile_ready(n, o))
                    f = (PIECES[n][3] - base) // P + o
                    act.activation(dst[:, f, :], piece_bank(n, o)[:, 0:T], ACT.Gelu_apprx_tanh).then_inc(tile_out(n, o)[0], 1)
            return post

        pieces("in_v", 4, gelu(vT, D))
        pieces("in_u", 3, gelu(uT, 0))
        root("ln_b0", 1, eps_l)
        pieces("in_u", 1, gelu(uT, 0), start=3)
        for j in range(2):
            job_copy("v_smp", j, vs_out[:, j * 512:(j + 1) * 512], TS)
        for j in range(4):
            c, half = j // 2, j % 2
            job_copy("v_tok", j, vtok[:, c, half * 512:(half + 1) * 512])
        feed("mixed")
        pieces("a_out", 4)

        def attention(i):
            residual_hi(V_XATT + i, "pw2" if i else "a_out", 4, f"q{i}")
            normed_pieces(f"q{i}", 4, f"xatt{i}")
            for j in range(4):
                tt, hh = j // 2, j % 2
                act.wait_ge(nmax_done, 4 * i + j + 1)
                for h2 in range(2):
                    h = 2 * hh + h2
                    ins = act.activation(pr[:, tt, h, :], job_bank(f"scores{i}", j)[:, h2 * MEM:(h2 + 1) * MEM], ACT.Exp,
                                         bias=att[:, 8 + 4 * tt + h:9 + 4 * tt + h], scale=SCALE,
                                         accum_out=att[:, 16 + 4 * tt + h:17 + 4 * tt + h])
                ins.then_inc(job_out(f"scores{i}", j)[0], 1)
            act.wait_ge(snmax_done, i + 1)
            n32 = TS * HEADS
            act.activation(psm[:, :], job_bank(f"s_t{i}")[0:n32, 0:MEM], ACT.Exp, bias=att[0:n32, 33:34], scale=SCALE,
                           accum_out=att[0:n32, 34:35]).then_inc(job_out(f"s_t{i}")[0], 1)
            for j in range(4):
                act.wait_ge(aux_ready, AUX[f"o_t{i}"] + j + 1)
                act.activation(xh[:, 2 * j:2 * j + 2, 0:TP],
                               job_bank(f"o_t{i}", j)[:, :].rearrange("p (f t) -> p f t", f=2), ACT.Copy).then_inc(xoh_done, 1)
            act.wait_ge(*job_out(f"os_t{i}"))
            act.activation(xh[:, :, TP:T], os8[:, :, :], ACT.Copy).then_inc(osh_done, 1)
            pieces(f"o{i}", 4)

        attention(0)
        residual_hi(V_FFN, "o0", 4, "gate_up")

        def gated(func, split_h):
            def post(n):
                c = (n - FIRST["gate_up" if split_h else "pw1"]) // 2
                gate = (n - FIRST["gate_up"]) % 2 == 0
                for o in range(2):
                    slot = 2 * (c % 2) + o
                    if gate:
                        act.wait_ge(*tile_out(n, o))
                        act.activation(sg[:, slot, :], sg[:, slot, :], func).then_inc(gate_done, 1)
                    elif split_h:
                        act.wait_ge(af_done, 2 * c + o + 1)
                        act.activation(ah[:, 2 * c + o, :], af[:, slot, :], ACT.Copy).then_inc(ah_done, 1)
            return post

        normed_pieces("gate_up", 22, "ffn0", gated(ACT.Silu, True))
        pieces("down", 12)
        residual_hi(V_MIX + 1, "down", 12, "pw1")
        glu_gate = gated(ACT.Sigmoid, False)

        def taps(first, last):
            for u in range(first, last):
                pair, j = u // TAPS, u % TAPS
                i = u - pair - 1
                if u == 0:
                    act.wait_ge(pad_done, 1)
                if j == 0:
                    act.wait_ge(glu_done, 2 * pair + 2)
                elif i >= 2:
                    act.wait_ge(tap_added, i - 1)
                for kk in range(2):
                    k = 2 * pair + kk
                    src, w = ce[:, k, j:j + TP], vecs[:, k, V_DW + j:V_DW + j + 1]
                    if j == 0:
                        ins = act.activation(cv[:, k, 0:TP], src, ACT.Identity, bias=vecs[:, k, V_BDW:V_BDW + 1], scale=w)
                    else:
                        ins = act.activation(tap[:, i % 2, kk, :], src, ACT.Copy, scale=w)
                ins.then_inc(tap_done, 1)

        def glu_post(n):
            glu_gate(n)
            o = n - FIRST["pw1"]
            if o >= 3:
                taps(2 * (o - 3), 2 * (o - 2))

        UNITS = CONV_POOL // 2 * TAPS - 10

        def tap_share(n):
            o = n - FIRST["k1"]
            taps(10 + UNITS * o // 8, 10 + UNITS * (o + 1) // 8)

        normed_pieces("pw1", 8, "mix1", glu_post)
        act.wait_ge(piece_done, FIRST["k1"])
        memory_hi(1, xh)
        for j in range(4):
            half, kq = j // 2, j % 2
            act.wait_ge(aux_ready, AUX["state_t"] + j + 1)
            act.activation(se[:, 4 * kq:4 * kq + 4, 4 * half:4 * half + 4, 0:STATE],
                           job_bank("state_t", j)[:, 0:480].rearrange("p (k s j) -> p k s j", k=4, s=4),
                           ACT.Copy).then_inc(job_out("state_t", j)[0], 1)
        pieces("k1", 4, tap_share)
        act.wait_ge(vm_out, 16)
        values_out = values(1)

        def values_post(n):
            values_out(n)
            tap_share(n)

        pieces("v1", 4, values_post)
        keys_out(1, kst1)
        act.wait_ge(tap_added, CONV_POOL // 2 * (TAPS - 1))
        for j in range(4):
            if j < 2:
                job_copy("c_tok", j, c_out[:, j * 512:(j + 1) * 512], STATE)
            else:
                job_copy("c_tok", j, cs_out[:, (j - 2) * 512:(j - 1) * 512], TS)
        root("ln_b1", 1, eps_l)
        act.wait_ge(lnv_done, 2)
        for k in range(KT):
            act.activation(sq[:, k, :], cv[:, k, :], ACT.Silu).then_inc(xn_done, 1)
        feed("conv")
        pieces("pw2", 4)
        attention(1)
        root("rms_ffn1", 0, eps_r)
        act.wait_ge(gate_gap, 1)
        act.activation(rt[:, 13, :, 0:1], rt[:, 12, :, 0:1], ACT.Exp).then_inc(gate_exp, 1)
        for j in range(6):
            tt, half = j // 2, j % 2
            n_rows = P if tt < 2 else TS
            act.wait_ge(aux_ready, AUX["hn_tok"] + j + 1)
            act.activation(hth[0:n_rows, tt, half * 512:(half + 1) * 512], job_bank("hn_tok", j)[0:n_rows, :],
                           ACT.Copy).then_inc(hth_done, 1)

        G, XB, TB, ACC = (bank[0], bank[2]), bank[7], bank[6], (bank[4], bank[5])

        def split_moe(ps, e, p):
            act.wait_ge(landed[p % RAW], 16 * (ND // RAW + ps * (EXPERTS * NE // RAW) + e * (NE // RAW) + p // RAW + 1))
            act.wait_ge(piece_done, piece_no(ps, e, p) - SPLIT + 1)
            act.activation(whi[:, p % SPLIT, :], raw[:, p % RAW, :], ACT.Copy).then_inc(hi_done, 1)

        def tokens_hi(first):
            for j, src in enumerate((XB, G[1])):
                act.wait_ge(gat_ready, first + j)
                act.activation(xeh[:, 4 * j:4 * j + 4, :], src[:, :].rearrange("p (k r) -> p k r", k=4), ACT.Copy)\
                    .then_inc(xeh_done, 1)

        def h_hi(value):
            act.wait_ge(t_ready, value)
            act.activation(hTh[:, :], TB[:, :], ACT.Copy).then_inc(hTh_done, 1)

        def piece(ps, e, p, last=False):
            kind, c, half = EP[p]
            if kind == "g" and half == 1:
                act.wait_ge(piece_done, piece_no(ps, e, p) + 1)
                act.activation(hb[:, c % 2, :], G[c % 2][:, :], ACT.Silu).then_inc(silu_done, 1)
            if kind == "u" and half == 0 and c >= 1:
                h_hi(56 * ps + 7 * e + c)
            if p == NE - 2:
                h_hi(56 * ps + 7 * e + CH)
                if not last:
                    tokens_hi(16 * ps + 2 * e + 3)
            if not last or p + SPLIT < NE:
                split_moe(ps, e, p + SPLIT)

        def expert(ps, e, last=False):
            for p in range(2, NE):
                piece(ps, e, p, last)
            act.wait_ge(prep_done, 8 * ps + e + 1)
            act.wait_ge(piece_done, piece_no(ps, e, NE))
            for half in range(2):
                act.activation(oeh[:, half * 512:(half + 1) * 512], ACC[half][:, :], ACT.Copy, scale=gr[:, 0:1])\
                    .then_inc(oeh_done, 1)
            if not last:
                piece(ps, e + 1, 0)
                piece(ps, e + 1, 1)

        def run_pass(ps):
            if not (isinstance(ps, int) and ps == 0):
                for p in range(SPLIT):
                    split_moe(ps, 0, p)
            tokens_hi(16 * ps + 1)
            piece(ps, 0, 0)
            piece(ps, 0, 1)
            with act.Fori(0, EXPERTS - 1) as e:
                expert(ps, e)
            expert(ps, EXPERTS - 1, last=True)

        run_pass(0)
        act.wait_ge(flag_ready, 1)
        most = act.value_load(flag[0:1, 0:1])
        with act.If(most > CAP):
            with act.Fori(1, 3) as ps:
                run_pass(ps)
        act.wait_ge(fin_sum, 1)
        act.activation(small[:, 36:39], small[:, 32:35], ACT.Sqrt, bias=eps_r, scale=1.0 / D).then_inc(fin_root, 1)

    @block.vector
    def _(dve):
        own = Own(dve, dve_own)

        def width(n):
            return PIECES[n][2] * PC if n < ND else PIECE

        def split(n):
            dve.wait_ge(hi_done, n + 1)
            w = width(n)
            dve.tensor_tensor(wlo[:, n % SPLIT, 0:w], raw[:, n % RAW, 0:w], whi[:, n % SPLIT, 0:w].bitcast(F32),
                              ALU.subtract).then_inc(lo_done, 1)

        def pieces(stage, count, post=None, start=0):
            for n in range(FIRST[stage] + start, FIRST[stage] + start + count):
                if post is not None:
                    post(n)
                split(n + SPLIT)

        def job_copy(name, j, dst, rows_=P, cols=512):
            dve.wait_ge(aux_ready, AUX[name] + j + 1)
            dve.tensor_copy(dst, job_bank(name, j)[0:rows_, 0:cols]).then_inc(job_out(name, j)[0], 1)

        def to_sbuf(dst, base):
            def post(n):
                for o in range(2):
                    dve.wait_ge(*tile_ready(n, o))
                    f = (PIECES[n][3] - base) // P + o
                    dve.tensor_copy(dst[:, f, :], piece_bank(n, o)[:, 0:dst.shape[2]]).then_inc(tile_out(n, o)[0], 1)
            return post

        def add_residual(n):
            if not PIECES[n][5]:
                return
            for o in range(2):
                dve.wait_ge(*tile_ready(n, o))
                f = PIECES[n][3] // P + o
                dve.tensor_tensor(hT[:, f, :], hT[:, f, :], piece_bank(n, o)[:, 0:T], ALU.add).then_inc(tile_out(n, o)[0], 1)
            dve.wait_ge(*tile_out(n, 1))
            if f < KT - 1:
                dve.tensor_tensor(sq[:, f - 1:f + 1, :], hT[:, f - 1:f + 1, :], hT[:, f - 1:f + 1, :], ALU.mult)

        def last_square():
            dve.tensor_tensor(sq[:, KT - 2:KT, :], hT[:, KT - 2:KT, :], hT[:, KT - 2:KT, :], ALU.mult).then_inc(sq_done, 1)

        def residual_lo(row, tag):
            for k in range(KT):
                dve.wait_ge(xh_done, FEED[tag] + k + 1)
                dve.scalar_tensor_tensor(out=xl[:, k, :], in0=hT[:, k, :], scalar=vecs[:, k, row:row + 1],
                                         in1=xh[:, k, :].bitcast(F32), op0=ALU.mult, op1=ALU.subtract).then_inc(x_done, 1)
            last_square()

        def normed_pieces(stage, count, tag, post):
            inverse_root("rms_" + tag)
            pieces(stage, count, post)

        def square(before):
            dve.wait_ge(*before)
            dve.tensor_tensor(sq[:, :, :], hT[:, :, :], hT[:, :, :], ALU.mult).then_inc(sq_done, 1)

        def inverse_root(job):
            dve.wait_ge(*job_out(job))
            own(dve.reciprocal(stat[:, 1, :], stat[:, 0, :]))
            own.settle()

        def feed_lo(tag, row=None):
            for k in range(KT):
                dve.wait_ge(xh_done, FEED[tag] + k + 1)
                hi = xh[:, k, :].bitcast(F32)
                if row is None:
                    ins = dve.tensor_tensor(xl[:, k, :], sq[:, k, :], hi, ALU.subtract)
                else:
                    ins = dve.scalar_tensor_tensor(out=xl[:, k, :], in0=sq[:, k, :], scalar=vecs[:, k, row:row + 1], in1=hi,
                                                   op0=ALU.mult, op1=ALU.subtract)
                ins.then_inc(x_done, 1)

        def rms_feed(tag, job, row):
            inverse_root(job)
            for k in range(KT):
                dve.tensor_tensor(sq[:, k, :], hT[:, k, :], stat[:, 1, :], ALU.mult).then_inc(xn_done, 1)
            feed_lo(tag, row)

        def memory_lo(i, hi, lo, done):
            for k in range(KT):
                dve.wait_ge(mh_done, 8 * i + k + 1)
                dve.scalar_tensor_tensor(out=lo[:, k, 0:MEM], in0=memT[:, k, :], scalar=vecs[:, k, V_MEM + i:V_MEM + i + 1],
                                         in1=hi[:, k, 0:MEM].bitcast(F32), op0=ALU.mult, op1=ALU.subtract).then_inc(done, 1)

        def layer_norm_a(job, x):
            dve.wait_ge(aux_ready, AUX[job] + 1)
            dve.tensor_scalar(stat[:, 0, :], job_bank(job)[:, 0:T], 1.0 / D, None, ALU.mult).then_inc(job_out(job)[0], 1)
            dve.wait_ge(*job_out(job))
            for k in range(KT):
                own(dve.tensor_tensor(x[:, k, :], x[:, k, :], stat[:, 0, :], ALU.subtract))
            own.settle()
            dve.tensor_tensor(sq[:, :, :], x[:, :, :], x[:, :, :], ALU.mult).then_inc(lnsq_done, 1)

        def layer_norm_b(job, x, row_g, row_b):
            dve.wait_ge(*job_out(job))
            own(dve.reciprocal(stat[:, 2, :], stat[:, 1, :]))
            own.settle()
            for k in range(KT):
                own(dve.tensor_tensor(x[:, k, :], x[:, k, :], stat[:, 2, :], ALU.mult))
            for k in range(KT):
                own.settle(KT - 1)
                ins = own(dve.tensor_scalar(x[:, k, :], x[:, k, :], vecs[:, k, row_g:row_g + 1], vecs[:, k, row_b:row_b + 1],
                                            ALU.mult, ALU.add))
            own.settle()
            own_signal(lnv_done)

        def own_signal(s):
            dve.sem_inc(s, 1)

        own(dve.memset(small[:, 0:1], RMS_EPS))
        own(dve.memset(small[:, 1:2], LN_EPS))
        for e in range(EXPERTS):
            own(dve.memset(small[:, 24 + e:25 + e], float(EXPERTS - e)))
        own(dve.memset(pz[:, :, :, :, :], 0.0))
        dve.memset(small[:, 32:35], 1.0).then_inc(eps_set, 1)
        dve.wait_ge(ld_mem, 16)
        for m in range(2):
            dve.tensor_tensor_reduce(sq[:, :, :].rearrange("p k t -> p (k t)")[:, m * D:(m + 1) * D], mem_in[:, m, :],
                                     mem_in[:, m, :], 1.0, 0.0, ALU.mult, ALU.add, small[:, 2 + m:3 + m]).then_inc(mem_sum, 1)
        dve.wait_ge(mem_root, 1)
        own(dve.reciprocal(small[:, 6:8], small[:, 4:6]))
        own.settle()
        for m in range(2):
            dve.tensor_scalar(mem_in[:, m, :], mem_in[:, m, :], small[:, 6 + m:7 + m], None, ALU.mult).then_inc(mem_n, 1)
        job_copy("vec", 0, vecs[:, :, :].rearrange("p k v -> p (k v)"), P, KT * NV)
        for j in range(4):
            job_copy("mem_t", j, memT[:, 2 * j:2 * j + 2, :].rearrange("p k m -> p (k m)"))
        memory_lo(0, mh, ml, m_done)
        for k in range(KT):
            job_copy("x_t", k, hT[:, k, :], P, T)
        dve.wait_ge(mem_sum, 2)
        square(job_out("x_t", KT - 1))
        job_copy("ws_0", 0, ws0, P, KT)
        for n in range(SPLIT):
            split(n)
        pieces("k0", 4, to_sbuf(kT, 0))
        rms_feed("mix0", "rms_mix0", V_MIX)
        pieces("v0", 4)
        pieces("in_v", 4)
        pieces("in_u", 1)
        layer_norm_a("ln_a0", vT)
        pieces("in_u", 2, start=1)
        layer_norm_b("ln_b0", vT, V_ALNG, V_ALNB)
        pieces("in_u", 1, start=3)
        dve.wait_ge(ld_misc, 16)
        dve.wait_ge(*job_out("ws_0"))
        own(dve.tensor_tensor(sq[:, :, TP:T], vT[:, :, TP:T], ws0.unsqueeze(2).to_broadcast([P, KT, TS]), ALU.mult))
        own.settle()
        own(dve.tensor_tensor(sq[:, :, TP:T], sq[:, :, TP:T], bs0.unsqueeze(2).to_broadcast([P, KT, TS]), ALU.add))
        for j in range(4):
            dve.wait_ge(aux_ready, AUX["mixed"] + j + 1)
            for gg in range(2):
                g = 2 * j + gg
                ins = dve.tensor_tensor(sq[:, g, 0:TP].rearrange("p (c t) -> p c t", c=2),
                                        job_bank("mixed", j)[:, gg * TP:(gg + 1) * TP].rearrange("p (c t) -> p c t", c=2),
                                        bsb[:, g:g + 1, :].to_broadcast([P, 2, P]), ALU.add)
            ins.then_inc(job_out("mixed", j)[0], 1)
        dve.wait_ge(*stage_out("in_u", 4))
        own.settle()
        for k in range(KT):
            if k % 2 == 0:
                dve.wait_ge(*job_out("mixed", k // 2))
            dve.tensor_tensor(sq[:, k, :], sq[:, k, :], uT[:, k, :], ALU.mult).then_inc(xn_done, 1)
        feed_lo("mixed")
        pieces("a_out", 4, add_residual)

        def attention(i):
            residual_lo(V_XATT + i, f"xatt{i}")

            def q_out(n):
                for o in range(2):
                    dve.wait_ge(*tile_ready(n, o))
                    dve.tensor_tensor(qT[:, PIECES[n][3] // P + o, :], piece_bank(n, o)[:, 0:T], stat[:, 1, :], ALU.mult)\
                        .then_inc(tile_out(n, o)[0], 1)

            normed_pieces(f"q{i}", 4, f"xatt{i}", q_out)
            if i == 1:
                dve.wait_ge(stored, 16 * 4)
            for j in range(2):
                job_copy(f"q_tok{i}", j, qs[:, j * 512:(j + 1) * 512], TS)
            for j in range(4):
                tt, hh = j // 2, j % 2
                c = 4 * tt + 2 * hh
                dve.wait_ge(aux_ready, AUX[f"scores{i}"] + j + 1)
                own(dve.tensor_reduce(att[:, c:c + 2], job_bank(f"scores{i}", j)[:, :].rearrange("p (h m) -> p h m", h=2),
                                      AX.X, ALU.max))
                own.settle()
                dve.tensor_scalar(att[:, 8 + c:10 + c], att[:, c:c + 2], -SCALE, None, ALU.mult).then_inc(nmax_done, 1)
            for j in range(4):
                tt, hh = j // 2, j % 2
                c = 4 * tt + 2 * hh
                dve.wait_ge(*job_out(f"scores{i}", j))
                own(dve.reciprocal(att[:, 24 + c:26 + c], att[:, 16 + c:18 + c]))
                own.settle()
                for h2 in range(2):
                    h = 2 * hh + h2
                    ins = dve.tensor_scalar(pr[:, tt, h, :], pr[:, tt, h, :], att[:, 24 + c + h2:25 + c + h2], None, ALU.mult)
                ins.then_inc(p_done, 1)
            for s in range(TS):
                n = i * 2 * TS + s
                dve.wait_ge(kv_in[n % 3], 16 * (n // 3 + 1))
                for c in range(2):
                    j = 2 * s + c
                    dve.wait_ge(aux_ready, AUX[f"q_bc{i}"] + j + 1)
                    for h in (2 * c, 2 * c + 1):
                        for mt in range(2):
                            k = kv[:, n % 3, mt, h * HD:(h + 1) * HD]
                            ins = dve.tensor_tensor_reduce(k, k, job_bank(f"q_bc{i}", j)[:, (h % 2) * HD:(h % 2 + 1) * HD],
                                                           1.0, 0.0, ALU.mult, ALU.add,
                                                           sc[:, mt, s * HEADS + h:s * HEADS + h + 1])
                    ins.then_inc(job_out(f"q_bc{i}", j)[0], 1)
            n32 = TS * HEADS
            dve.wait_ge(aux_ready, AUX[f"s_t{i}"] + 1)
            own(dve.tensor_reduce(att[0:n32, 32:33], job_bank(f"s_t{i}")[0:n32, 0:MEM], AX.X, ALU.max))
            own.settle()
            dve.tensor_scalar(att[0:n32, 33:34], att[0:n32, 32:33], -SCALE, None, ALU.mult).then_inc(snmax_done, 1)
            for j in range(2):
                job_copy(f"p_t{i}", j, pT[:, j, :, 0:P])
            dve.wait_ge(*job_out(f"s_t{i}"))
            own(dve.reciprocal(att[0:n32, 35:36], att[0:n32, 34:35]))
            own.settle()
            dve.tensor_scalar(psm[:, :], psm[:, :], att[0:n32, 35:36], None, ALU.mult).then_inc(sp_done, 1)
            for j in range(2, 4):
                job_copy(f"p_t{i}", j, pT[:, j - 2, :, P:TP])
            dve.wait_ge(aux_ready, AUX[f"ps_t{i}"] + 1)
            for mt in range(2):
                src = job_bank(f"ps_t{i}")[:, mt * n32:(mt + 1) * n32].rearrange("p (s h) -> p h s", h=HEADS)
                ins = dve.tensor_copy(pz[:, mt, :, :, :].rearrange("p h s t -> p h (s t)")[:, :, 0:64:9], src)
            ins.then_inc(job_out(f"ps_t{i}")[0], 1)
            for j in range(4):
                dve.wait_ge(xoh_done, 4 * i + j + 1)
                dve.tensor_tensor(xl[:, 2 * j:2 * j + 2, 0:TP], job_bank(f"o_t{i}", j)[:, :].rearrange("p (f t) -> p f t", f=2),
                                  xh[:, 2 * j:2 * j + 2, 0:TP].bitcast(F32), ALU.subtract).then_inc(job_out(f"o_t{i}", j)[0], 1)
            for j in range(2):
                job_copy(f"s_o{i}", j, qs[:, j * 512:(j + 1) * 512], TS)
            job_copy(f"os_t{i}", 0, os8[:, :, :].rearrange("p k s -> p (k s)"), P, KT * TS)
            dve.wait_ge(osh_done, i + 1)
            dve.wait_ge(*job_out(f"o_t{i}", 3))
            for k in range(KT):
                dve.tensor_tensor(xl[:, k, TP:T], os8[:, k, :], xh[:, k, TP:T].bitcast(F32), ALU.subtract).then_inc(x_done, 1)
            pieces(f"o{i}", 4, add_residual)

        attention(0)
        residual_lo(V_FFN, "ffn0")

        def scaled_out(n, c, dst):
            for o in range(2):
                dve.wait_ge(*tile_ready(n, o))
                dve.tensor_tensor(dst[:, 2 * (c % 2) + o, :], piece_bank(n, o)[:, 0:T], stat[:, 1, :], ALU.mult)\
                    .then_inc(tile_out(n, o)[0], 1)

        def gated(n):
            c = (n - FIRST["gate_up"]) // 2
            if (n - FIRST["gate_up"]) % 2 == 0:
                if c >= 2:
                    dve.wait_ge(af_done, 2 * c - 2)
                scaled_out(n, c, sg)
                return
            if c >= 2:
                dve.wait_ge(a_done, 2 * c - 2)
            scaled_out(n, c, af)
            for o in range(2):
                slot = 2 * (c % 2) + o
                dve.wait_ge(gate_done, 2 * c + o + 1)
                dve.wait_ge(*tile_out(n, o))
                dve.tensor_tensor(af[:, slot, :], sg[:, slot, :], af[:, slot, :], ALU.mult).then_inc(af_done, 1)
            for o in range(2):
                dve.wait_ge(ah_done, 2 * c + o + 1)
                dve.tensor_tensor(al[:, 2 * c + o, :], af[:, 2 * (c % 2) + o, :], ah[:, 2 * c + o, :].bitcast(F32),
                                  ALU.subtract).then_inc(a_done, 1)

        normed_pieces("gate_up", 22, "ffn0", gated)
        dve.wait_ge(a_done, FT)
        pieces("down", 12, add_residual)
        residual_lo(V_MIX + 1, "mix1")

        def glu(n):
            c = (n - FIRST["pw1"]) // 2
            if (n - FIRST["pw1"]) % 2 == 0:
                if c >= 2:
                    dve.wait_ge(glu_done, 2 * c - 2)
                scaled_out(n, c, sg)
                return
            scaled_out(n, c, af)
            for o in range(2):
                f, slot = 2 * c + o, 2 * (c % 2) + o
                dve.wait_ge(gate_done, FT + f + 1)
                dve.wait_ge(*tile_out(n, o))
                dve.tensor_tensor(ce[:, f, STATE:STATE + TP], af[:, slot, 0:TP], sg[:, slot, 0:TP], ALU.mult)
                dve.tensor_tensor(se[:, f, :, STATE], af[:, slot, TP:T], sg[:, slot, TP:T], ALU.mult).then_inc(glu_done, 1)

        normed_pieces("pw1", 8, "mix1", glu)
        memory_lo(1, xh, xl, x_done)

        def conv_part(quarter):
            if quarter == 0:
                dve.wait_ge(pad_done, 1)
                dve.wait_ge(glu_done, KT)
            for j in range(4 * quarter, min(4 * quarter + 4, TAPS)):
                for k in range(CONV_POOL, KT):
                    w = vecs[:, k, V_DW + j:V_DW + j + 1]
                    if j == 0:
                        own(dve.tensor_scalar(cv[:, k, 0:TP], ce[:, k, 0:TP], w, vecs[:, k, V_BDW:V_BDW + 1], ALU.mult, ALU.add))
                    else:
                        own.settle(3)
                        own(dve.scalar_tensor_tensor(out=cv[:, k, 0:TP], in0=ce[:, k, j:j + TP], scalar=w, in1=cv[:, k, 0:TP],
                                                     op0=ALU.mult, op1=ALU.add))

        def with_conv(post, first):
            def both(n):
                if post is not None:
                    post(n)
                conv_part(n - FIRST["k1"])
            return both

        pieces("k1", 4, with_conv(to_sbuf(kT, 0), 0))
        pieces("v1", 4, with_conv(None, 4))
        dve.wait_ge(*job_out("state_t", 3))
        for k in range(KT):
            own(dve.tensor_tensor(sq[:, k, 0:TS * TAPS].rearrange("p (s j) -> p s j", s=TS), se[:, k, :, :],
                                  vecs[:, k:k + 1, V_DW:NV].to_broadcast([P, TS, TAPS]), ALU.mult))
        for k in range(KT):
            own.settle(KT - 1)
            own(dve.tensor_reduce(cv[:, k, TP:T], sq[:, k, 0:TS * TAPS].rearrange("p (s j) -> p s j", s=TS), AX.X, ALU.add))
        for k in range(KT):
            own.settle(KT - 1)
            own(dve.tensor_scalar(cv[:, k, TP:T], cv[:, k, TP:T], vecs[:, k, V_BDW:V_BDW + 1], None, ALU.add))
        own.settle()
        dve.wait_ge(tap_added, CONV_POOL // 2 * (TAPS - 1))
        own_signal(conv_done)
        layer_norm_a("ln_a1", cv)
        layer_norm_b("ln_b1", cv, V_BLNG, V_BLNB)
        feed_lo("conv")
        pieces("pw2", 4, add_residual)
        attention(1)

        last_square()
        inverse_root("rms_ffn1")
        for k in range(KT):
            dve.scalar_tensor_tensor(out=sq[:, k, :], in0=hT[:, k, :], scalar=vecs[:, k, V_FFN + 1:V_FFN + 2],
                                     in1=stat[:, 1, :], op0=ALU.mult, op1=ALU.mult).then_inc(hn_ready, 1)
        E = EXPERTS
        own(dve.memset(rt[:, :, :, :], 0.0))
        own.settle()
        dve.wait_ge(aux_ready, AUX["route"] + 1)
        y = job_bank("route")
        own(dve.tensor_copy(rt[:, 3, 0:2, 0:E], y[:, 0:32].rearrange("p (t e) -> p t e", e=16)[:, :, 0:E]))
        dve.tensor_copy(rt[0:TS, 3, 2, 0:E], y[0:TS, 32:32 + E]).then_inc(job_out("route")[0], 1)
        dve.wait_ge(*job_out("route"))
        own.settle()
        L = rt[:, 3, :, 0:E]
        order = order8.unsqueeze(1).to_broadcast([P, 3, E])

        def wide(x):
            return x.to_broadcast([P, 3, E])

        def first_of_largest(x, top, tmp, best, sel):
            own(dve.tensor_reduce(top, x, AX.X, ALU.max))
            own.settle()
            own(dve.tensor_tensor(tmp, x, wide(top), ALU.is_equal))
            own.settle()
            own(dve.tensor_tensor(tmp, tmp, order, ALU.mult))
            own.settle()
            own(dve.tensor_reduce(best, tmp, AX.X, ALU.max))
            own.settle()
            own(dve.tensor_tensor(sel, tmp, wide(best), ALU.is_equal))
            own.settle()

        top1, top2, best = rt[:, 10, :, 0:1], rt[:, 11, :, 0:1], rt[:, 9, :, 0:1]
        sel1, sel2, L2 = rt[:, 5, :, 0:E], rt[:, 8, :, 0:E], rt[:, 6, :, 0:E]
        first_of_largest(L, top1, rt[:, 4, :, 0:E], best, sel1)
        own(dve.scalar_tensor_tensor(out=L2, in0=sel1, scalar=-3.0e38, in1=L, op0=ALU.mult, op1=ALU.add))
        own.settle()
        first_of_largest(L2, top2, rt[:, 4, :, 0:E], best, sel2)
        dve.tensor_tensor(rt[:, 12, :, 0:1], top2, top1, ALU.subtract).then_inc(gate_gap, 1)
        own(dve.tensor_tensor(rt[:, 0, :, 0:E], sel1, sel2, ALU.add))
        own.settle()
        own_signal(mask_done)
        dve.wait_ge(gate_exp, 1)
        gexp, den, w1, w2 = rt[:, 13, :, 0:1], rt[:, 14, :, 0:1], rt[:, 15, :, 0:1], rt[:, 15, :, 1:2]
        own(dve.tensor_scalar(den, gexp, 1.0, None, ALU.add))
        own.settle()
        own(dve.reciprocal(w1, den))
        own.settle()
        own(dve.tensor_tensor(w2, gexp, w1, ALU.mult))
        own(dve.tensor_tensor(sel1, sel1, wide(w1), ALU.mult))
        own.settle()
        own(dve.tensor_tensor(sel2, sel2, wide(w2), ALU.mult))
        own.settle()
        own(dve.tensor_tensor(rt[:, 1, :, 0:E], sel1, sel2, ALU.add))
        dve.wait_ge(aux_ready, AUX["pos"] + 1)
        y = job_bank("pos", 0)
        own(dve.tensor_copy(rt[:, 2, 0:2, :], y[:, 0:32].rearrange("p (t e) -> p t e", e=16)[:, :, 0:E + 1]))
        dve.tensor_copy(rt[0:TS, 2, 2, :], y[0:TS, 32:33 + E]).then_inc(job_out("pos", 0)[0], 1)
        dve.wait_ge(*job_out("pos", 0))
        dve.wait_ge(aux_ready, AUX["pos"] + 2)
        dve.tensor_reduce(small[:, 40:41], job_bank("pos", 1)[:, 0:E], AX.X, ALU.max).then_inc(job_out("pos", 1)[0], 1)
        dve.wait_ge(*job_out("pos", 1))
        dve.tensor_copy(flag[:, 0:1], small[:, 40:41]).then_inc(flag_ready, 1)
        for j in range(6):
            tt, half = j // 2, j % 2
            n_rows = P if tt < 2 else TS
            cols = slice(half * 512, (half + 1) * 512)
            dve.wait_ge(hth_done, j + 1)
            dve.tensor_tensor(htl[0:n_rows, tt, cols], job_bank("hn_tok", j)[0:n_rows, :], hth[0:n_rows, tt, cols].bitcast(F32),
                              ALU.subtract).then_inc(job_out("hn_tok", j)[0], 1)
        for j in range(6):
            tt, half = j // 2, j % 2
            n_rows = P if tt < 2 else TS
            job_copy("y_tok", j, ytok[0:n_rows, tt, half * 512:(half + 1) * 512], n_rows)
        dve.wait_ge(*job_out("y_tok", 5))
        own.settle()
        dve.wait_ge(flag_ready, 1)

        G, U, ACC, TB, XB = (bank[0], bank[2]), (bank[1], bank[3]), (bank[4], bank[5]), bank[6], bank[7]
        ROWS = (P, P, TS)

        def split_moe(ps, e, p):
            dve.wait_ge(hi_done, piece_no(ps, e, p) + 1)
            dve.tensor_tensor(wlo[:, p % SPLIT, :], raw[:, p % RAW, :], whi[:, p % SPLIT, :].bitcast(F32),
                              ALU.subtract).then_inc(lo_done, 1)

        def build_s(column):
            for tt, n_rows in enumerate(ROWS):
                for dst in (sf, sr):
                    ins = dve.tensor_scalar(dst[0:n_rows, tt, :], iota[0:n_rows, :], rt[0:n_rows, 2, tt, bass.ds(column, 1)],
                                            rt[0:n_rows, 0, tt, bass.ds(column, 1)], ALU.is_equal, ALU.mult)
            ins.then_inc(s_built, 1)

        def tokens_lo(first):
            for j, src in enumerate((XB, G[1])):
                dve.wait_ge(xeh_done, first + j)
                dve.tensor_tensor(xel[:, 4 * j:4 * j + 4, :], src[:, :].rearrange("p (k r) -> p k r", k=4),
                                  xeh[:, 4 * j:4 * j + 4, :].bitcast(F32), ALU.subtract).then_inc(xel_done, 1)

        def take_prepared(value):
            dve.wait_ge(prep_ready, value)
            dve.tensor_copy(st[:, :], XB[:, 0:T])
            dve.tensor_copy(gr[:, 0:1], XB[:, 272:273]).then_inc(prep_done, 1)

        def h_lo(value):
            dve.wait_ge(hTh_done, value)
            dve.tensor_tensor(hTl[:, :], TB[:, :], hTh[:, :].bitcast(F32), ALU.subtract).then_inc(hTl_done, 1)

        def piece(ps, e, p, last=False):
            kind, c, half = EP[p]
            if kind == "u" and half == 0 and c >= 1:
                h_lo(56 * ps + 7 * e + c)
            if kind == "u" and half == 1:
                dve.wait_ge(silu_done, 56 * ps + 7 * e + c + 1)
                dve.wait_ge(piece_done, piece_no(ps, e, p) + 1)
                dve.tensor_tensor(hb[:, c % 2, :], hb[:, c % 2, :], U[c % 2][:, :], ALU.mult).then_inc(h_done, 1)
            if kind == "g" and half == 0 and c == 1:
                take_prepared(8 * ps + e + 1)
            if kind == "g" and half == 0 and c == 3 and not last:
                dve.wait_ge(prep_ready, 8 * ps + e + 1)
                build_s(e + 1)
            if p == NE - 2:
                h_lo(56 * ps + 7 * e + CH)
                if not last:
                    tokens_lo(16 * ps + 2 * e + 3)
            if not last or p + SPLIT < NE:
                split_moe(ps, e, p + SPLIT)

        def expert(ps, e, last=False):
            for p in range(2, NE):
                piece(ps, e, p, last)
            for half in range(2):
                dve.wait_ge(oeh_done, 16 * ps + 2 * e + half + 1)
                dve.scalar_tensor_tensor(out=oel[:, half * 512:(half + 1) * 512], in0=ACC[half][:, :], scalar=gr[:, 0:1],
                                         in1=oeh[:, half * 512:(half + 1) * 512].bitcast(F32), op0=ALU.mult,
                                         op1=ALU.subtract).then_inc(oel_done, 1)
            if not last:
                piece(ps, e + 1, 0)
                piece(ps, e + 1, 1)
            dve.wait_ge(y_added, sums(ps, e, 5))
            for j, src in enumerate((XB, TB, ACC[0], ACC[1], G[1], U[1])):
                tt, half = SCATTER[j]
                y = ytok[0:ROWS[tt], tt, half * 512:(half + 1) * 512]
                dve.wait_ge(sca_ready, 48 * ps + 6 * e + j + 1)
                dve.tensor_tensor(y, y, src[0:ROWS[tt], :], ALU.add).then_inc(y_added, 1)

        def run_pass(ps):
            if not (isinstance(ps, int) and ps == 0):
                dve.wait_ge(prep_ready, 8 * ps)
                dve.wait_ge(prep_done, 8 * ps)
                dve.tensor_scalar(rt[:, 2, :, :], rt[:, 2, :, :], float(-CAP), None, ALU.add).then_inc(pos_moved, 1)
                dve.wait_ge(pos_moved, ps)
            if not (isinstance(ps, int) and ps == 0):
                for p in range(SPLIT):
                    split_moe(ps, 0, p)
            build_s(0)
            tokens_lo(16 * ps + 1)
            piece(ps, 0, 0)
            piece(ps, 0, 1)
            with dve.Fori(0, EXPERTS - 1) as e:
                expert(ps, e)
            expert(ps, EXPERTS - 1, last=True)
            dve.wait_ge(y_added, 48 * ps + 54)

        dve.sem_inc(y_added, 6)
        dve.wait_ge(moe_const, 2)
        run_pass(0)
        most = dve.value_load(flag[0:1, 0:1])
        with dve.If(most > CAP):
            with dve.Fori(1, 3) as ps:
                run_pass(ps)

        for tt, n_rows in enumerate(ROWS):
            ins = dve.tensor_tensor_reduce(yo[0:n_rows, tt, :], ytok[0:n_rows, tt, :], ytok[0:n_rows, tt, :], 1.0, 0.0, ALU.mult,
                                           ALU.add, small[0:n_rows, 32 + tt:33 + tt])
        ins.then_inc(fin_sum, 1)
        dve.wait_ge(fin_root, 1)
        own(dve.reciprocal(small[:, 42:45], small[:, 36:39]))
        own.settle()
        dve.wait_ge(ld_grow, 16)
        for tt, n_rows in enumerate(ROWS):
            dve.scalar_tensor_tensor(out=yo[0:n_rows, tt, :], in0=ytok[0:n_rows, tt, :], scalar=small[0:n_rows, 42 + tt:43 + tt],
                                     in1=grow[0:n_rows, :], op0=ALU.mult, op1=ALU.mult).then_inc(fin_done, 1)


_IN = ['x_prompt', 'x_sample', 'mem_prompt', 'cache_mem_k', 'cache_mem_v', 'state_conv', 'norm_mix', 'norm_xattn', 'norm_ffn',
       'norm_mem', 'norm_final', 'w_xq', 'w_xk', 'w_xv', 'w_xo', 'a_w_in', 'a_ln_g', 'a_ln_b', 'a_w_s', 'a_b_s', 'a_w_out',
       'b_w_pw1', 'b_w_dw', 'b_b_dw', 'b_ln_g', 'b_ln_b', 'b_w_pw2', 'ffn_w_gate', 'ffn_w_up', 'ffn_w_down', 'moe_w_router',
       'moe_w_gate', 'moe_w_up', 'moe_w_down']
_OUT = [("y", (1, TP, D)), ("ys", (TS, 1, D)), ("k", (2, 1, MEM, HEADS, HD)), ("v", (2, 1, MEM, HEADS, HD)),
        ("conv_p", (1, 1, STATE, D)), ("conv_s", (1, TS, STATE, D)), ("chunk", (1, TS, 1, D))]


def kernel(**inputs):
    import numpy as np
    import concourse.bacc as bacc
    from concourse.bass_utils import run_bass_kernel_spmd

    nc = bacc.Bacc("TRN2", target_bir_lowering=False, num_devices=1)
    arrays, a, out = {}, {}, {}
    for name in _IN:
        arrays["in_" + name] = np.ascontiguousarray(inputs[name])
        a[name] = nc.dram_tensor("in_" + name, arrays["in_" + name].shape, F32, kind="ExternalInput").ap()
    for name, shape in _OUT:
        out[name] = nc.dram_tensor("out_" + name, shape, F32, kind="ExternalOutput").ap()
    with ExitStack() as ctx:
        build_step(nc, ctx, a, out)
    r = run_bass_kernel_spmd(nc, [arrays], core_ids=[0])
    return tuple(r.results[0]["out_" + name] for name, _ in _OUT)
```

```python
from contextlib import ExitStack

import concourse.bass as bass
from concourse import mybir

F32 = mybir.dt.float32
F32R = mybir.dt.float32r
I32 = mybir.dt.int32
ALU = mybir.AluOpType
ACT = mybir.ActivationFunctionType
AX = mybir.AxisListType

P = 128
D = 1024
KT = D // P
TP = 256
TS = 8
T = TP + TS
MEM = 256
HEADS = 4
HD = D // HEADS
CHUNK = 128
TAPS = 31
STATE = TAPS - 1
FFN = 2816
FT = FFN // P
EXPERTS = 8
EDIM = 3584
RMS_EPS = 1e-6
LN_EPS = 1e-5
SCALE = float(HD) ** -0.5

RAW = 6
SPLIT = 3
PIECE = 2048
PC = 256

(V_MIX, V_XATT, V_FFN, V_MEM, V_ALNG, V_ALNB, V_BDW, V_BLNG, V_BLNB, V_DW) = (0, 2, 4, 6, 8, 9, 10, 11, 12, 13)
NV = V_DW + TAPS

CONV_POOL = 4

EC = 512
CH = EDIM // EC
CAP = 128


def dense_pieces():
    out, first = [], {}

    def add(stage, weight, col, k0=0, nk=KT, opens=True, closes=True):
        first.setdefault(stage, len(out))
        out.append((weight, k0, nk, col, opens, closes))

    def whole(stage, weight, cols, base=0):
        for c in range(cols // PC):
            add(stage, weight, base + c * PC)

    whole("k0", "xk0", D)
    whole("v0", "xv0", D)
    whole("in_v", "a_in", D, D)
    whole("in_u", "a_in", D)
    whole("a_out", "a_out", D)
    whole("q0", "xq0", D)
    whole("o0", "xo0", D)
    for c in range(FFN // PC):
        add("gate_up", "gate", c * PC)
        add("gate_up", "up", c * PC)
    for c in range(D // PC):
        for k0 in range(0, FT, KT):
            add("down", "down", c * PC, k0, min(KT, FT - k0), k0 == 0, k0 + KT >= FT)
    for c in range(D // PC):
        add("pw1", "pw1", D + c * PC)
        add("pw1", "pw1", c * PC)
    whole("k1", "xk1", D)
    whole("v1", "xv1", D)
    whole("pw2", "pw2", D)
    whole("q1", "xq1", D)
    whole("o1", "xo1", D)
    groups, g = [], -1
    for p in out:
        g += p[4]
        groups.append(g)
    return out, groups, first


PIECES, GROUP, FIRST = dense_pieces()
ND = len(PIECES)
assert ND % RAW == 0 and ND % SPLIT == 0

EP = []
for _c in range(CH):
    EP += [("g", _c, 0), ("g", _c, 1), ("u", _c, 0), ("u", _c, 1)]
    if _c:
        EP += [("d", _c - 1, 0), ("d", _c - 1, 1)]
EP += [("d", CH - 1, 0), ("d", CH - 1, 1)]
NE = len(EP)
assert NE % RAW == 0 and NE % SPLIT == 0
ROWS = (P, P, TS)
SCATTER = ((0, 0), (0, 1), (1, 0), (1, 1), (2, 0), (2, 1))

AUX, _n = {}, 0
_ATT = [("rms_xatt", 1), ("q_tok", 2), ("scores", 4), ("q_bc", 16), ("s_t", 1), ("p_t", 4), ("ps_t", 1), ("o_t", 4),
        ("s_o", 2), ("os_t", 1)]
for _name, _count in (
    [("vec", 1), ("mem_t", 4), ("x_t", 8), ("ws_t", 2), ("ws_0", 1), ("rms_mix0", 1), ("k_tok0", 4), ("ln_a0", 1), ("ln_b0", 1),
     ("v_smp", 2), ("v_tok", 4), ("mixed", 4)] + [(n + "0", c) for n, c in _ATT]
    + [("rms_ffn0", 1), ("rms_mix1", 1), ("state_t", 4), ("k_tok1", 4), ("ln_a1", 1), ("ln_b1", 1), ("c_tok", 4)]
    + [(n + "1", c) for n, c in _ATT] + [("y_tok", 6), ("route", 1), ("pos", 2)]
):
    AUX[_name] = _n
    _n += _count

XW = {n: 8 * i for i, n in enumerate(["mix0", "mixed", "xatt0", "att0", "ffn0", "mix1", "mem1", "conv", "xatt1", "att1"])}
FEED = {n: 8 * i for i, n in enumerate(["mix0", "mixed", "xatt0", "ffn0", "mix1", "conv", "xatt1"])}
XN = {n: 8 * i for i, n in enumerate(["mix0", "mixed", "conv"])}
SQ = {n: i + 1 for i, n in enumerate(["mix0", "xatt0", "ffn0", "mix1", "xatt1"])}


class Own:

    def __init__(self, eng, chain):
        self.eng, self.chain, self.count, self.waited = eng, chain, 0, 0

    def __call__(self, ins):
        self.count += 1
        return ins.then_inc(self.chain, 1)

    def settle(self, lag=0):
        if self.count - lag > self.waited:
            self.waited = self.count - lag
            self.eng.wait_ge(self.chain, self.waited)


def build_step(nc, ctx, a, out):
    place = [-(-nc.sbuf_base // 32) * 32]

    def at(name, shape, dt, off=None):
        size = 4
        for n in shape[1:]:
            size *= n
        if off is None:
            off = place[0]
            place[0] += -(-size // 32) * 32
        assert off % 32 == 0 and off + size <= nc.sbuf_usable_end, (name, off + size, nc.sbuf_usable_end)
        return nc.alloc_sbuf_tensor_at(name, shape, dt, offset=off)

    def sem(name):
        return ctx.enter_context(nc.semaphore(name))

    raw = at("raw", [P, RAW, PIECE], F32)
    whi = at("whi", [P, SPLIT, PIECE], F32R)
    wlo = at("wlo", [P, SPLIT, PIECE], F32R)
    vecs = at("vecs", [P, KT, NV], F32)
    ident = at("ident", [P, P], F32)
    ones = at("ones", [P, P], F32)
    stat = at("stat", [P, 3, T], F32)
    sprob = at("sprob", [P, 2, TS * HEADS], F32)
    pick = at("pick", [P, TS, TS], F32)
    wr = at("wr", [P, KT, EXPERTS], F32)
    small = at("small", [P, 48], F32)
    os8 = at("os8", [P, KT, TS], F32)
    flag = at("flag", [P, 8], I32)
    b_off = place[0]
    hT = at("hT", [P, KT, T], F32)
    xh = at("xh", [P, KT, T], F32R)
    xl = at("xl", [P, KT, T], F32R)
    sq_off = place[0]
    sq = at("sq", [P, KT, T], F32)
    c_off = place[0]
    memT = at("memT", [P, KT, MEM], F32)
    kT = at("kT", [P, KT, MEM], F32)
    vm = at("vm", [P, 2, D], F32)
    e_off = place[0]
    mh = at("mh", [P, KT, MEM], F32R, e_off)
    ml = at("ml", [P, KT, MEM], F32R, e_off + 8192)
    mem_in = at("mem_in", [P, 2, D], F32, e_off + 16384)
    x_in = at("x_in", [P, 3, D], F32, e_off + 24576)
    rows = at("rows", [NV, D], F32, e_off + 37376)
    ws_in = at("ws_in", [P, KT, P], F32, e_off + 41472)
    uT = at("uT", [P, KT, T], F32, e_off)
    vT = at("vT", [P, KT, T], F32, e_off + 8448)
    vtok = at("vtok", [P, 2, D], F32, e_off + 16896)
    kst = at("kst", [P, 2, D], F32, e_off + 25088)
    wsT = at("wsT", [P, KT, P], F32, e_off + 33280)
    bsb = at("bsb", [P, KT, P], F32, e_off + 37376)
    vs_out = at("vs_out", [TS, D], F32, e_off + 41472)
    qT = at("qT", [P, KT, T], F32, e_off)
    pT = at("pT", [P, 2, HEADS, TP], F32, e_off + 8448)
    qs = at("qs", [TS, D], F32, e_off + 16640)
    kv = at("kv", [P, 3, 2, D], F32, e_off + 20736)
    va = at("va", [P, 2, D], F32, e_off)
    vb = at("vb", [P, 2, D], F32, c_off + 8192)
    sc = at("sc", [P, 2, TS * HEADS], F32, e_off + 45312)
    att = at("att", [P, 64], F32, e_off + 45568)
    psm = at("psm", [TS * HEADS, MEM], F32, e_off + 45824)
    pr = at("pr", [P, 2, HEADS, MEM], F32, sq_off)
    ah = at("ah", [P, FT, T], F32R, e_off)
    al = at("al", [P, FT, T], F32R, e_off + 23232)
    sg = at("sg", [P, 4, T], F32, sq_off)
    af = at("af", [P, 4, T], F32, sq_off + 4224)
    ce = at("ce", [P, KT, STATE + TP], F32, e_off)
    se = at("se", [P, KT, TS, TAPS], F32, e_off + 9152)
    cv = at("cv", [P, KT, T], F32, e_off + 17088)
    st_in = at("st_in", [4 * STATE, 2, D], F32, e_off + 25536)
    kst1 = at("kst1", [P, 2, D], F32, e_off + 33728)
    tap = at("tap", [P, 2, 2, TP], F32, e_off + 41920)
    c_out = at("c_out", [STATE, D], F32, e_off + 41920)
    cs_out = at("cs_out", [TS, D], F32, e_off + 29632)
    hth = at("hth", [P, 3, D], F32R, e_off)
    htl = at("htl", [P, 3, D], F32R, e_off + 12288)
    hnf = at("hnf", [P, 3, D], F32, e_off + 12288)
    frow = at("frow", [P, D], F32, c_off + 4096)
    ytok = at("ytok", [P, 3, D], F32, e_off + 24576)
    hb = at("hb", [P, 2, EC], F32, e_off + 36864)
    sf = at("sf", [P, 3, CAP], F32, e_off + 40960)
    sr = at("sr", [P, 3, CAP], F32R, e_off + 42496)
    st = at("st", [CAP, T], F32R, e_off + 44032)
    gr = at("gr", [CAP, 8], F32, e_off + 45088)
    iota = at("iota", [P, CAP], F32, e_off + 45120)
    tri = at("tri", [P, P], F32, e_off + 45632)
    xeh = at("xeh", [P, KT, CAP], F32R, c_off)
    xel = at("xel", [P, KT, CAP], F32R, c_off + 4096)
    hTh = at("hTh", [P, EC], F32R, c_off + 8192)
    hTl = at("hTl", [P, EC], F32R, c_off + 10240)
    oeh = at("oeh", [CAP, D], F32R, c_off + 12288)
    oel = at("oel", [CAP, D], F32R, c_off + 16384)
    grow = at("grow", [P, D], F32, c_off + 20480)
    rt = at("rt", [P, 16, 3, EXPERTS + 1], F32, b_off + 8448)
    yo = at("yo", [P, 3, D], F32, b_off)

    bank = [nc.alloc_psum_tensor(f"bank{i}", [P, 512], F32) for i in range(8)]
    eps_r, eps_l = small[:, 0:1], small[:, 1:2]
    ws0, bs0 = small[:, 8:16], bsb[:, :, 0]
    order8 = small[:, 24:32]

    landed = [sem(f"raw{i}_landed") for i in range(RAW)]
    hi_done, lo_done, piece_done, tile0_done = sem("hi_done"), sem("lo_done"), sem("piece_done"), sem("tile0_done")
    evac = [sem(f"bank{i}_evac") for i in range(4)]
    aux_ready = sem("aux_ready")
    aux_free = [sem(f"aux{i}_free") for i in range(4)]
    act_own, dve_own, pool_own = sem("act_own"), sem("dve_own"), sem("pool_own")
    x_done, xn_done, xh_done, xoh_done, osh_done, mh_done, m_done, sq_done = (
        sem(n) for n in ("x_done", "xn_done", "xh_done", "xoh_done", "osh_done", "mh_done", "m_done", "sq_done"))
    consts, ld_mem, ld_x, ld_rows, ld_ws, ld_misc, ld_state, ld_wr, ld_grow = (
        sem(n) for n in ("consts", "ld_mem", "ld_x", "ld_rows", "ld_ws", "ld_misc", "ld_state", "ld_wr", "ld_grow"))
    kv_in = [sem(f"kv{i}_in") for i in range(3)]
    mem_sum, mem_root, mem_n, ws_masked, kst_out, vm_out, stored, eps_set = (
        sem(n) for n in ("mem_sum", "mem_root", "mem_n", "ws_masked", "kst_out", "vm_out", "stored", "eps_set"))
    ah_done, a_done, lnsq_done, lnv_done, conv_done, nmax_done, p_done, snmax_done, sp_done, vused, pad_done = (
        sem(n) for n in ("ah_done", "a_done", "lnsq_done", "lnv_done", "conv_done", "nmax_done", "p_done", "snmax_done",
                         "sp_done", "vused", "pad_done"))
    gate_gap, gate_exp, mask_done, hth_done, flag_ready, moe_const = (
        sem(n) for n in ("gate_gap", "gate_exp", "mask_done", "hth_done", "flag_ready", "moe_const"))
    t_ready, gat_ready, sca_ready, prep_ready = (sem(n) for n in ("t_ready", "gat_ready", "sca_ready", "prep_ready"))
    silu_done, hTh_done, xeh_done, oeh_done = (sem(n) for n in ("silu_done", "hTh_done", "xeh_done", "oeh_done"))
    h_done, hTl_done, xel_done, oel_done, y_added, s_built, prep_done, pos_moved = (
        sem(n) for n in ("h_done", "hTl_done", "xel_done", "oel_done", "y_added", "s_built", "prep_done", "pos_moved"))
    ld_frow, wr_scaled, tok_sum, tok_root, hn_done = (
        sem(n) for n in ("ld_frow", "wr_scaled", "tok_sum", "tok_root", "hn_done"))
    v_scaled, v_summed, va_in, vb_in = sem("v_scaled"), sem("v_summed"), sem("va_in"), sem("vb_in")
    samples_done, lnx_done, rsum_done = sem("samples_done"), sem("lnx_done"), sem("rsum_done")
    gate_done, af_done, glu_done, tap_done, tap_added = (sem(n) for n in ("gate_done", "af_done", "glu_done", "tap_done", "tap_added"))
    y_stored = sem("y_stored")
    fin_start, fin_sum, fin_root, fin_done = (sem(n) for n in ("fin_start", "fin_sum", "fin_root", "fin_done"))

    def by_row_tiles(w):
        return w.rearrange("(t p) n -> p t n", p=P)

    W = {"a_in": by_row_tiles(a["a_w_in"][0]), "a_out": by_row_tiles(a["a_w_out"][0]),
         "gate": by_row_tiles(a["ffn_w_gate"][0]), "up": by_row_tiles(a["ffn_w_up"][0]),
         "down": by_row_tiles(a["ffn_w_down"][0]), "pw1": by_row_tiles(a["b_w_pw1"][0]),
         "pw2": by_row_tiles(a["b_w_pw2"][0])}
    for i in range(2):
        for n in "qkvo":
            W[f"x{n}{i}"] = by_row_tiles(a[f"w_x{n}"][i])
    moe = {"g": a["moe_w_gate"].rearrange("o e (t p) n -> p (o e t) n", p=P),
           "u": a["moe_w_up"].rearrange("o e (t p) n -> p (o e t) n", p=P),
           "d": a["moe_w_down"].rearrange("o e (t p) n -> p (o e t) n", p=P)}

    def moe_source(e, p):
        kind, c, half = EP[p]
        if kind == "d":
            return moe["d"][:, bass.ds(e * (EDIM // P) + 4 * c, 4), half * EC:(half + 1) * EC]
        return moe[kind][:, bass.ds(e * KT + 4 * half, 4), c * EC:(c + 1) * EC]

    def piece_no(ps, e, p):
        return ND + ps * (EXPERTS * NE) + e * NE + p

    def sums(ps, e, j):
        return 48 * ps + 6 * e + j + 1

    def tile_ready(n, o):
        return (tile0_done, GROUP[n] + 1) if o == 0 else (piece_done, n + 1)

    def tile_out(n, o):
        return evac[2 * (GROUP[n] % 2) + o], GROUP[n] // 2 + 1

    def stage_out(stage, count):
        return tile_out(FIRST[stage] + count - 1, 1)

    def ring_slot(r):
        return kv[:, r % 3, :, :], (kv_in[r % 3], 16 * (r // 3 + 1))

    def key_slot(i, s):
        return ring_slot(12 * i + s)

    def value_slot(i, s):
        if s in (0, 5):
            return va[:, :, :], (va_in, 16 * (2 * i + s // 5 + 1))
        if s in (1, 6):
            return vb[:, :, :], (vb_in, 16 * (2 * i + s // 6 + 1))
        return ring_slot(12 * i + 8 + (2, 3, 4, 7).index(s))

    def residual_out(stage, count, k):
        return tile_out(FIRST[stage] + (k // 2 + 1) * (count // 4) - 1, k % 2)

    def job_out(name, j=0):
        n = AUX[name] + j
        return aux_free[n % 4], n // 4 + 1

    def job_bank(name, j=0):
        return bank[4 + (AUX[name] + j) % 4]

    def piece_bank(n, o):
        return bank[2 * (GROUP[n] % 2) + o]

    block = ctx.enter_context(nc.Block())

    @block.sync
    def _(sp):
        sp.dma_start(mem_in[:, :, :], a["mem_prompt"][0].rearrange("(m p) d -> p m d", p=P)).then_inc(ld_mem, 16)
        for v0, n, name in ((V_MIX, 2, "norm_mix"), (V_XATT, 2, "norm_xattn"), (V_FFN, 2, "norm_ffn"), (V_MEM, 2, "norm_mem"),
                            (V_ALNG, 1, "a_ln_g"), (V_ALNB, 1, "a_ln_b"), (V_BDW, 1, "b_b_dw"), (V_BLNG, 1, "b_ln_g"),
                            (V_BLNB, 1, "b_ln_b")):
            sp.dma_start(rows[v0:v0 + n, :], a[name]).then_inc(ld_rows, 16)
        sp.dma_start(rows[V_DW:NV, :], a["b_w_dw"][0]).then_inc(ld_rows, 16)
        sp.dma_start(x_in[:, 0:2, :], a["x_prompt"][0].rearrange("(m p) d -> p m d", p=P)).then_inc(ld_x, 16)
        sp.dma_start(x_in[0:TS, 2, :], a["x_sample"].rearrange("b s d -> (b s) d")).then_inc(ld_x, 16)
        sp.dma_start(ws_in[:, :, :], a["a_w_s"][0].rearrange("g t s -> t g s")).then_inc(ld_ws, 16)
        for n, (w, k0, nk, c0, _, _) in enumerate(PIECES):
            if n >= RAW:
                sp.wait_ge(lo_done, n - RAW + 1)
            dst = raw[:, n % RAW, 0:nk * PC].rearrange("p (t n) -> p t n", n=PC)
            sp.dma_start(dst, W[w][:, k0:k0 + nk, c0:c0 + PC]).then_inc(landed[n % RAW], 16)

        def load(ps, e, p):
            sp.wait_ge(lo_done, piece_no(ps, e, p) - RAW + 1)
            dst = raw[:, p % RAW, :].rearrange("p (t n) -> p t n", n=EC)
            sp.dma_start(dst, moe_source(e, p)).then_inc(landed[p % RAW], 16)

        def run_pass(ps):
            with sp.Fori(0, EXPERTS) as e:
                for p in range(NE):
                    load(ps, e, p)

        run_pass(0)
        sp.wait_ge(flag_ready, 1)
        most = sp.value_load(flag[0:1, 0:1])
        with sp.If(most > CAP):
            with sp.Fori(1, 3) as ps:
                run_pass(ps)
        for tt in range(2):
            sp.wait_ge(fin_done, tt + 1)
            sp.dma_start(out["y"][0, tt * P:(tt + 1) * P, :], yo[:, tt, :]).then_inc(y_stored, 16)
        sp.wait_ge(fin_done, 3)
        sp.dma_start(out["ys"].rearrange("b s d -> (b s) d"), yo[0:TS, 2, :]).then_inc(y_stored, 16)
        sp.wait_ge(y_stored, 16 * 3)

    @block.gpsimd
    def _(pool):
        own = Own(pool, pool_own)
        own(pool.memset(ident[:, :], 0.0))
        pool.memset(ones[:, :], 1.0).then_inc(consts, 1)
        own.settle()
        pool.affine_select(out=ident[:, :], in_=ident[:, :], compare_op=ALU.not_equal, fill=1.0, base=0,
                           pattern=[[-1, P]], channel_multiplier=1).then_inc(consts, 1)
        pool.dma_start(wr[:, :, :], a["moe_w_router"][0].rearrange("(t p) n -> p t n", p=P)).then_inc(ld_wr, 16)
        pool.wait_ge(*job_out("vec"))
        pool.dma_start(bsb[:, :, :], a["a_b_s"].to_broadcast([P, KT, P])).then_inc(ld_misc, 16)
        pool.wait_ge(*job_out("ws_t", 0))
        pool.wait_ge(*job_out("ws_t", 1))
        pool.affine_select(out=wsT[:, :, :], in_=wsT[:, :, :], compare_op=ALU.is_ge, fill=0.0, base=0,
                           pattern=[[0, KT], [1, P]], channel_multiplier=-1).then_inc(ws_masked, 1)

        def store_memory(i, stage):
            pool.wait_ge(*stage_out(f"v{i}", 4))
            pool.dma_start(out["v"][i, 0].rearrange("(m p) h d -> p m (h d)", p=P), vm[:, :, :]).then_inc(vm_out, 16)
            pool.wait_ge(*job_out(f"k_tok{i}", 3))
            pool.dma_start(out["k"][i, 0].rearrange("(m p) h d -> p m (h d)", p=P), stage[:, :, :]).then_inc(kst_out, 16)

        def load_caches(i):
            def load(cache, s, place):
                dst, (loaded, _) = place
                pool.dma_start(dst, a[cache][i, s].rearrange("(m p) h d -> p m (h d)", p=P)).then_inc(loaded, 16)

            for s in range(TS):
                if s == 3:
                    pool.wait_ge(aux_ready, AUX[f"scores{i}"] + 4)
                    load("cache_mem_v", 0, value_slot(i, 0))
                    load("cache_mem_v", 1, value_slot(i, 1))
                if s >= 3:
                    pool.wait_ge(*job_out(f"q_bc{i}", 2 * (s - 3) + 1))
                elif i == 1 and s < 2:
                    pool.wait_ge(vused, s + 4)
                elif i == 1:
                    pool.wait_ge(aux_ready, AUX["s_o0"] + 2)
                load("cache_mem_k", s, key_slot(i, s))
            for s in range(2, TS):
                if s < 5:
                    pool.wait_ge(*job_out(f"q_bc{i}", 2 * (s + 3) + 1))
                else:
                    pool.wait_ge(vused, (TS - 1) * i + s - 4)
                load("cache_mem_v", s, value_slot(i, s))

        store_memory(0, kst)
        pool.wait_ge(*job_out("v_smp", 1))
        pool.dma_start(out["chunk"].rearrange("l b s d -> (l b s) d"), vs_out[:, :]).then_inc(stored, 16)
        pool.wait_ge(kst_out, 16)
        pool.wait_ge(stored, 16)
        pool.wait_ge(x_done, XW["mixed"] + 8)
        load_caches(0)
        pool.wait_ge(piece_done, FIRST["pw1"])
        pool.memset(ce[:, :, 0:STATE], 0.0).then_inc(pad_done, 1)
        for half in range(2):
            src = a["state_conv"][0, 4 * half:4 * half + 4].rearrange("s j d -> (s j) d")
            pool.dma_start(st_in[:, half, :], src).then_inc(ld_state, 16)
        pool.dma_start(out["conv_s"][0, :, 0:STATE - 1, :], a["state_conv"][0, :, 1:STATE, :]).then_inc(stored, 16)
        for u in range(CONV_POOL // 2 * TAPS):
            pair, j = u // TAPS, u % TAPS
            if j == 0:
                continue
            i = u - pair - 1
            pool.wait_ge(tap_done, u + 1)
            if i > 0:
                pool.wait_ge(tap_added, i)
            acc = cv[:, 2 * pair:2 * pair + 2, 0:TP]
            pool.tensor_tensor(acc, acc, tap[:, i % 2, :, :], ALU.add).then_inc(tap_added, 1)
        store_memory(1, kst1)
        pool.wait_ge(*job_out("c_tok", 3))
        pool.wait_ge(*job_out("c_tok", 1))
        pool.dma_start(out["conv_p"][0, 0], c_out[:, :]).then_inc(stored, 16)
        pool.dma_start(out["conv_s"][0, :, STATE - 1, :], cs_out[:, :]).then_inc(stored, 16)
        pool.wait_ge(kst_out, 32)
        pool.wait_ge(vm_out, 32)
        pool.wait_ge(stored, 16 * 4)
        pool.wait_ge(x_done, XW["conv"] + 8)
        pool.dma_start(frow[:, :], a["norm_ffn"][1:2, :].to_broadcast([P, D])).then_inc(ld_frow, 16)
        load_caches(1)
        pool.wait_ge(piece_done, ND)
        pool.dma_start(grow[:, :], a["norm_final"].rearrange("(o d) -> o d", o=1).to_broadcast([P, D])).then_inc(ld_grow, 16)
        pool.iota(iota[:, :], pattern=[[1, CAP]], base=0, channel_multiplier=0,
                  allow_small_or_imprecise_dtypes=True).then_inc(moe_const, 1)
        own(pool.memset(tri[:, :], 1.0))
        own.settle()
        pool.affine_select(out=tri[:, :], in_=tri[:, :], compare_op=ALU.is_gt, fill=0.0, base=0,
                           pattern=[[1, P]], channel_multiplier=-1).then_inc(moe_const, 1)

    @block.tensor
    def _(pe):
        def aux(name, j=0):
            n = AUX[name] + j
            if n >= 4:
                pe.wait_ge(aux_free[n % 4], n // 4)
            return bank[4 + n % 4]

        def product(stage, count, hi, lo, ready=None, tokens_stationary=False, start=0):
            for n in range(FIRST[stage] + start, FIRST[stage] + start + count):
                _, k0, nk, _, opens, closes = PIECES[n]
                g = GROUP[n]
                pe.wait_ge(lo_done, n + 1)
                for o in range(2):
                    b = 2 * (g % 2) + o
                    if opens and g >= 2:
                        pe.wait_ge(evac[b], g // 2)
                    for k in range(nk):
                        if ready is not None and n == FIRST[stage] and o == 0:
                            pe.wait_ge(ready[0], ready[1] + k + 1)
                        w_hi = whi[:, n % SPLIT, k * PC:(k + 1) * PC]
                        w_lo = wlo[:, n % SPLIT, k * PC:(k + 1) * PC]
                        first, last = opens and k == 0, closes and k == nk - 1
                        if tokens_stationary:
                            x_hi, x_lo = hi[:, k0 + k, o * P:(o + 1) * P], lo[:, k0 + k, o * P:(o + 1) * P]
                            y = bank[b][:, 0:PC]
                            pe.matmul(y, x_hi, w_hi, start=first, stop=False)
                            pe.matmul(y, x_hi, w_lo, start=False, stop=False)
                            mm = pe.matmul(y, x_lo, w_hi, start=False, stop=last)
                        else:
                            x_hi, x_lo = hi[:, k0 + k, :], lo[:, k0 + k, :]
                            y = bank[b][:, 0:hi.shape[2]]
                            cols = slice(o * P, (o + 1) * P)
                            pe.matmul(y, w_hi[:, cols], x_hi, start=first, stop=False)
                            pe.matmul(y, w_hi[:, cols], x_lo, start=False, stop=False)
                            mm = pe.matmul(y, w_lo[:, cols], x_hi, start=False, stop=last)
                    if o == 0 and closes:
                        mm.then_inc(tile0_done, 1)
                mm.then_inc(piece_done, 1)

        def channel_sum(job, src, waits, order=range(KT)):
            y = aux(job)
            for k in order:
                for wait in waits.get(k, ()):
                    pe.wait_ge(*wait)
                mm = pe.matmul(y[:, 0:T], ones[:, :], src[:, k, :], start=(k == order[0]), stop=(k == order[-1]))
            mm.then_inc(aux_ready, 1)

        def pairs(first):
            return {k: [(lnsq_done, first + k // 2 + 1)] for k in range(0, KT, 2)}

        def turn(dst, src, rows_):
            return pe.transpose(dst, src, ident[0:rows_, 0:rows_])

        pe.wait_ge(consts, 2)
        pe.wait_ge(ld_rows, 160)
        y = aux("vec")
        for k in range(KT):
            mm = turn(y[:, k * NV:(k + 1) * NV], rows[:, k * P:(k + 1) * P], NV)
        mm.then_inc(aux_ready, 1)
        pe.wait_ge(mem_n, 2)
        for j in range(4):
            y = aux("mem_t", j)
            for kk in range(2):
                for m in range(2):
                    k = 2 * j + kk
                    mm = turn(y[:, kk * MEM + m * P:kk * MEM + (m + 1) * P], mem_in[:, m, k * P:(k + 1) * P], P)
            mm.then_inc(aux_ready, 1)
        product("k0", 1, mh[:, :, :], ml[:, :, :], (m_done, 0))
        pe.wait_ge(ld_x, 32)
        for k in range(KT):
            y = aux("x_t", k)
            for m in range(2):
                turn(y[:, m * P:(m + 1) * P], x_in[:, m, k * P:(k + 1) * P], P)
            turn(y[:, TP:T], x_in[0:TS, 2, k * P:(k + 1) * P], TS).then_inc(aux_ready, 1)
        pe.wait_ge(ld_ws, 16)
        for j in range(2):
            y = aux("ws_t", j)
            for gg in range(4):
                mm = turn(y[:, gg * P:(gg + 1) * P], ws_in[:, 4 * j + gg, :], P)
            mm.then_inc(aux_ready, 1)
        pe.matmul(aux("ws_0")[:, 0:KT], ones[0:1, :], ws_in[0:1, :, 0], start=True, stop=True).then_inc(aux_ready, 1)

        def memory(i, hi, lo):
            product(f"v{i}", 4, hi, lo, None, True)
            pe.wait_ge(*stage_out(f"k{i}", 4))
            for j in range(4):
                y = aux(f"k_tok{i}", j)
                m, half = j // 2, j % 2
                for kk in range(4):
                    mm = turn(y[:, kk * P:(kk + 1) * P], kT[:, 4 * half + kk, m * P:(m + 1) * P], P)
                mm.then_inc(aux_ready, 1)

        product("k0", 3, mh[:, :, :], ml[:, :, :], start=1)
        channel_sum("rms_mix0", sq, {0: [(sq_done, SQ["mix0"])]})
        memory(0, mh[:, :, :], ml[:, :, :])
        x_hi, x_lo = xh[:, :, :], xl[:, :, :]
        product("in_v", 4, x_hi, x_lo, (x_done, XW["mix0"]))
        product("in_u", 1, x_hi, x_lo)
        channel_sum("ln_a0", vT, {0: [stage_out("in_v", 4)]})
        product("in_u", 2, x_hi, x_lo, start=1)
        channel_sum("ln_b0", sq, pairs(0))
        product("in_u", 1, x_hi, x_lo, start=3)
        pe.wait_ge(lnv_done, 1)
        for j in range(2):
            y = aux("v_smp", j)
            for kk in range(4):
                mm = turn(y[0:TS, kk * P:(kk + 1) * P], vT[:, 4 * j + kk, TP:T], P)
            mm.then_inc(aux_ready, 1)
        for j in range(4):
            y = aux("v_tok", j)
            c, half = j // 2, j % 2
            for kk in range(4):
                mm = turn(y[:, kk * P:(kk + 1) * P], vT[:, 4 * half + kk, c * CHUNK:(c + 1) * CHUNK], P)
            mm.then_inc(aux_ready, 1)
        pe.wait_ge(ws_masked, 1)
        pe.wait_ge(*job_out("v_tok", 3))
        for j in range(4):
            y = aux("mixed", j)
            for gg in range(2):
                g = 2 * j + gg
                for c in range(2):
                    mm = pe.matmul(y[:, (2 * gg + c) * P:(2 * gg + c + 1) * P], vtok[:, c, g * P:(g + 1) * P], wsT[:, g, :],
                                   start=(gg == 0 and c == 0), stop=True, skip_group_check=True)
            mm.then_inc(aux_ready, 1)
        product("a_out", 4, x_hi, x_lo, (x_done, XW["mixed"]))

        def normed_product(stage, count, tag):
            product(stage, 1, x_hi, x_lo, (x_done, XW[tag]))
            channel_sum("rms_" + tag, sq, {0: [(sq_done, SQ[tag])]})
            product(stage, count - 1, x_hi, x_lo, start=1)

        def attention(i):
            normed_product(f"q{i}", 4, f"xatt{i}")
            pe.wait_ge(*stage_out(f"q{i}", 4))
            for j in range(2):
                y = aux(f"q_tok{i}", j)
                for kk in range(4):
                    mm = turn(y[0:TS, kk * P:(kk + 1) * P], qT[:, 4 * j + kk, TP:T], P)
                mm.then_inc(aux_ready, 1)
            for j in range(4):
                y = aux(f"scores{i}", j)
                tt, hh = j // 2, j % 2
                for h2 in range(2):
                    for dh in range(2):
                        f = 2 * (2 * hh + h2) + dh
                        mm = pe.matmul(y[:, h2 * MEM:(h2 + 1) * MEM], qT[:, f, tt * P:(tt + 1) * P], kT[:, f, :],
                                       start=(h2 == 0 and dh == 0), stop=(dh == 1), skip_group_check=True)
                mm.then_inc(aux_ready, 1)
            pe.wait_ge(*job_out(f"q_tok{i}", 0))
            pe.wait_ge(*job_out(f"q_tok{i}", 1))
            for s in range(TS):
                for c in range(2):
                    y = aux(f"q_bc{i}", 2 * s + c)
                    pe.matmul(y[:, :], ident[0:TS, s:s + 1].to_broadcast([TS, P]), qs[:, c * 512:(c + 1) * 512],
                              start=True, stop=True).then_inc(aux_ready, 1)
            pe.wait_ge(*job_out(f"q_bc{i}", 15))
            y = aux(f"s_t{i}")
            for mt in range(2):
                mm = turn(y[0:TS * HEADS, mt * P:(mt + 1) * P], sc[:, mt, :], P)
            mm.then_inc(aux_ready, 1)
            for j in range(4):
                tt, mt = j // 2, j % 2
                y = aux(f"p_t{i}", j)
                pe.wait_ge(p_done, 4 * i + 2 * tt + 2)
                for h in range(HEADS):
                    mm = turn(y[:, h * P:(h + 1) * P], pr[:, tt, h, mt * P:(mt + 1) * P], P)
                mm.then_inc(aux_ready, 1)
            y = aux(f"ps_t{i}")
            pe.wait_ge(sp_done, i + 1)
            for mt in range(2):
                mm = turn(y[:, mt * 32:(mt + 1) * 32], psm[:, mt * P:(mt + 1) * P], TS * HEADS)
            mm.then_inc(aux_ready, 1)
            pe.wait_ge(*job_out(f"p_t{i}", 3))
            for j in range(4):
                y = aux(f"o_t{i}", j)
                for ff in range(2):
                    f = 2 * j + ff
                    for mt in range(2):
                        mm = pe.matmul(y[:, ff * TP:(ff + 1) * TP], vm[:, mt, f * P:(f + 1) * P], pT[:, mt, f // 2, :],
                                       start=(ff == 0 and mt == 0), stop=(mt == 1), skip_group_check=True)
                mm.then_inc(aux_ready, 1)
            y = [aux(f"s_o{i}", 0), aux(f"s_o{i}", 1)]
            for s in range(TS):
                v, _ = value_slot(i, s)
                pe.wait_ge(v_summed, TS * i + s + 1)
                for c in range(2):
                    mm = pe.matmul(y[c][0:TS, :], pick[:, s, :], v[:, 0, c * 512:(c + 1) * 512],
                                   start=(s == 0), stop=(s == TS - 1))
                    if s == TS - 1:
                        mm.then_inc(aux_ready, 1)
                if s < TS - 1:
                    mm.then_inc(vused, 1)
            y = aux(f"os_t{i}")
            pe.wait_ge(*job_out(f"s_o{i}", 0))
            pe.wait_ge(*job_out(f"s_o{i}", 1))
            for k in range(KT):
                mm = turn(y[:, k * TS:(k + 1) * TS], qs[:, k * P:(k + 1) * P], TS)
            mm.then_inc(aux_ready, 1)
            if i == 0:
                product("o0", 4, x_hi, x_lo, (x_done, XW["att0"]))

        attention(0)
        normed_product("gate_up", 22, "ffn0")
        for start in range(3):
            pe.wait_ge(a_done, min(FT, KT * (start + 1)))
            product("down", 1, ah[:, :, :], al[:, :, :], start=start)
        product("down", 9, ah[:, :, :], al[:, :, :], start=3)
        normed_product("pw1", 8, "mix1")
        pe.wait_ge(ld_state, 32)
        for j in range(4):
            y = aux("state_t", j)
            half, kq = j // 2, j % 2
            for kk in range(4):
                mm = turn(y[:, kk * 120:(kk + 1) * 120], st_in[:, half, (4 * kq + kk) * P:(4 * kq + kk + 1) * P], 4 * STATE)
            mm.then_inc(aux_ready, 1)
        product("k1", 4, xh[:, :, 0:MEM], xl[:, :, 0:MEM], (x_done, XW["mem1"]))
        memory(1, xh[:, :, 0:MEM], xl[:, :, 0:MEM])
        channel_sum("ln_a1", cv, {0: [(samples_done, 1), (tap_added, TAPS - 1)], 4: [(conv_done, 1)],
                                  2: [(tap_added, 2 * (TAPS - 1))]}, (0, 1, 4, 5, 6, 7, 2, 3))
        channel_sum("ln_b1", sq, pairs(4))
        for j in range(4):
            y = aux("c_tok", j)
            for kk in range(4):
                k = 4 * (j % 2) + kk
                if j < 2:
                    mm = turn(y[0:STATE, kk * P:(kk + 1) * P], ce[:, k, TP:TP + STATE], P)
                else:
                    mm = turn(y[0:TS, kk * P:(kk + 1) * P], se[:, k, :, STATE], P)
            mm.then_inc(aux_ready, 1)
        product("pw2", 4, x_hi, x_lo, (x_done, XW["conv"]))
        attention(1)
        TT = ((0, P), (1, P), (2, TS))

        def residual_turned(half):
            for tt, n_rows in TT:
                y = aux("y_tok", 3 * half + tt)
                for kk in range(4):
                    k = 4 * half + kk
                    pe.wait_ge(*residual_out("o1", 4, k))
                    mm = turn(y[0:n_rows, kk * P:(kk + 1) * P], hT[:, k, tt * P:tt * P + n_rows], P)
                mm.then_inc(aux_ready, 1)

        product("o1", 3, x_hi, x_lo, (x_done, XW["att1"]))
        residual_turned(0)
        product("o1", 1, x_hi, x_lo, start=3)
        residual_turned(1)

        E1 = EXPERTS + 1
        y = aux("route")
        pe.wait_ge(wr_scaled, 1)
        for tt, n_rows in TT:
            for k in range(KT):
                mm = pe.matmul(y[0:n_rows, tt * 16:tt * 16 + EXPERTS], hT[:, k, tt * P:tt * P + n_rows], wr[:, k, :],
                               start=(tt == 0 and k == 0), stop=(k == KT - 1), skip_group_check=True)
        mm.then_inc(aux_ready, 1)
        pe.wait_ge(mask_done, 1)
        pe.wait_ge(moe_const, 2)
        chosen = rt[:, 0, :, :]
        y = aux("pos", 0)
        for tt, n_rows in TT:
            for t2 in range(tt):
                pe.matmul(y[0:n_rows, tt * 16:tt * 16 + E1], ones[:, 0:n_rows], chosen[:, t2, :],
                          start=(tt == 0), stop=False, skip_group_check=True)
            mm = pe.matmul(y[0:n_rows, tt * 16:tt * 16 + E1], tri[0:n_rows, 0:n_rows], chosen[0:n_rows, tt, :],
                           start=(tt == 0), stop=True, skip_group_check=True)
        mm.then_inc(aux_ready, 1)
        y = aux("pos", 1)
        for tt, n_rows in TT:
            mm = pe.matmul(y[:, 0:E1], ones[0:n_rows, :], chosen[0:n_rows, tt, :], start=(tt == 0), stop=(tt == 2))
        mm.then_inc(aux_ready, 1)

        G, U, ACC, TB, XB = (bank[0], bank[2]), (bank[1], bank[3]), (bank[4], bank[5]), bank[6], bank[7]

        def gather(ready):
            pe.wait_ge(s_built, ready)
            for dst, k0 in ((XB, 0), (G[1], 4)):
                for kk in range(4):
                    for tt, n_rows in TT:
                        for part in (hth, htl):
                            mm = pe.matmul(dst[:, kk * CAP:(kk + 1) * CAP], part[0:n_rows, tt, (k0 + kk) * P:(k0 + kk + 1) * P],
                                           sr[0:n_rows, tt, :], start=(tt == 0 and kk == 0 and part is hth),
                                           stop=(tt == 2 and part is htl), skip_group_check=True)
                mm.then_inc(gat_ready, 1)

        def prepare(column):
            for tt, n_rows in TT:
                pe.matmul(XB[:, tt * P:tt * P + n_rows], sf[0:n_rows, tt, :], ident[0:n_rows, 0:n_rows], is_transpose=True,
                          start=(tt == 0), stop=True, skip_group_check=True)
            for tt, n_rows in TT:
                mm = pe.matmul(XB[:, 272:273], sf[0:n_rows, tt, :], rt[0:n_rows, 1, tt, bass.ds(column, 1)],
                               start=False, stop=(tt == 2), skip_group_check=True)
            mm.then_inc(prep_ready, 1)

        def transposes(ps, e, c):
            pe.wait_ge(h_done, 56 * ps + 7 * e + c + 1)
            if c == 0:
                pe.wait_ge(y_added, sums(ps, e, 1))
            else:
                pe.wait_ge(hTl_done, 56 * ps + 7 * e + c)
            for k in range(4):
                mm = turn(TB[:, k * P:(k + 1) * P], hb[:, c % 2, k * P:(k + 1) * P], P)
            mm.then_inc(t_ready, 1)

        def piece(ps, e, p, opens_pass=False, last=False):
            kind, c, half = EP[p]
            if kind == "u" and half == 0 and c >= 1:
                transposes(ps, e, c - 1)
            if kind == "u" and half == 1 and c == 0:
                pe.wait_ge(y_added, sums(ps, e, 0))
                prepare(e)
            if p == NE - 2:
                transposes(ps, e, CH - 1)
                if not last:
                    pe.wait_ge(prep_done, 8 * ps + e + 1)
                    gather(8 * ps + e + 2)
            pe.wait_ge(lo_done, piece_no(ps, e, p) + 1)
            if half == 0:
                if kind == "g" and c == 0:
                    pe.wait_ge(xel_done, 16 * ps + 2 * e + 2)
                    if not opens_pass:
                        pe.wait_ge(silu_done, 56 * ps + 7 * e)
                elif kind == "g" and c == 1:
                    pe.wait_ge(y_added, sums(ps, e, 4))
                elif kind == "g":
                    pe.wait_ge(silu_done, 56 * ps + 7 * e + c - 1)
                elif kind == "u" and c == 1:
                    pe.wait_ge(y_added, sums(ps, e, 5))
                elif kind == "u" and c >= 2:
                    pe.wait_ge(h_done, 56 * ps + 7 * e + c - 1)
                elif kind == "d":
                    pe.wait_ge(hTl_done, 56 * ps + 7 * e + c + 1)
                    if c == 0:
                        pe.wait_ge(y_added, sums(ps, e, 3))
            y = {"g": G[c % 2], "u": U[c % 2], "d": ACC[half]}[kind]
            for k in range(4):
                w_hi, w_lo = whi[:, p % SPLIT, k * EC:(k + 1) * EC], wlo[:, p % SPLIT, k * EC:(k + 1) * EC]
                if kind == "d":
                    x_hi, x_lo = hTh[:, k * P:(k + 1) * P], hTl[:, k * P:(k + 1) * P]
                    first, last = c == 0 and k == 0, c == CH - 1 and k == 3
                else:
                    x_hi, x_lo = xeh[:, 4 * half + k, :], xel[:, 4 * half + k, :]
                    first, last = half == 0 and k == 0, half == 1 and k == 3
                pe.matmul(y[:, :], x_hi, w_hi, start=first, stop=False)
                pe.matmul(y[:, :], x_hi, w_lo, start=False, stop=False)
                mm = pe.matmul(y[:, :], x_lo, w_hi, start=False, stop=last)
            mm.then_inc(piece_done, 1)

        def expert(ps, e, last=False):
            for p in range(2, NE):
                piece(ps, e, p, last=last)
            if not last:
                piece(ps, e + 1, 0)
                piece(ps, e + 1, 1)
            pe.wait_ge(oel_done, 16 * ps + 2 * e + 2)
            for j, dst in enumerate((XB, TB, ACC[0], ACC[1], G[1], U[1])):
                tt, half = SCATTER[j]
                n_rows = TT[tt][1]
                cols = slice(half * 512, (half + 1) * 512)
                pe.matmul(dst[0:n_rows, :], st[:, tt * P:tt * P + n_rows], oeh[:, cols], start=True, stop=False)
                pe.matmul(dst[0:n_rows, :], st[:, tt * P:tt * P + n_rows], oel[:, cols], start=False,
                          stop=True).then_inc(sca_ready, 1)

        def run_pass(ps):
            if not (isinstance(ps, int) and ps == 0):
                pe.wait_ge(y_added, sums(ps, 0, 5))
            gather(8 * ps + 1)
            piece(ps, 0, 0, opens_pass=True)
            piece(ps, 0, 1)
            with pe.Fori(0, EXPERTS - 1) as e:
                expert(ps, e)
            expert(ps, EXPERTS - 1, last=True)

        run_pass(0)
        pe.wait_ge(flag_ready, 1)
        most = pe.value_load(flag[0:1, 0:1])
        with pe.If(most > CAP):
            with pe.Fori(1, 3) as ps:
                run_pass(ps)

    @block.scalar
    def _(act):
        own = Own(act, act_own)

        def width(n):
            return PIECES[n][2] * PC if n < ND else PIECE

        def split(n):
            act.wait_ge(landed[n % RAW], 16 * (n // RAW + 1))
            if n >= SPLIT:
                act.wait_ge(piece_done, n - SPLIT + 1)
            w = width(n)
            act.activation(whi[:, n % SPLIT, 0:w], raw[:, n % RAW, 0:w], ACT.Copy).then_inc(hi_done, 1)

        def pieces(stage, count, post=None, start=0, tail=None):
            for n in range(FIRST[stage] + start, FIRST[stage] + start + count):
                if post is not None:
                    post(n)
                if tail is not None and n == FIRST[stage] + start + count - 1:
                    tail()
                split(n + SPLIT)

        def job_copy(name, j, dst, rows_=P, cols=512):
            act.wait_ge(aux_ready, AUX[name] + j + 1)
            act.activation(dst, job_bank(name, j)[0:rows_, 0:cols], ACT.Copy).then_inc(job_out(name, j)[0], 1)

        def root(job, slot, eps):
            act.wait_ge(aux_ready, AUX[job] + 1)
            act.activation(stat[:, slot, :], job_bank(job)[:, 0:T], ACT.Sqrt, bias=eps, scale=1.0 / D).then_inc(job_out(job)[0], 1)

        def feed(tag, row=None):
            for k in range(KT):
                act.wait_ge(xn_done, XN[tag] + k + 1)
                scale = 1.0 if row is None else vecs[:, k, row:row + 1]
                act.activation(xh[:, k, :], sq[:, k, :], ACT.Copy, scale=scale).then_inc(xh_done, 1)

        def residual_hi(row, before, count, after):
            act.wait_ge(piece_done, FIRST[after])
            for k in range(KT):
                act.wait_ge(*residual_out(before, count, k))
                act.activation(xh[:, k, :], hT[:, k, :], ACT.Copy, scale=vecs[:, k, row:row + 1]).then_inc(xh_done, 1)

        def normed_pieces(stage, count, tag, post=None):
            pieces(stage, 1)
            root("rms_" + tag, 0, eps_r)
            if post is not None:
                post(FIRST[stage])
            pieces(stage, count - 1, post, start=1)

        def memory_hi(i, dst):
            act.wait_ge(*job_out("vec"))
            act.wait_ge(*job_out("mem_t", 3))
            for k in range(KT):
                act.activation(dst[:, k, 0:MEM], memT[:, k, :], ACT.Copy, scale=vecs[:, k, V_MEM + i:V_MEM + i + 1])\
                    .then_inc(mh_done, 1)

        act.wait_ge(mem_sum, 2)
        act.wait_ge(eps_set, 1)
        act.activation(small[:, 4:6], small[:, 2:4], ACT.Sqrt, bias=eps_r, scale=1.0 / D).then_inc(mem_root, 1)
        split(0)
        memory_hi(0, mh)
        for n in range(1, SPLIT):
            split(n)
        for j in range(2):
            job_copy("ws_t", j, wsT[:, 4 * j:4 * j + 4, :].rearrange("p g s -> p (g s)"))
        pieces("k0", 4)
        root("rms_mix0", 0, eps_r)
        feed("mix0", V_MIX)

        def values(i):
            def post(n):
                for o in range(2):
                    act.wait_ge(*tile_ready(n, o))
                    c = PIECES[n][3]
                    act.activation(vm[:, o, c:c + PC], piece_bank(n, o)[:, 0:PC], ACT.Copy).then_inc(tile_out(n, o)[0], 1)
            return post

        def keys_out(i, dst):
            for j in range(4):
                m, half = j // 2, j % 2
                job_copy(f"k_tok{i}", j, dst[:, m, half * 512:(half + 1) * 512])

        pieces("v0", 4, values(0))
        act.wait_ge(piece_done, FIRST["in_v"])
        keys_out(0, kst)

        def gelu(dst, base):
            def post(n):
                for o in range(2):
                    act.wait_ge(*tile_ready(n, o))
                    f = (PIECES[n][3] - base) // P + o
                    act.activation(dst[:, f, :], piece_bank(n, o)[:, 0:T], ACT.Gelu_apprx_tanh).then_inc(tile_out(n, o)[0], 1)
            return post

        pieces("in_v", 4, gelu(vT, D))
        pieces("in_u", 3, gelu(uT, 0))
        root("ln_b0", 1, eps_l)
        pieces("in_u", 1, gelu(uT, 0), start=3)
        for j in range(2):
            job_copy("v_smp", j, vs_out[:, j * 512:(j + 1) * 512], TS)
        for j in range(4):
            c, half = j // 2, j % 2
            job_copy("v_tok", j, vtok[:, c, half * 512:(half + 1) * 512])
        feed("mixed")
        pieces("a_out", 4, tail=lambda: residual_hi(V_XATT, "a_out", 4, "q0"))

        def attention(i):
            normed_pieces(f"q{i}", 4, f"xatt{i}")
            if i == 1:
                act.wait_ge(stored, 16 * 4)
            for j in range(2):
                job_copy(f"q_tok{i}", j, qs[:, j * 512:(j + 1) * 512], TS)
            for j in range(4):
                tt, hh = j // 2, j % 2
                act.wait_ge(nmax_done, 4 * i + j + 1)
                for h2 in range(2):
                    h = 2 * hh + h2
                    ins = act.activation(pr[:, tt, h, :], job_bank(f"scores{i}", j)[:, h2 * MEM:(h2 + 1) * MEM], ACT.Exp,
                                         bias=att[:, 8 + 4 * tt + h:9 + 4 * tt + h], scale=SCALE,
                                         accum_out=att[:, 16 + 4 * tt + h:17 + 4 * tt + h])
                ins.then_inc(job_out(f"scores{i}", j)[0], 1)
            for j in range(4):
                act.wait_ge(rsum_done, 4 * i + j + 1)
                for h2 in range(2):
                    tt, h = j // 2, 2 * (j % 2) + h2
                    ins = act.activation(pr[:, tt, h, :], pr[:, tt, h, :], ACT.Copy,
                                         scale=att[:, 24 + 4 * tt + h:25 + 4 * tt + h])
                ins.then_inc(p_done, 1)
            act.wait_ge(snmax_done, i + 1)
            n32 = TS * HEADS
            act.activation(psm[:, :], job_bank(f"s_t{i}")[0:n32, 0:MEM], ACT.Exp, bias=att[0:n32, 33:34], scale=SCALE,
                           accum_out=att[0:n32, 34:35]).then_inc(job_out(f"s_t{i}")[0], 1)
            for j in range(4):
                job_copy(f"p_t{i}", j, pT[:, j % 2, :, (j // 2) * P:(j // 2 + 1) * P])

            def scaled_values(first, last):
                for s in range(first, last):
                    place, loaded = value_slot(i, s)
                    act.wait_ge(*loaded)
                    for h in range(HEADS):
                        v = place[:, 0, h * HD:(h + 1) * HD]
                        ins = act.activation(v, v, ACT.Copy, scale=sprob[:, 0, s * HEADS + h:s * HEADS + h + 1])
                    ins.then_inc(v_scaled, 1)

            act.wait_ge(*job_out(f"ps_t{i}"))
            scaled_values(0, 2)
            for j in range(4):
                act.wait_ge(aux_ready, AUX[f"o_t{i}"] + j + 1)
                act.activation(xh[:, 2 * j:2 * j + 2, 0:TP],
                               job_bank(f"o_t{i}", j)[:, :].rearrange("p (f t) -> p f t", f=2), ACT.Copy).then_inc(xoh_done, 1)
            scaled_values(2, TS)
            job_copy(f"s_o{i}", 1, qs[:, 512:D], TS)
            act.wait_ge(*job_out(f"os_t{i}"))
            act.activation(xh[:, :, TP:T], os8[:, :, :], ACT.Copy).then_inc(osh_done, 1)

        attention(0)
        pieces("o0", 4, tail=lambda: residual_hi(V_FFN, "o0", 4, "gate_up"))

        def gated(func, split_h):
            def post(n):
                c = (n - FIRST["gate_up" if split_h else "pw1"]) // 2
                gate = (n - FIRST["gate_up"]) % 2 == 0
                for o in range(2):
                    slot = 2 * (c % 2) + o
                    if gate:
                        act.wait_ge(*tile_out(n, o))
                        act.activation(sg[:, slot, :], sg[:, slot, :], func).then_inc(gate_done, 1)
                    elif split_h:
                        act.wait_ge(af_done, 2 * c + o + 1)
                        act.activation(ah[:, 2 * c + o, :], af[:, slot, :], ACT.Copy).then_inc(ah_done, 1)
            return post

        normed_pieces("gate_up", 22, "ffn0", gated(ACT.Silu, True))
        pieces("down", 12, tail=lambda: residual_hi(V_MIX + 1, "down", 12, "pw1"))
        glu_gate = gated(ACT.Sigmoid, False)

        def taps(first, last):
            for u in range(first, last):
                pair, j = u // TAPS, u % TAPS
                i = u - pair - 1
                if u == 0:
                    act.wait_ge(pad_done, 1)
                if j == 0:
                    act.wait_ge(glu_done, 2 * pair + 2)
                elif i >= 2:
                    act.wait_ge(tap_added, i - 1)
                for kk in range(2):
                    k = 2 * pair + kk
                    src, w = ce[:, k, j:j + TP], vecs[:, k, V_DW + j:V_DW + j + 1]
                    if j == 0:
                        ins = act.activation(cv[:, k, 0:TP], src, ACT.Identity, bias=vecs[:, k, V_BDW:V_BDW + 1], scale=w)
                    else:
                        ins = act.activation(tap[:, i % 2, kk, :], src, ACT.Copy, scale=w)
                ins.then_inc(tap_done, 1)

        def glu_post(n):
            glu_gate(n)
            o = n - FIRST["pw1"]
            if o >= 3:
                taps(EARLY * (o - 3), EARLY * (o - 2))

        EARLY = 2
        UNITS = CONV_POOL // 2 * TAPS - 5 * EARLY

        def tap_share(n):
            o = n - FIRST["k1"]
            taps(5 * EARLY + UNITS * o // 8, 5 * EARLY + UNITS * (o + 1) // 8)


        normed_pieces("pw1", 8, "mix1", glu_post)
        act.wait_ge(piece_done, FIRST["k1"])
        memory_hi(1, xh)
        for j in range(4):
            half, kq = j // 2, j % 2
            act.wait_ge(aux_ready, AUX["state_t"] + j + 1)
            act.activation(se[:, 4 * kq:4 * kq + 4, 4 * half:4 * half + 4, 0:STATE],
                           job_bank("state_t", j)[:, 0:480].rearrange("p (k s j) -> p k s j", k=4, s=4),
                           ACT.Copy).then_inc(job_out("state_t", j)[0], 1)
        pieces("k1", 4, tap_share)
        act.wait_ge(vm_out, 16)
        values_out = values(1)

        def values_post(n):
            values_out(n)
            tap_share(n)

        pieces("v1", 4, values_post)
        keys_out(1, kst1)
        act.wait_ge(tap_added, CONV_POOL // 2 * (TAPS - 1))
        root("ln_b1", 1, eps_l)
        for k in range(KT + 1):
            if k < KT:
                act.wait_ge(lnx_done, k + 1)
                act.activation(sq[:, k, :], cv[:, k, :], ACT.Silu, bias=vecs[:, k, V_BLNB:V_BLNB + 1],
                               scale=vecs[:, k, V_BLNG:V_BLNG + 1]).then_inc(xn_done, 1)
            if k > 0:
                act.wait_ge(xn_done, XN["conv"] + k)
                act.activation(xh[:, k - 1, :], sq[:, k - 1, :], ACT.Copy).then_inc(xh_done, 1)
        for j in range(4):
            if j < 2:
                job_copy("c_tok", j, c_out[:, j * 512:(j + 1) * 512], STATE)
            else:
                job_copy("c_tok", j, cs_out[:, (j - 2) * 512:(j - 1) * 512], TS)
        pieces("pw2", 4, tail=lambda: residual_hi(V_XATT + 1, "pw2", 4, "q1"))
        attention(1)
        pieces("o1", 4)

        def squares(half):
            for tt, n_rows in enumerate(ROWS):
                j = 3 * half + tt
                cols = slice(half * 512, (half + 1) * 512)
                act.wait_ge(*job_out("y_tok", j))
                act.activation(hnf[0:n_rows, tt, cols], ytok[0:n_rows, tt, cols], ACT.Square,
                               accum_out=small[0:n_rows, 16 + j:17 + j]).then_inc(tok_sum, 1)

        squares(0)
        for tt, n_rows in enumerate(ROWS):
            job_copy("y_tok", 3 + tt, ytok[0:n_rows, tt, 512:D], n_rows)
        squares(1)
        act.wait_ge(tok_sum, 7)
        act.activation(small[:, 2:5], small[:, 45:48], ACT.Sqrt, bias=eps_r, scale=1.0 / D).then_inc(tok_root, 1)
        for tt, n_rows in enumerate(ROWS):
            act.wait_ge(hn_done, tt + 1)
            act.activation(hth[0:n_rows, tt, :], hnf[0:n_rows, tt, :], ACT.Copy).then_inc(hth_done, 1)
        act.wait_ge(gate_gap, 1)
        act.activation(rt[:, 13, :, 0:1], rt[:, 12, :, 0:1], ACT.Exp).then_inc(gate_exp, 1)

        G, XB, TB, ACC = (bank[0], bank[2]), bank[7], bank[6], (bank[4], bank[5])

        def split_moe(ps, e, p):
            act.wait_ge(landed[p % RAW], 16 * (ND // RAW + ps * (EXPERTS * NE // RAW) + e * (NE // RAW) + p // RAW + 1))
            act.wait_ge(piece_done, piece_no(ps, e, p) - SPLIT + 1)
            act.activation(whi[:, p % SPLIT, :], raw[:, p % RAW, :], ACT.Copy).then_inc(hi_done, 1)

        def tokens_hi(first):
            for j, src in enumerate((XB, G[1])):
                act.wait_ge(gat_ready, first + j)
                act.activation(xeh[:, 4 * j:4 * j + 4, :], src[:, :].rearrange("p (k r) -> p k r", k=4), ACT.Copy)\
                    .then_inc(xeh_done, 1)

        def h_hi(value):
            act.wait_ge(t_ready, value)
            act.activation(hTh[:, :], TB[:, :], ACT.Copy).then_inc(hTh_done, 1)

        def piece(ps, e, p, last=False):
            kind, c, half = EP[p]
            if kind == "g" and half == 1:
                act.wait_ge(piece_done, piece_no(ps, e, p) + 1)
                act.activation(hb[:, c % 2, :], G[c % 2][:, :], ACT.Silu).then_inc(silu_done, 1)
            if kind == "u" and half == 0 and c >= 1:
                h_hi(56 * ps + 7 * e + c)
            if p == NE - 2:
                h_hi(56 * ps + 7 * e + CH)
                if not last:
                    tokens_hi(16 * ps + 2 * e + 3)
            if not last or p + SPLIT < NE:
                split_moe(ps, e, p + SPLIT)

        def expert(ps, e, last=False):
            for p in range(2, NE):
                piece(ps, e, p, last)
            act.wait_ge(prep_done, 8 * ps + e + 1)
            act.wait_ge(piece_done, piece_no(ps, e, NE))
            for half in range(2):
                act.activation(oeh[:, half * 512:(half + 1) * 512], ACC[half][:, :], ACT.Copy, scale=gr[:, 0:1])\
                    .then_inc(oeh_done, 1)
            if not last:
                piece(ps, e + 1, 0)
                piece(ps, e + 1, 1)

        def run_pass(ps):
            if not (isinstance(ps, int) and ps == 0):
                for p in range(SPLIT):
                    split_moe(ps, 0, p)
            tokens_hi(16 * ps + 1)
            piece(ps, 0, 0)
            piece(ps, 0, 1)
            with act.Fori(0, EXPERTS - 1) as e:
                expert(ps, e)
            expert(ps, EXPERTS - 1, last=True)

        run_pass(0)
        act.wait_ge(flag_ready, 1)
        most = act.value_load(flag[0:1, 0:1])
        with act.If(most > CAP):
            with act.Fori(1, 3) as ps:
                run_pass(ps)
        act.wait_ge(fin_start, 1)
        act.activation(yo[:, 1, :], ytok[:, 1, :], ACT.Square, accum_out=small[:, 33:34]).then_inc(fin_sum, 1)
        act.wait_ge(fin_sum, 2)
        act.activation(small[:, 36:39], small[:, 32:35], ACT.Sqrt, bias=eps_r, scale=1.0 / D).then_inc(fin_root, 1)

    @block.vector
    def _(dve):
        own = Own(dve, dve_own)

        def width(n):
            return PIECES[n][2] * PC if n < ND else PIECE

        def split(n):
            dve.wait_ge(hi_done, n + 1)
            w = width(n)
            dve.tensor_tensor(wlo[:, n % SPLIT, 0:w], raw[:, n % RAW, 0:w], whi[:, n % SPLIT, 0:w].bitcast(F32),
                              ALU.subtract).then_inc(lo_done, 1)

        def pieces(stage, count, post=None, start=0, tail=None):
            for n in range(FIRST[stage] + start, FIRST[stage] + start + count):
                if post is not None:
                    post(n)
                if tail is not None and n == FIRST[stage] + start + count - 1:
                    tail()
                split(n + SPLIT)

        def job_copy(name, j, dst, rows_=P, cols=512):
            dve.wait_ge(aux_ready, AUX[name] + j + 1)
            dve.tensor_copy(dst, job_bank(name, j)[0:rows_, 0:cols]).then_inc(job_out(name, j)[0], 1)

        def to_sbuf(dst, base):
            def post(n):
                for o in range(2):
                    dve.wait_ge(*tile_ready(n, o))
                    f = (PIECES[n][3] - base) // P + o
                    dve.tensor_copy(dst[:, f, :], piece_bank(n, o)[:, 0:dst.shape[2]]).then_inc(tile_out(n, o)[0], 1)
            return post

        def add_residual(n):
            if not PIECES[n][5]:
                return
            if n == ND - 1:
                for tt, n_rows in enumerate(ROWS):
                    job_copy("y_tok", tt, ytok[0:n_rows, tt, 0:512], n_rows)
            for o in range(2):
                dve.wait_ge(*tile_ready(n, o))
                f = PIECES[n][3] // P + o
                dve.tensor_tensor(hT[:, f, :], hT[:, f, :], piece_bank(n, o)[:, 0:T], ALU.add).then_inc(tile_out(n, o)[0], 1)
            dve.wait_ge(*tile_out(n, 1))
            if f < KT - 1 and n < FIRST["o1"]:
                dve.tensor_tensor(sq[:, f - 1:f + 1, :], hT[:, f - 1:f + 1, :], hT[:, f - 1:f + 1, :], ALU.mult)

        def last_square():
            dve.tensor_tensor(sq[:, KT - 2:KT, :], hT[:, KT - 2:KT, :], hT[:, KT - 2:KT, :], ALU.mult).then_inc(sq_done, 1)

        def residual_lo(row, tag):
            for k in range(KT):
                dve.wait_ge(xh_done, FEED[tag] + k + 1)
                dve.scalar_tensor_tensor(out=xl[:, k, :], in0=hT[:, k, :], scalar=vecs[:, k, row:row + 1],
                                         in1=xh[:, k, :].bitcast(F32), op0=ALU.mult, op1=ALU.subtract).then_inc(x_done, 1)
            last_square()

        def normed_pieces(stage, count, tag, post):
            inverse_root("rms_" + tag)
            pieces(stage, count, post)

        def square(before):
            dve.wait_ge(*before)
            dve.tensor_tensor(sq[:, :, :], hT[:, :, :], hT[:, :, :], ALU.mult).then_inc(sq_done, 1)

        def inverse_root(job):
            dve.wait_ge(*job_out(job))
            own(dve.reciprocal(stat[:, 1, :], stat[:, 0, :]))
            own.settle()

        def feed_lo(tag, row=None):
            for k in range(KT):
                dve.wait_ge(xh_done, FEED[tag] + k + 1)
                hi = xh[:, k, :].bitcast(F32)
                if row is None:
                    ins = dve.tensor_tensor(xl[:, k, :], sq[:, k, :], hi, ALU.subtract)
                else:
                    ins = dve.scalar_tensor_tensor(out=xl[:, k, :], in0=sq[:, k, :], scalar=vecs[:, k, row:row + 1], in1=hi,
                                                   op0=ALU.mult, op1=ALU.subtract)
                ins.then_inc(x_done, 1)

        def rms_feed(tag, job, row):
            inverse_root(job)
            for k in range(KT):
                dve.tensor_tensor(sq[:, k, :], hT[:, k, :], stat[:, 1, :], ALU.mult).then_inc(xn_done, 1)
            feed_lo(tag, row)

        def memory_lo(i, hi, lo, done):
            for k in range(KT):
                dve.wait_ge(mh_done, 8 * i + k + 1)
                dve.scalar_tensor_tensor(out=lo[:, k, 0:MEM], in0=memT[:, k, :], scalar=vecs[:, k, V_MEM + i:V_MEM + i + 1],
                                         in1=hi[:, k, 0:MEM].bitcast(F32), op0=ALU.mult, op1=ALU.subtract).then_inc(done, 1)

        def layer_norm_a(job, x):
            dve.wait_ge(aux_ready, AUX[job] + 1)
            dve.tensor_scalar(stat[:, 0, :], job_bank(job)[:, 0:T], 1.0 / D, None, ALU.mult).then_inc(job_out(job)[0], 1)
            dve.wait_ge(*job_out(job))
            for k in range(0, KT + 2, 2):
                if k < KT:
                    own(dve.tensor_tensor(x[:, k, :], x[:, k, :], stat[:, 0, :], ALU.subtract))
                    own(dve.tensor_tensor(x[:, k + 1, :], x[:, k + 1, :], stat[:, 0, :], ALU.subtract))
                if k > 0:
                    own.settle(2 if k < KT else 0)
                    dve.tensor_tensor(sq[:, k - 2:k, :], x[:, k - 2:k, :], x[:, k - 2:k, :], ALU.mult).then_inc(lnsq_done, 1)

        def layer_norm_b(job, x, row_g, row_b):
            dve.wait_ge(*job_out(job))
            own(dve.reciprocal(stat[:, 2, :], stat[:, 1, :]))
            own.settle()
            for k in range(KT):
                own(dve.tensor_tensor(x[:, k, :], x[:, k, :], stat[:, 2, :], ALU.mult))
            for k in range(KT):
                own.settle(KT - 1)
                ins = own(dve.tensor_scalar(x[:, k, :], x[:, k, :], vecs[:, k, row_g:row_g + 1], vecs[:, k, row_b:row_b + 1],
                                            ALU.mult, ALU.add))
            own.settle()
            dve.sem_inc(lnv_done, 1)

        own(dve.memset(small[:, 0:1], RMS_EPS))
        own(dve.memset(small[:, 1:2], LN_EPS))
        for e in range(EXPERTS):
            own(dve.memset(small[:, 24 + e:25 + e], float(EXPERTS - e)))
        own(dve.memset(pick[:, :, :], 0.0))
        own.settle()
        own(dve.memset(pick[:, :, :].rearrange("p s t -> p (s t)")[:, 0:TS * TS:TS + 1], 1.0))
        own(dve.memset(small[:, 16:22], 1.0))
        dve.memset(small[:, 32:35], 1.0).then_inc(eps_set, 1)
        dve.wait_ge(ld_mem, 16)
        for m in range(2):
            dve.tensor_tensor_reduce(sq[:, :, :].rearrange("p k t -> p (k t)")[:, m * D:(m + 1) * D], mem_in[:, m, :],
                                     mem_in[:, m, :], 1.0, 0.0, ALU.mult, ALU.add, small[:, 2 + m:3 + m]).then_inc(mem_sum, 1)
        dve.wait_ge(mem_root, 1)
        own(dve.reciprocal(small[:, 6:8], small[:, 4:6]))
        own.settle()
        for m in range(2):
            dve.tensor_scalar(mem_in[:, m, :], mem_in[:, m, :], small[:, 6 + m:7 + m], None, ALU.mult).then_inc(mem_n, 1)
        job_copy("vec", 0, vecs[:, :, :].rearrange("p k v -> p (k v)"), P, KT * NV)
        for j in range(4):
            job_copy("mem_t", j, memT[:, 2 * j:2 * j + 2, :].rearrange("p k m -> p (k m)"))
        split(0)
        memory_lo(0, mh, ml, m_done)
        split(1)
        for k in range(KT):
            job_copy("x_t", k, hT[:, k, :], P, T)
        dve.wait_ge(mem_sum, 2)
        square(job_out("x_t", KT - 1))
        job_copy("ws_0", 0, ws0, P, KT)
        dve.wait_ge(ld_wr, 16)
        dve.tensor_tensor(wr[:, :, :], wr[:, :, :], vecs[:, :, V_FFN + 1:V_FFN + 2].to_broadcast([P, KT, EXPERTS]),
                          ALU.mult).then_inc(wr_scaled, 1)
        split(2)
        pieces("k0", 4, to_sbuf(kT, 0))
        rms_feed("mix0", "rms_mix0", V_MIX)
        pieces("v0", 4)
        pieces("in_v", 4)
        pieces("in_u", 1)
        layer_norm_a("ln_a0", vT)
        pieces("in_u", 2, start=1)
        layer_norm_b("ln_b0", vT, V_ALNG, V_ALNB)
        pieces("in_u", 1, start=3)
        dve.wait_ge(ld_misc, 16)
        dve.wait_ge(*job_out("ws_0"))
        own(dve.tensor_tensor(sq[:, :, TP:T], vT[:, :, TP:T], ws0.unsqueeze(2).to_broadcast([P, KT, TS]), ALU.mult))
        own.settle()
        own(dve.tensor_tensor(sq[:, :, TP:T], sq[:, :, TP:T], bs0.unsqueeze(2).to_broadcast([P, KT, TS]), ALU.add))
        for j in range(4):
            dve.wait_ge(aux_ready, AUX["mixed"] + j + 1)
            for gg in range(2):
                g = 2 * j + gg
                ins = dve.tensor_tensor(sq[:, g, 0:TP].rearrange("p (c t) -> p c t", c=2),
                                        job_bank("mixed", j)[:, gg * TP:(gg + 1) * TP].rearrange("p (c t) -> p c t", c=2),
                                        bsb[:, g:g + 1, :].to_broadcast([P, 2, P]), ALU.add)
            ins.then_inc(job_out("mixed", j)[0], 1)
        dve.wait_ge(*stage_out("in_u", 4))
        own.settle()
        for k in range(KT):
            if k % 2 == 0:
                dve.wait_ge(*job_out("mixed", k // 2))
            dve.tensor_tensor(sq[:, k, :], sq[:, k, :], uT[:, k, :], ALU.mult).then_inc(xn_done, 1)
        feed_lo("mixed")
        pieces("a_out", 4, add_residual, tail=lambda: residual_lo(V_XATT, "xatt0"))

        def attention(i):
            def q_out(n):
                for o in range(2):
                    dve.wait_ge(*tile_ready(n, o))
                    dve.tensor_tensor(qT[:, PIECES[n][3] // P + o, :], piece_bank(n, o)[:, 0:T], stat[:, 1, :], ALU.mult)\
                        .then_inc(tile_out(n, o)[0], 1)

            normed_pieces(f"q{i}", 4, f"xatt{i}", q_out)
            if i == 1:
                dve.wait_ge(stored, 16 * 4)
            for j in range(4):
                tt, hh = j // 2, j % 2
                c = 4 * tt + 2 * hh
                dve.wait_ge(aux_ready, AUX[f"scores{i}"] + j + 1)
                own(dve.tensor_reduce(att[:, c:c + 2], job_bank(f"scores{i}", j)[:, :].rearrange("p (h m) -> p h m", h=2),
                                      AX.X, ALU.max))
                own.settle()
                dve.tensor_scalar(att[:, 8 + c:10 + c], att[:, c:c + 2], -SCALE, None, ALU.mult).then_inc(nmax_done, 1)
            for j in range(4):
                tt, hh = j // 2, j % 2
                c = 4 * tt + 2 * hh
                dve.wait_ge(*job_out(f"scores{i}", j))
                dve.reciprocal(att[:, 24 + c:26 + c], att[:, 16 + c:18 + c]).then_inc(rsum_done, 1)
            for s in range(TS):
                keys, loaded = key_slot(i, s)
                dve.wait_ge(*loaded)
                for c in range(2):
                    j = 2 * s + c
                    dve.wait_ge(aux_ready, AUX[f"q_bc{i}"] + j + 1)
                    for h in (2 * c, 2 * c + 1):
                        for mt in range(2):
                            k = keys[:, mt, h * HD:(h + 1) * HD]
                            ins = dve.tensor_tensor_reduce(k, k, job_bank(f"q_bc{i}", j)[:, (h % 2) * HD:(h % 2 + 1) * HD],
                                                           1.0, 0.0, ALU.mult, ALU.add,
                                                           sc[:, mt, s * HEADS + h:s * HEADS + h + 1])
                    ins.then_inc(job_out(f"q_bc{i}", j)[0], 1)
            n32 = TS * HEADS
            dve.wait_ge(aux_ready, AUX[f"s_t{i}"] + 1)
            own(dve.tensor_reduce(att[0:n32, 32:33], job_bank(f"s_t{i}")[0:n32, 0:MEM], AX.X, ALU.max))
            own.settle()
            dve.tensor_scalar(att[0:n32, 33:34], att[0:n32, 32:33], -SCALE, None, ALU.mult).then_inc(snmax_done, 1)
            dve.wait_ge(*job_out(f"s_t{i}"))
            own(dve.reciprocal(att[0:n32, 35:36], att[0:n32, 34:35]))
            own.settle()
            dve.tensor_scalar(psm[:, :], psm[:, :], att[0:n32, 35:36], None, ALU.mult).then_inc(sp_done, 1)
            dve.wait_ge(aux_ready, AUX[f"ps_t{i}"] + 1)
            for mt in range(2):
                ins = dve.tensor_copy(sprob[:, mt, :], job_bank(f"ps_t{i}")[:, mt * n32:(mt + 1) * n32])
            ins.then_inc(job_out(f"ps_t{i}")[0], 1)

            def weighted_values(first, last):
                for s in range(first, last):
                    place, _ = value_slot(i, s)
                    dve.wait_ge(v_scaled, TS * i + s + 1)
                    for h in range(HEADS):
                        v = place[:, :, h * HD:(h + 1) * HD]
                        ins = dve.scalar_tensor_tensor(out=v[:, 0, :], in0=v[:, 1, :], scalar=sprob[:, 1, s * HEADS + h:s * HEADS + h + 1],
                                                       in1=v[:, 0, :], op0=ALU.mult, op1=ALU.add)
                    ins.then_inc(v_summed, 1)

            dve.wait_ge(*job_out(f"ps_t{i}"))
            weighted_values(0, 2)
            for j in range(4):
                dve.wait_ge(xoh_done, 4 * i + j + 1)
                dve.tensor_tensor(xl[:, 2 * j:2 * j + 2, 0:TP], job_bank(f"o_t{i}", j)[:, :].rearrange("p (f t) -> p f t", f=2),
                                  xh[:, 2 * j:2 * j + 2, 0:TP].bitcast(F32), ALU.subtract).then_inc(job_out(f"o_t{i}", j)[0], 1)
            weighted_values(2, TS)
            job_copy(f"s_o{i}", 0, qs[:, 0:512], TS)
            job_copy(f"os_t{i}", 0, os8[:, :, :].rearrange("p k s -> p (k s)"), P, KT * TS)
            dve.wait_ge(osh_done, i + 1)
            dve.wait_ge(*job_out(f"o_t{i}", 3))
            for k in range(KT):
                dve.tensor_tensor(xl[:, k, TP:T], os8[:, k, :], xh[:, k, TP:T].bitcast(F32), ALU.subtract).then_inc(x_done, 1)

        attention(0)
        pieces("o0", 4, add_residual, tail=lambda: residual_lo(V_FFN, "ffn0"))

        def scaled_out(n, c, dst):
            for o in range(2):
                dve.wait_ge(*tile_ready(n, o))
                dve.tensor_tensor(dst[:, 2 * (c % 2) + o, :], piece_bank(n, o)[:, 0:T], stat[:, 1, :], ALU.mult)\
                    .then_inc(tile_out(n, o)[0], 1)

        def gated(n):
            c = (n - FIRST["gate_up"]) // 2
            if (n - FIRST["gate_up"]) % 2 == 0:
                if c >= 2:
                    dve.wait_ge(af_done, 2 * c - 2)
                scaled_out(n, c, sg)
                return
            if c >= 2:
                dve.wait_ge(a_done, 2 * c - 2)
            scaled_out(n, c, af)
            for o in range(2):
                slot = 2 * (c % 2) + o
                dve.wait_ge(gate_done, 2 * c + o + 1)
                dve.wait_ge(*tile_out(n, o))
                dve.tensor_tensor(af[:, slot, :], sg[:, slot, :], af[:, slot, :], ALU.mult).then_inc(af_done, 1)
            for o in range(2):
                dve.wait_ge(ah_done, 2 * c + o + 1)
                dve.tensor_tensor(al[:, 2 * c + o, :], af[:, 2 * (c % 2) + o, :], ah[:, 2 * c + o, :].bitcast(F32),
                                  ALU.subtract).then_inc(a_done, 1)

        normed_pieces("gate_up", 22, "ffn0", gated)
        dve.wait_ge(a_done, FT)
        pieces("down", 12, add_residual, tail=lambda: residual_lo(V_MIX + 1, "mix1"))

        def glu(n):
            c = (n - FIRST["pw1"]) // 2
            if (n - FIRST["pw1"]) % 2 == 0:
                if c >= 2:
                    dve.wait_ge(glu_done, 2 * c - 2)
                scaled_out(n, c, sg)
                return
            scaled_out(n, c, af)
            for o in range(2):
                f, slot = 2 * c + o, 2 * (c % 2) + o
                dve.wait_ge(gate_done, FT + f + 1)
                dve.wait_ge(*tile_out(n, o))
                dve.tensor_tensor(ce[:, f, STATE:STATE + TP], af[:, slot, 0:TP], sg[:, slot, 0:TP], ALU.mult)
                dve.tensor_tensor(se[:, f, :, STATE], af[:, slot, TP:T], sg[:, slot, TP:T], ALU.mult).then_inc(glu_done, 1)

        normed_pieces("pw1", 8, "mix1", glu)
        memory_lo(1, xh, xl, x_done)

        def samples_conv():
            dve.wait_ge(*job_out("state_t", 3))
            for k in range(KT):
                own(dve.tensor_tensor(sq[:, k, 0:TS * TAPS].rearrange("p (s j) -> p s j", s=TS), se[:, k, :, :],
                                      vecs[:, k:k + 1, V_DW:NV].to_broadcast([P, TS, TAPS]), ALU.mult))
            for k in range(KT):
                own.settle(KT - 1)
                own(dve.tensor_reduce(cv[:, k, TP:T], sq[:, k, 0:TS * TAPS].rearrange("p (s j) -> p s j", s=TS), AX.X, ALU.add))
            for k in range(KT):
                own.settle(KT - 1)
                own(dve.tensor_scalar(cv[:, k, TP:T], cv[:, k, TP:T], vecs[:, k, V_BDW:V_BDW + 1], None, ALU.add))
            own.settle()
            dve.sem_inc(samples_done, 1)

        def conv_part(quarter):
            if quarter == 0:
                dve.wait_ge(pad_done, 1)
                dve.wait_ge(glu_done, KT)
            for j in range(4 * quarter, min(4 * quarter + 4, TAPS)):
                for k in range(CONV_POOL, KT):
                    w = vecs[:, k, V_DW + j:V_DW + j + 1]
                    if j == 0:
                        own(dve.tensor_scalar(cv[:, k, 0:TP], ce[:, k, 0:TP], w, vecs[:, k, V_BDW:V_BDW + 1], ALU.mult, ALU.add))
                    else:
                        own.settle(3)
                        own(dve.scalar_tensor_tensor(out=cv[:, k, 0:TP], in0=ce[:, k, j:j + TP], scalar=w, in1=cv[:, k, 0:TP],
                                                     op0=ALU.mult, op1=ALU.add))

        keys_out_of_banks = to_sbuf(kT, 0)

        def with_conv(n):
            if n < FIRST["v1"]:
                keys_out_of_banks(n)
            conv_part(n - FIRST["k1"])

        pieces("k1", 4, with_conv)
        samples_conv()

        def finish_conv():
            own.settle()
            dve.sem_inc(conv_done, 1)

        pieces("v1", 4, with_conv, tail=finish_conv)
        layer_norm_a("ln_a1", cv)
        dve.wait_ge(*job_out("ln_b1"))
        own(dve.reciprocal(stat[:, 2, :], stat[:, 1, :]))
        own.settle()
        for k in range(KT):
            dve.tensor_tensor(cv[:, k, :], cv[:, k, :], stat[:, 2, :], ALU.mult).then_inc(lnx_done, 1)
        feed_lo("conv")
        pieces("pw2", 4, add_residual, tail=lambda: residual_lo(V_XATT + 1, "xatt1"))
        attention(1)
        pieces("o1", 4, add_residual)

        E = EXPERTS
        own(dve.memset(rt[:, :, :, :], 0.0))
        own.settle()
        dve.wait_ge(tok_sum, 6)
        dve.tensor_tensor(small[:, 45:48], small[:, 16:19], small[:, 19:22], ALU.add).then_inc(tok_sum, 1)
        inv_tok = small[:, 5:8]
        dve.wait_ge(tok_root, 1)
        own(dve.reciprocal(inv_tok, small[:, 2:5]))
        own.settle()
        dve.wait_ge(ld_frow, 16)
        for tt, n_rows in enumerate(ROWS):
            dve.scalar_tensor_tensor(out=hnf[0:n_rows, tt, :], in0=ytok[0:n_rows, tt, :], scalar=small[0:n_rows, 5 + tt:6 + tt],
                                     in1=frow[0:n_rows, :], op0=ALU.mult, op1=ALU.mult).then_inc(hn_done, 1)
        dve.wait_ge(aux_ready, AUX["route"] + 1)
        y = job_bank("route")
        own(dve.tensor_copy(rt[:, 3, 0:2, 0:E], y[:, 0:32].rearrange("p (t e) -> p t e", e=16)[:, :, 0:E]))
        dve.tensor_copy(rt[0:TS, 3, 2, 0:E], y[0:TS, 32:32 + E]).then_inc(job_out("route")[0], 1)
        dve.wait_ge(*job_out("route"))
        own.settle()
        L = rt[:, 3, :, 0:E]
        order = order8.unsqueeze(1).to_broadcast([P, 3, E])

        def wide(x):
            return x.to_broadcast([P, 3, E])

        def first_of_largest(x, top, tmp, best, sel):
            own(dve.tensor_reduce(top, x, AX.X, ALU.max))
            own.settle()
            own(dve.tensor_tensor(tmp, x, wide(top), ALU.is_equal))
            own.settle()
            own(dve.tensor_tensor(tmp, tmp, order, ALU.mult))
            own.settle()
            own(dve.tensor_reduce(best, tmp, AX.X, ALU.max))
            own.settle()
            own(dve.tensor_tensor(sel, tmp, wide(best), ALU.is_equal))
            own.settle()

        top1, top2, best = rt[:, 10, :, 0:1], rt[:, 11, :, 0:1], rt[:, 9, :, 0:1]
        sel1, sel2, L2 = rt[:, 5, :, 0:E], rt[:, 8, :, 0:E], rt[:, 6, :, 0:E]
        first_of_largest(L, top1, rt[:, 4, :, 0:E], best, sel1)
        own(dve.scalar_tensor_tensor(out=L2, in0=sel1, scalar=-3.0e38, in1=L, op0=ALU.mult, op1=ALU.add))
        own.settle()
        first_of_largest(L2, top2, rt[:, 4, :, 0:E], best, sel2)
        own(dve.tensor_tensor(rt[:, 12, :, 0:1], top2, top1, ALU.subtract))
        own.settle()
        dve.tensor_tensor(rt[:, 12, :, 0:1], rt[:, 12, :, 0:1], inv_tok.unsqueeze(2), ALU.mult).then_inc(gate_gap, 1)
        own(dve.tensor_tensor(rt[:, 0, :, 0:E], sel1, sel2, ALU.add))
        own.settle()
        dve.sem_inc(mask_done, 1)
        for tt, n_rows in enumerate(ROWS):
            dve.wait_ge(hth_done, tt + 1)
            own(dve.tensor_tensor(htl[0:n_rows, tt, :], hnf[0:n_rows, tt, :], hth[0:n_rows, tt, :].bitcast(F32), ALU.subtract))
        dve.wait_ge(gate_exp, 1)
        gexp, den, w1, w2 = rt[:, 13, :, 0:1], rt[:, 14, :, 0:1], rt[:, 15, :, 0:1], rt[:, 15, :, 1:2]
        own(dve.tensor_scalar(den, gexp, 1.0, None, ALU.add))
        own.settle()
        own(dve.reciprocal(w1, den))
        own.settle()
        own(dve.tensor_tensor(w2, gexp, w1, ALU.mult))
        own(dve.tensor_tensor(sel1, sel1, wide(w1), ALU.mult))
        own.settle()
        own(dve.tensor_tensor(sel2, sel2, wide(w2), ALU.mult))
        own.settle()
        own(dve.tensor_tensor(rt[:, 1, :, 0:E], sel1, sel2, ALU.add))
        dve.wait_ge(aux_ready, AUX["pos"] + 1)
        y = job_bank("pos", 0)
        own(dve.tensor_copy(rt[:, 2, 0:2, :], y[:, 0:32].rearrange("p (t e) -> p t e", e=16)[:, :, 0:E + 1]))
        dve.tensor_copy(rt[0:TS, 2, 2, :], y[0:TS, 32:33 + E]).then_inc(job_out("pos", 0)[0], 1)
        dve.wait_ge(*job_out("pos", 0))
        dve.wait_ge(aux_ready, AUX["pos"] + 2)
        dve.tensor_reduce(small[:, 40:41], job_bank("pos", 1)[:, 0:E], AX.X, ALU.max).then_inc(job_out("pos", 1)[0], 1)
        dve.wait_ge(*job_out("pos", 1))
        dve.tensor_copy(flag[:, 0:1], small[:, 40:41]).then_inc(flag_ready, 1)
        own.settle()
        dve.wait_ge(flag_ready, 1)

        G, U, ACC, TB, XB = (bank[0], bank[2]), (bank[1], bank[3]), (bank[4], bank[5]), bank[6], bank[7]

        def split_moe(ps, e, p):
            dve.wait_ge(hi_done, piece_no(ps, e, p) + 1)
            dve.tensor_tensor(wlo[:, p % SPLIT, :], raw[:, p % RAW, :], whi[:, p % SPLIT, :].bitcast(F32),
                              ALU.subtract).then_inc(lo_done, 1)

        def build_s(column):
            for tt, n_rows in enumerate(ROWS):
                for dst in (sf, sr):
                    ins = dve.tensor_scalar(dst[0:n_rows, tt, :], iota[0:n_rows, :], rt[0:n_rows, 2, tt, bass.ds(column, 1)],
                                            rt[0:n_rows, 0, tt, bass.ds(column, 1)], ALU.is_equal, ALU.mult)
            ins.then_inc(s_built, 1)

        def tokens_lo(first):
            for j, src in enumerate((XB, G[1])):
                dve.wait_ge(xeh_done, first + j)
                dve.tensor_tensor(xel[:, 4 * j:4 * j + 4, :], src[:, :].rearrange("p (k r) -> p k r", k=4),
                                  xeh[:, 4 * j:4 * j + 4, :].bitcast(F32), ALU.subtract).then_inc(xel_done, 1)

        def take_prepared(value):
            dve.wait_ge(prep_ready, value)
            dve.tensor_copy(st[:, :], XB[:, 0:T])
            dve.tensor_copy(gr[:, 0:1], XB[:, 272:273]).then_inc(prep_done, 1)

        def h_lo(value):
            dve.wait_ge(hTh_done, value)
            dve.tensor_tensor(hTl[:, :], TB[:, :], hTh[:, :].bitcast(F32), ALU.subtract).then_inc(hTl_done, 1)

        def piece(ps, e, p, last=False):
            kind, c, half = EP[p]
            if kind == "u" and half == 0 and c >= 1:
                h_lo(56 * ps + 7 * e + c)
            if kind == "u" and half == 1:
                dve.wait_ge(silu_done, 56 * ps + 7 * e + c + 1)
                dve.wait_ge(piece_done, piece_no(ps, e, p) + 1)
                dve.tensor_tensor(hb[:, c % 2, :], hb[:, c % 2, :], U[c % 2][:, :], ALU.mult).then_inc(h_done, 1)
            if kind == "g" and half == 0 and c == 1:
                take_prepared(8 * ps + e + 1)
            if kind == "g" and half == 0 and c == 3 and not last:
                dve.wait_ge(prep_ready, 8 * ps + e + 1)
                build_s(e + 1)
            if p == NE - 2:
                h_lo(56 * ps + 7 * e + CH)
                if not last:
                    tokens_lo(16 * ps + 2 * e + 3)
            if not last or p + SPLIT < NE:
                split_moe(ps, e, p + SPLIT)

        def expert(ps, e, last=False):
            for p in range(2, NE):
                piece(ps, e, p, last)
            for half in range(2):
                dve.wait_ge(oeh_done, 16 * ps + 2 * e + half + 1)
                dve.scalar_tensor_tensor(out=oel[:, half * 512:(half + 1) * 512], in0=ACC[half][:, :], scalar=gr[:, 0:1],
                                         in1=oeh[:, half * 512:(half + 1) * 512].bitcast(F32), op0=ALU.mult,
                                         op1=ALU.subtract).then_inc(oel_done, 1)
            if not last:
                piece(ps, e + 1, 0)
                piece(ps, e + 1, 1)
            dve.wait_ge(y_added, sums(ps, e, 5))
            for j, src in enumerate((XB, TB, ACC[0], ACC[1], G[1], U[1])):
                tt, half = SCATTER[j]
                y = ytok[0:ROWS[tt], tt, half * 512:(half + 1) * 512]
                dve.wait_ge(sca_ready, 48 * ps + 6 * e + j + 1)
                dve.tensor_tensor(y, y, src[0:ROWS[tt], :], ALU.add).then_inc(y_added, 1)

        def run_pass(ps):
            if not (isinstance(ps, int) and ps == 0):
                dve.wait_ge(prep_ready, 8 * ps)
                dve.wait_ge(prep_done, 8 * ps)
                dve.tensor_scalar(rt[:, 2, :, :], rt[:, 2, :, :], float(-CAP), None, ALU.add).then_inc(pos_moved, 1)
                dve.wait_ge(pos_moved, ps)
            if not (isinstance(ps, int) and ps == 0):
                for p in range(SPLIT):
                    split_moe(ps, 0, p)
            build_s(0)
            tokens_lo(16 * ps + 1)
            piece(ps, 0, 0)
            piece(ps, 0, 1)
            with dve.Fori(0, EXPERTS - 1) as e:
                expert(ps, e)
            expert(ps, EXPERTS - 1, last=True)
            dve.wait_ge(y_added, 48 * ps + 54)

        dve.sem_inc(y_added, 6)
        dve.wait_ge(moe_const, 2)
        run_pass(0)
        most = dve.value_load(flag[0:1, 0:1])
        with dve.If(most > CAP):
            with dve.Fori(1, 3) as ps:
                run_pass(ps)

        dve.sem_inc(fin_start, 1)
        for tt, n_rows in ((0, P), (2, TS)):
            ins = dve.tensor_tensor_reduce(yo[0:n_rows, tt, :], ytok[0:n_rows, tt, :], ytok[0:n_rows, tt, :], 1.0, 0.0, ALU.mult,
                                           ALU.add, small[0:n_rows, 32 + tt:33 + tt])
        ins.then_inc(fin_sum, 1)
        dve.wait_ge(fin_root, 1)
        own(dve.reciprocal(small[:, 42:45], small[:, 36:39]))
        own.settle()
        dve.wait_ge(ld_grow, 16)
        for tt, n_rows in enumerate(ROWS):
            dve.scalar_tensor_tensor(out=yo[0:n_rows, tt, :], in0=ytok[0:n_rows, tt, :], scalar=small[0:n_rows, 42 + tt:43 + tt],
                                     in1=grow[0:n_rows, :], op0=ALU.mult, op1=ALU.mult).then_inc(fin_done, 1)


_IN = ['x_prompt', 'x_sample', 'mem_prompt', 'cache_mem_k', 'cache_mem_v', 'state_conv', 'norm_mix', 'norm_xattn', 'norm_ffn',
       'norm_mem', 'norm_final', 'w_xq', 'w_xk', 'w_xv', 'w_xo', 'a_w_in', 'a_ln_g', 'a_ln_b', 'a_w_s', 'a_b_s', 'a_w_out',
       'b_w_pw1', 'b_w_dw', 'b_b_dw', 'b_ln_g', 'b_ln_b', 'b_w_pw2', 'ffn_w_gate', 'ffn_w_up', 'ffn_w_down', 'moe_w_router',
       'moe_w_gate', 'moe_w_up', 'moe_w_down']
_OUT = [("y", (1, TP, D)), ("ys", (TS, 1, D)), ("k", (2, 1, MEM, HEADS, HD)), ("v", (2, 1, MEM, HEADS, HD)),
        ("conv_p", (1, 1, STATE, D)), ("conv_s", (1, TS, STATE, D)), ("chunk", (1, TS, 1, D))]


def kernel(**inputs):
    import numpy as np
    import concourse.bacc as bacc
    from concourse.bass_utils import run_bass_kernel_spmd

    nc = bacc.Bacc("TRN2", target_bir_lowering=False, num_devices=1)
    arrays, a, out = {}, {}, {}
    for name in _IN:
        arrays["in_" + name] = np.ascontiguousarray(inputs[name])
        a[name] = nc.dram_tensor("in_" + name, arrays["in_" + name].shape, F32, kind="ExternalInput").ap()
    for name, shape in _OUT:
        out[name] = nc.dram_tensor("out_" + name, shape, F32, kind="ExternalOutput").ap()
    with ExitStack() as ctx:
        build_step(nc, ctx, a, out)
    r = run_bass_kernel_spmd(nc, [arrays], core_ids=[0])
    return tuple(r.results[0]["out_" + name] for name, _ in _OUT)
```
